# Optimizing a Trainium2 kernel written in Bass

```python
import math
import jax, jax.numpy as jnp
from jax import lax
import numpy as np

D_MODEL = 1024
BATCH = 1
SEQ = 256
DEPTH = 2

DN_HEADS = 8
DN_DK = 128
DN_DV = 128
DN_CONV = 4
DN_CHUNK = 64
SB_HEADS = 8
SB_DH = 64
SB_BLOCK = 128
D_FF = 3584
N_EXPERTS = 8
TOP_K = 2
MOE_BLOCK = 128
EPS = 1e-6
N_DENSE = (DEPTH + 1) // 2
N_MOE = DEPTH // 2
N_BRANCH = 2

DN_QK = DN_HEADS * DN_DK
DN_V = DN_HEADS * DN_DV
SB_W = SB_HEADS * SB_DH
_WIDTHS = (2 * DN_QK + DN_V, DN_V, DN_HEADS, DN_HEADS, SB_W, SB_W, SB_W, N_BRANCH * D_MODEL)
IN_COLS = sum(_WIDTHS)
SPLIT_AT = tuple(int(s) for s in np.cumsum(_WIDTHS)[:-1])


def rms_norm(x, w):
    xf = x.astype(jnp.float32)
    y = xf * lax.rsqrt(jnp.mean(xf * xf, axis=-1, keepdims=True) + EPS)
    return (y * w.astype(jnp.float32)).astype(x.dtype)

def l2_norm(x):
    xf = x.astype(jnp.float32)
    return xf * lax.rsqrt(jnp.sum(xf * xf, axis=-1, keepdims=True) + EPS)

def causal_depthwise_conv(x, w):
    k = w.shape[0]
    y = lax.conv_general_dilated(x, w[:, None, :].astype(x.dtype), window_strides=(1,),
                                 padding=[(k - 1, 0)], dimension_numbers=('NWC', 'WIO', 'NWC'),
                                 feature_group_count=x.shape[-1])
    return jax.nn.silu(y)

def gated_delta_rule(q, k, v, g, beta):
    B, S, H, DK = q.shape
    DV = v.shape[-1]
    N = S // DN_CHUNK

    def chunk(t):
        return jnp.moveaxis(t.reshape((B, N, DN_CHUNK) + t.shape[2:]), 2, 3)

    q, k, v, g, beta = (chunk(t) for t in (q, k, v, g, beta))
    g = jnp.cumsum(g, axis=-1)
    idx = jnp.arange(DN_CHUNK)
    lower = idx[:, None] >= idx[None, :]
    strict = idx[:, None] > idx[None, :]
    decay = jnp.exp(jnp.where(lower, g[..., :, None] - g[..., None, :], -jnp.inf))
    kk = jnp.einsum('bnhcd,bnhed->bnhce', k, k)
    lmat = jnp.where(strict, beta[..., :, None] * kk * decay, 0.0)
    amat = lmat + jnp.eye(DN_CHUNK, dtype=lmat.dtype)
    rhs = jnp.concatenate([v * beta[..., None], k * (beta * jnp.exp(g))[..., None]], axis=-1)
    sol = lax.linalg.triangular_solve(amat, rhs, left_side=True, lower=True, unit_diagonal=True)
    u, w = sol[..., :DV], sol[..., DV:]
    qk = jnp.einsum('bnhcd,bnhed->bnhce', q, k) * decay
    q_dec = q * jnp.exp(g)[..., None]
    k_dec = k * jnp.exp(g[..., -1:] - g)[..., None]
    g_last = jnp.exp(g[..., -1])

    def step(state, inp):
        qd, kd, u_c, w_c, qk_c, gl = inp
        v_new = u_c - jnp.einsum('bhcd,bhde->bhce', w_c, state)
        o = jnp.einsum('bhcd,bhde->bhce', qd, state) + jnp.einsum('bhcs,bhse->bhce', qk_c, v_new)
        state = state * gl[..., None, None] + jnp.einsum('bhcd,bhce->bhde', kd, v_new)
        return state, o

    xs = tuple(jnp.moveaxis(t, 1, 0) for t in (q_dec, k_dec, u, w, qk, g_last))
    _, o = lax.scan(step, jnp.zeros((B, H, DK, DV), jnp.float32), xs)
    return jnp.transpose(o, (1, 0, 3, 2, 4)).reshape(B, S, H, DV)

def stick_breaking_attention(q, k, v):
    B, S, H, Dh = q.shape
    nq = S // SB_BLOCK
    scale = Dh ** -0.5
    kf = k.astype(jnp.float32)
    vf = v.astype(jnp.float32)
    qb = jnp.moveaxis(q.astype(jnp.float32).reshape(B, nq, SB_BLOCK, H, Dh), 1, 0)
    key_pos = jnp.arange(S)

    def block(args):
        q_blk, i = args
        z = jnp.einsum('bqhd,bkhd->bhqk', q_blk, kf) * scale
        q_pos = i * SB_BLOCK + jnp.arange(SB_BLOCK)
        causal = key_pos[None, :] < q_pos[:, None]
        log_rem = jnp.where(causal, jax.nn.log_sigmoid(-z), 0.0)
        after = lax.cumsum(log_rem, axis=3, reverse=True) - log_rem
        attn = jnp.where(causal, jnp.exp(jax.nn.log_sigmoid(z) + after), 0.0)
        return jnp.einsum('bhqk,bkhd->bqhd', attn, vf)

    o = lax.map(block, (qb, jnp.arange(nq)))
    return jnp.moveaxis(o, 0, 1).reshape(B, S, H, Dh)

def hybrid_mixer(h, w_in, conv_w, a_log, dt_bias, out_norm, w_up_dn, w_up_sb, w_out):
    B, S, _ = h.shape
    proj = h @ w_in
    dn_qkv, dn_z, dn_b, dn_a, sb_q, sb_k, sb_v, gates = jnp.split(proj, SPLIT_AT, axis=-1)
    dn_qkv = causal_depthwise_conv(dn_qkv, conv_w)
    dq, dk, dv = jnp.split(dn_qkv, [DN_QK, 2 * DN_QK], axis=-1)
    q = l2_norm(dq.reshape(B, S, DN_HEADS, DN_DK)) * (DN_DK ** -0.5)
    k = l2_norm(dk.reshape(B, S, DN_HEADS, DN_DK))
    v = dv.reshape(B, S, DN_HEADS, DN_DV).astype(jnp.float32)
    beta = jax.nn.sigmoid(dn_b.astype(jnp.float32))
    g = -jnp.exp(a_log.astype(jnp.float32)) * jax.nn.softplus(dn_a.astype(jnp.float32) + dt_bias.astype(jnp.float32))
    o = gated_delta_rule(q, k, v, g, beta)
    o = rms_norm(o, out_norm) * jax.nn.silu(dn_z.reshape(B, S, DN_HEADS, DN_DV).astype(jnp.float32))
    y_dn = o.reshape(B, S, DN_V).astype(h.dtype) @ w_up_dn
    o_sb = stick_breaking_attention(sb_q.reshape(B, S, SB_HEADS, SB_DH),
                                    sb_k.reshape(B, S, SB_HEADS, SB_DH),
                                    sb_v.reshape(B, S, SB_HEADS, SB_DH))
    y_sb = o_sb.reshape(B, S, SB_W).astype(h.dtype) @ w_up_sb
    g_dn, g_sb = jnp.split(jax.nn.sigmoid(gates), N_BRANCH, axis=-1)
    return (g_dn * y_dn + g_sb * y_sb) @ w_out

def swiglu(h, w1, w3, w2):
    return (jax.nn.silu(h @ w1) * (h @ w3)) @ w2

def moe_swiglu(h, router_w, router_b, w1, w3, w2):
    B, S, D = h.shape
    T = B * S
    hf = h.reshape(T, D)
    logits = (hf @ router_w).astype(jnp.float32) + router_b.astype(jnp.float32)
    top_logit, top_idx = lax.top_k(logits, TOP_K)
    top_w = jax.nn.softmax(top_logit, axis=-1)
    n_assign = T * TOP_K
    flat_e = top_idx.reshape(-1).astype(jnp.int32)
    flat_tok = jnp.arange(n_assign, dtype=jnp.int32) // TOP_K
    order = jnp.argsort(flat_e)
    e_sorted = flat_e[order]
    counts = jnp.bincount(flat_e, length=N_EXPERTS).astype(jnp.int32)
    padded = (counts + MOE_BLOCK - 1) // MOE_BLOCK * MOE_BLOCK
    pad_end = jnp.cumsum(padded)
    pad_start = pad_end - padded
    start = jnp.cumsum(counts) - counts
    dest = pad_start[e_sorted] + jnp.arange(n_assign, dtype=jnp.int32) - start[e_sorted]
    n_rows = (n_assign + N_EXPERTS * (MOE_BLOCK - 1) + MOE_BLOCK - 1) // MOE_BLOCK * MOE_BLOCK
    n_blocks = n_rows // MOE_BLOCK
    row_tok = jnp.full((n_rows,), T, jnp.int32).at[dest].set(flat_tok[order])
    row_w = jnp.zeros((n_rows,), jnp.float32).at[dest].set(top_w.reshape(-1)[order])
    block_start = jnp.arange(n_blocks, dtype=jnp.int32) * MOE_BLOCK
    block_e = jnp.minimum(jnp.sum(pad_end[None, :] <= block_start[:, None], axis=1), N_EXPERTS - 1)
    h_pad = jnp.concatenate([hf, jnp.zeros((1, D), hf.dtype)], axis=0)

    def expert_block(args):
        toks, e = args
        xb = h_pad[toks]
        return (jax.nn.silu(xb @ w1[e]) * (xb @ w3[e])) @ w2[e]

    y = lax.map(expert_block, (row_tok.reshape(n_blocks, MOE_BLOCK), block_e))
    y = y.reshape(n_rows, D) * row_w[:, None].astype(h.dtype)
    out = jax.ops.segment_sum(y, row_tok, num_segments=T + 1)[:T]
    return out.reshape(B, S, D)

def first_inputs(seed: int = 0) -> dict:
    key = jax.random.key(seed)
    ks = jax.random.split(key, 26)
    f32 = jnp.float32

    def nrm(k, shape, scale):
        return jax.random.normal(k, shape, f32) * scale

    L = DEPTH
    dt = jnp.exp(jax.random.uniform(ks[9], (L, DN_HEADS), f32, math.log(1e-3), math.log(1e-1)))
    return {
        "x": nrm(ks[0], (BATCH, SEQ, D_MODEL), 1.0),
        "c": nrm(ks[1], (BATCH, D_MODEL), 1.0),
        "ada_w": nrm(ks[2], (L, D_MODEL, 6 * D_MODEL), 0.5 * D_MODEL ** -0.5),
        "ada_b": nrm(ks[3], (L, 6 * D_MODEL), 0.02),
        "norm_mix": 1.0 + nrm(ks[4], (L, D_MODEL), 0.05),
        "norm_ffn": 1.0 + nrm(ks[5], (L, D_MODEL), 0.05),
        "w_in": nrm(ks[6], (L, D_MODEL, IN_COLS), D_MODEL ** -0.5),
        "conv_w": nrm(ks[7], (L, DN_CONV, 2 * DN_QK + DN_V), DN_CONV ** -0.5),
        "dn_a_log": jnp.log(jax.random.uniform(ks[8], (L, DN_HEADS), f32, 1.0, 16.0)),
        "dn_dt_bias": dt + jnp.log(-jnp.expm1(-dt)),
        "dn_out_norm": 1.0 + nrm(ks[10], (L, DN_DV), 0.05),
        "w_up_dn": nrm(ks[11], (L, DN_V, D_MODEL), DN_V ** -0.5),
        "w_up_sb": nrm(ks[12], (L, SB_W, D_MODEL), SB_W ** -0.5),
        "w_out": nrm(ks[13], (L, D_MODEL, D_MODEL), D_MODEL ** -0.5),
        "ffn_w1": nrm(ks[14], (N_DENSE, D_MODEL, D_FF), D_MODEL ** -0.5),
        "ffn_w3": nrm(ks[15], (N_DENSE, D_MODEL, D_FF), D_MODEL ** -0.5),
        "ffn_w2": nrm(ks[16], (N_DENSE, D_FF, D_MODEL), D_FF ** -0.5),
        "router_w": nrm(ks[17], (N_MOE, D_MODEL, N_EXPERTS), D_MODEL ** -0.5),
        "router_b": nrm(ks[18], (N_MOE, N_EXPERTS), 0.01),
        "moe_w1": nrm(ks[19], (N_MOE, N_EXPERTS, D_MODEL, D_FF), D_MODEL ** -0.5),
        "moe_w3": nrm(ks[20], (N_MOE, N_EXPERTS, D_MODEL, D_FF), D_MODEL ** -0.5),
        "moe_w2": nrm(ks[21], (N_MOE, N_EXPERTS, D_FF, D_MODEL), D_FF ** -0.5),
        "final_norm": 1.0 + nrm(ks[22], (D_MODEL,), 0.05),
    }

def first_block(x, c, ada_w, ada_b, norm_mix, norm_ffn, w_in, conv_w, dn_a_log, dn_dt_bias,
              dn_out_norm, w_up_dn, w_up_sb, w_out, ffn_w1, ffn_w3, ffn_w2, router_w, router_b,
              moe_w1, moe_w3, moe_w2, final_norm):
    c_act = jax.nn.silu(c)
    for l in range(DEPTH):
        mod = (c_act @ ada_w[l] + ada_b[l])[:, None, :]
        sh1, sc1, gt1, sh2, sc2, gt2 = jnp.split(mod, 6, axis=-1)
        h = rms_norm(x, norm_mix[l]) * (1.0 + sc1) + sh1
        x = x + gt1 * hybrid_mixer(h, w_in[l], conv_w[l], dn_a_log[l], dn_dt_bias[l], dn_out_norm[l],
                                   w_up_dn[l], w_up_sb[l], w_out[l])
        h = rms_norm(x, norm_ffn[l]) * (1.0 + sc2) + sh2
        if l % 2 == 0:
            f = swiglu(h, ffn_w1[l // 2], ffn_w3[l // 2], ffn_w2[l // 2])
        else:
            j = l // 2
            f = moe_swiglu(h, router_w[j], router_b[j], moe_w1[j], moe_w3[j], moe_w2[j])
        x = x + gt2 * f
    return rms_norm(x, final_norm)


N_A_LAYERS = DEPTH // 2
N_B_LAYERS = DEPTH - N_A_LAYERS
D_FF_2 = 2816
RMS_EPS = 1e-6

S5_GROUP_CH = 16
S5_GROUPS = D_MODEL // S5_GROUP_CH
S5_STATE = 64
DT_MIN = 0.001
DT_MAX = 0.1

N_HEADS = 16
HEAD_DIM = D_MODEL // N_HEADS
N_KV_HEADS = 4
Q_PER_KV = N_HEADS // N_KV_HEADS
CMP_LEN = 32
CMP_STRIDE = 16
CMP_HIDDEN = 2 * HEAD_DIM
SEL_LEN = 64
SEL_TOPN = 8
WIN = 512
WIN_QB = 128
SEL_QB = 64
N_BRANCH_2 = 3
ATTN_SCALE = HEAD_DIM ** -0.5

NUM_BUCKETS = 32
MAX_DISTANCE = 128

NEG_INF = -1e30
BIG = 1e9


def _rmsnorm(x, g):
    xf = x.astype(jnp.float32)
    y = xf * lax.rsqrt(jnp.mean(xf * xf, axis=-1, keepdims=True) + RMS_EPS)
    return (y * g.astype(jnp.float32)).astype(x.dtype)

def _swiglu(x, w_in, w_out):
    a, b = jnp.split(x @ w_in, 2, axis=-1)
    return (jax.nn.silu(a) * b) @ w_out

def _rel_bucket(dist):
    n = jnp.maximum(dist, 0)
    max_exact = NUM_BUCKETS // 2
    logv = jnp.log(jnp.maximum(n, 1).astype(jnp.float32) / max_exact) / math.log(MAX_DISTANCE / max_exact)
    large = jnp.minimum(max_exact + (logv * (NUM_BUCKETS - max_exact)).astype(jnp.int32), NUM_BUCKETS - 1)
    return jnp.where(n < max_exact, n, large)

def _masked_softmax(logits, mask):
    return jax.nn.softmax(jnp.where(mask, logits, NEG_INF), axis=-1)

def _s5_mixer(u, a_re, a_im, log_dt, b_re, b_im, c_re, c_im, d_skip, w_glu):
    bsz, seq, _ = u.shape
    ug = u.reshape(bsz, seq, S5_GROUPS, S5_GROUP_CH)
    dt = jnp.exp(log_dt)[:, None]
    mag = jnp.exp(a_re * dt)
    ab_re = mag * jnp.cos(a_im * dt)
    ab_im = mag * jnp.sin(a_im * dt)
    den = a_re * a_re + a_im * a_im
    z_re = ((ab_re - 1.0) * a_re + ab_im * a_im) / den
    z_im = (ab_im * a_re - (ab_re - 1.0) * a_im) / den
    bb_re = z_re[..., None] * b_re - z_im[..., None] * b_im
    bb_im = z_re[..., None] * b_im + z_im[..., None] * b_re
    bu_re = jnp.einsum('bsgh,gph->bsgp', ug, bb_re)
    bu_im = jnp.einsum('bsgh,gph->bsgp', ug, bb_im)
    shape = (1, seq, S5_GROUPS, S5_STATE)
    la_re = jnp.broadcast_to(ab_re, shape)
    la_im = jnp.broadcast_to(ab_im, shape)

    def combine(e1, e2):
        ar1, ai1, br1, bi1 = e1
        ar2, ai2, br2, bi2 = e2
        return (ar2 * ar1 - ai2 * ai1,
                ar2 * ai1 + ai2 * ar1,
                ar2 * br1 - ai2 * bi1 + br2,
                ar2 * bi1 + ai2 * br1 + bi2)

    _, _, x_re, x_im = lax.associative_scan(combine, (la_re, la_im, bu_re, bu_im), axis=1)
    y = (jnp.einsum('bsgp,ghp->bsgh', x_re, c_re) - jnp.einsum('bsgp,ghp->bsgh', x_im, c_im)
         + d_skip * ug)
    y = jax.nn.gelu(y.reshape(bsz, seq, D_MODEL))
    return y * jax.nn.sigmoid(y @ w_glu)

def _shared_kv(h, kv_norm, w_kv, k_norm_cmp, k_norm_slc, k_norm_win,
               cmp_pos_k, cmp_pos_v, cmp_k_w1, cmp_k_w2, cmp_v_w1, cmp_v_w2):
    bsz, seq, _ = h.shape
    kv = (_rmsnorm(h, kv_norm) @ w_kv).reshape(bsz, seq, 2 * N_BRANCH_2, N_KV_HEADS, HEAD_DIM)
    n_cmp = (seq - CMP_LEN) // CMP_STRIDE + 1
    blk = jnp.arange(n_cmp)[:, None] * CMP_STRIDE + jnp.arange(CMP_LEN)[None, :]

    def compress(src, pos, w1, w2):
        blocks = src[:, blk] + pos[None, None, :, None, :]
        hid = jax.nn.gelu(jnp.einsum('bclgd,ldh->bcgh', blocks, w1))
        return jnp.einsum('bcgh,hd->bcgd', hid, w2)

    k_cmp = _rmsnorm(compress(kv[:, :, 0], cmp_pos_k, cmp_k_w1, cmp_k_w2), k_norm_cmp)
    v_cmp = compress(kv[:, :, 1], cmp_pos_v, cmp_v_w1, cmp_v_w2)
    k_slc = _rmsnorm(kv[:, :, 2], k_norm_slc)
    v_slc = kv[:, :, 3]
    k_win = _rmsnorm(kv[:, :, 4], k_norm_win)
    v_win = kv[:, :, 5]
    return (k_cmp, v_cmp, k_slc, v_slc, k_win, v_win)

def _compressed_branch(q, k_cmp, v_cmp, rel_bias):
    seq = q.shape[1]
    n_cmp = k_cmp.shape[1]
    n_sel = seq // SEL_LEN
    t = jnp.arange(seq)
    c_start = jnp.arange(n_cmp) * CMP_STRIDE
    dist = t[:, None] - (c_start + CMP_LEN - 1)[None, :]
    valid = dist >= 0
    bias = rel_bias[_rel_bucket(dist)].transpose(2, 0, 1).reshape(N_KV_HEADS, Q_PER_KV, seq, n_cmp)
    logits = jnp.einsum('bsgrd,bcgd->bgrsc', q, k_cmp).astype(jnp.float32) * ATTN_SCALE + bias
    p = _masked_softmax(logits, valid) * jnp.any(valid, axis=-1)[:, None].astype(jnp.float32)
    o = jnp.einsum('bgrsc,bcgd->bsgrd', p.astype(v_cmp.dtype), v_cmp)
    j_start = jnp.arange(n_sel) * SEL_LEN
    ov = jnp.clip(jnp.minimum(c_start[:, None] + CMP_LEN, j_start[None, :] + SEL_LEN)
                  - jnp.maximum(c_start[:, None], j_start[None, :]), 0, None)
    overlap = ov.astype(jnp.float32) / CMP_LEN
    p_slc = jnp.einsum('bgrsc,cj->bgsj', p, overlap)
    return o, p_slc

def _select_blocks(p_slc):
    seq, n_sel = p_slc.shape[2], p_slc.shape[3]
    k = min(SEL_TOPN, n_sel)
    t = jnp.arange(seq)[:, None]
    j = jnp.arange(n_sel)[None, :]
    cur = t // SEL_LEN
    forced = (j == 0) | (j == cur) | (j == cur - 1)
    causal = j * SEL_LEN <= t
    score = jnp.where(forced, BIG, jnp.where(causal, p_slc, -BIG))
    _, idx = lax.top_k(score, k)
    return idx

def _selected_branch(q, k_slc, v_slc, idx, rel_bias):
    bsz, seq = q.shape[0], q.shape[1]
    n_top = idx.shape[-1]
    kl = n_top * SEL_LEN
    n_ch = seq // SEL_QB
    kst = k_slc.transpose(0, 2, 1, 3)
    vst = v_slc.transpose(0, 2, 1, 3)
    table = rel_bias.reshape(NUM_BUCKETS, N_KV_HEADS, Q_PER_KV).transpose(1, 0, 2)
    gather = jax.vmap(jax.vmap(lambda a, i: a[i]))
    qc = q.reshape(bsz, n_ch, SEL_QB, N_KV_HEADS, Q_PER_KV, HEAD_DIM).transpose(1, 0, 2, 3, 4, 5)
    ic = idx.reshape(bsz, N_KV_HEADS, n_ch, SEL_QB, n_top).transpose(2, 0, 1, 3, 4)

    def step(args):
        ci, qb, ib = args
        tok = (ib[..., None] * SEL_LEN + jnp.arange(SEL_LEN)).reshape(bsz, N_KV_HEADS, SEL_QB * kl)
        kg = gather(kst, tok).reshape(bsz, N_KV_HEADS, SEL_QB, kl, HEAD_DIM)
        vg = gather(vst, tok).reshape(bsz, N_KV_HEADS, SEL_QB, kl, HEAD_DIM)
        tok = tok.reshape(bsz, N_KV_HEADS, SEL_QB, kl)
        qpos = ci * SEL_QB + jnp.arange(SEL_QB)
        dist = qpos[None, None, :, None] - tok
        bias = table[jnp.arange(N_KV_HEADS)[None, :, None, None], _rel_bucket(dist)]
        logits = (jnp.einsum('bqgrd,bgqkd->bgrqk', qb, kg).astype(jnp.float32) * ATTN_SCALE
                  + bias.transpose(0, 1, 4, 2, 3))
        p = _masked_softmax(logits, (dist >= 0)[:, :, None])
        return jnp.einsum('bgrqk,bgqkd->bqgrd', p.astype(vg.dtype), vg)

    out = lax.map(step, (jnp.arange(n_ch), qc, ic))
    return out.transpose(1, 0, 2, 3, 4, 5).reshape(bsz, seq, N_KV_HEADS, Q_PER_KV, HEAD_DIM)

def _window_branch(q, k_win, v_win, rel_bias):
    bsz, seq = q.shape[0], q.shape[1]
    n_blk = seq // WIN_QB
    span = WIN + WIN_QB
    kp = jnp.pad(k_win, ((0, 0), (WIN, 0), (0, 0), (0, 0)))
    vp = jnp.pad(v_win, ((0, 0), (WIN, 0), (0, 0), (0, 0)))
    dist = WIN + jnp.arange(WIN_QB)[:, None] - jnp.arange(span)[None, :]
    band = (dist >= 0) & (dist < WIN)
    bias = rel_bias[_rel_bucket(dist)].transpose(2, 0, 1).reshape(N_KV_HEADS, Q_PER_KV, WIN_QB, span)
    qb_all = q.reshape(bsz, n_blk, WIN_QB, N_KV_HEADS, Q_PER_KV, HEAD_DIM).transpose(1, 0, 2, 3, 4, 5)

    def step(args):
        bi, qb = args
        start = bi * WIN_QB
        kb = lax.dynamic_slice_in_dim(kp, start, span, axis=1)
        vb = lax.dynamic_slice_in_dim(vp, start, span, axis=1)
        kpos = start - WIN + jnp.arange(span)
        mask = band & (kpos >= 0)[None, :]
        logits = jnp.einsum('bqgrd,bkgd->bgrqk', qb, kb).astype(jnp.float32) * ATTN_SCALE + bias
        p = _masked_softmax(logits, mask)
        return jnp.einsum('bgrqk,bkgd->bqgrd', p.astype(vb.dtype), vb)

    out = lax.map(step, (jnp.arange(n_blk), qb_all))
    return out.transpose(1, 0, 2, 3, 4, 5).reshape(bsz, seq, N_KV_HEADS, Q_PER_KV, HEAD_DIM)

def _nsa_mixer(u, kv, w_qg, q_norm, w_o, rel_bias):
    k_cmp, v_cmp, k_slc, v_slc, k_win, v_win = kv
    bsz, seq, _ = u.shape
    qg = u @ w_qg
    q = _rmsnorm(qg[..., :N_HEADS * HEAD_DIM].reshape(bsz, seq, N_KV_HEADS, Q_PER_KV, HEAD_DIM), q_norm)
    gates = jax.nn.sigmoid(qg[..., N_HEADS * HEAD_DIM:].reshape(bsz, seq, N_KV_HEADS, Q_PER_KV, N_BRANCH_2))
    o_cmp, p_slc = _compressed_branch(q, k_cmp, v_cmp, rel_bias)
    idx = _select_blocks(p_slc)
    o_slc = _selected_branch(q, k_slc, v_slc, idx, rel_bias)
    o_win = _window_branch(q, k_win, v_win, rel_bias)
    o = gates[..., 0:1] * o_cmp + gates[..., 1:2] * o_slc + gates[..., 2:3] * o_win
    return o.reshape(bsz, seq, D_MODEL) @ w_o

def second_inputs(seed: int = 0) -> dict:
    key = jax.random.key(seed)
    ks = iter(jax.random.split(key, 40))

    def nrm(shape, scale):
        return jax.random.normal(next(ks), shape, jnp.float32) * scale

    def gain(shape):
        return 1.0 + nrm(shape, 0.02)

    na, nb = N_A_LAYERS, N_B_LAYERS
    g, p, ch = S5_GROUPS, S5_STATE, S5_GROUP_CH
    return {
        'x': nrm((BATCH, SEQ, D_MODEL), 1.0),
        'rel_bias': nrm((NUM_BUCKETS, N_HEADS), 0.5),
        'ffn1_norm': gain((DEPTH, D_MODEL)),
        'ffn1_w_in': nrm((DEPTH, D_MODEL, 2 * D_FF_2), D_MODEL ** -0.5),
        'ffn1_w_out': nrm((DEPTH, D_FF_2, D_MODEL), D_FF_2 ** -0.5),
        'mix_norm': gain((DEPTH, D_MODEL)),
        'ffn2_norm': gain((DEPTH, D_MODEL)),
        'ffn2_w_in': nrm((DEPTH, D_MODEL, 2 * D_FF_2), D_MODEL ** -0.5),
        'ffn2_w_out': nrm((DEPTH, D_FF_2, D_MODEL), D_FF_2 ** -0.5),
        's5_a_re': -0.5 + nrm((na, g, p), 0.01),
        's5_a_im': jnp.pi * jnp.arange(p, dtype=jnp.float32)[None, None, :] + nrm((na, g, p), 0.01),
        's5_log_dt': jax.random.uniform(next(ks), (na, g), jnp.float32, math.log(DT_MIN), math.log(DT_MAX)),
        's5_b_re': nrm((na, g, p, ch), (2.0 * ch) ** -0.5),
        's5_b_im': nrm((na, g, p, ch), (2.0 * ch) ** -0.5),
        's5_c_re': nrm((na, g, ch, p), (2.0 * p) ** -0.5),
        's5_c_im': nrm((na, g, ch, p), (2.0 * p) ** -0.5),
        's5_d': nrm((na, g, ch), 1.0),
        's5_w_glu': nrm((na, D_MODEL, D_MODEL), D_MODEL ** -0.5),
        'kv_norm': gain((D_MODEL,)),
        'w_kv': nrm((D_MODEL, 2 * N_BRANCH_2 * N_KV_HEADS * HEAD_DIM), D_MODEL ** -0.5),
        'k_norm_cmp': gain((HEAD_DIM,)),
        'k_norm_slc': gain((HEAD_DIM,)),
        'k_norm_win': gain((HEAD_DIM,)),
        'cmp_pos_k': nrm((CMP_LEN, HEAD_DIM), 0.1),
        'cmp_pos_v': nrm((CMP_LEN, HEAD_DIM), 0.1),
        'cmp_k_w1': nrm((CMP_LEN, HEAD_DIM, CMP_HIDDEN), (CMP_LEN * HEAD_DIM) ** -0.5),
        'cmp_k_w2': nrm((CMP_HIDDEN, HEAD_DIM), CMP_HIDDEN ** -0.5),
        'cmp_v_w1': nrm((CMP_LEN, HEAD_DIM, CMP_HIDDEN), (CMP_LEN * HEAD_DIM) ** -0.5),
        'cmp_v_w2': nrm((CMP_HIDDEN, HEAD_DIM), CMP_HIDDEN ** -0.5),
        'w_qg': nrm((nb, D_MODEL, N_HEADS * HEAD_DIM + N_BRANCH_2 * N_HEADS), D_MODEL ** -0.5),
        'q_norm': gain((nb, HEAD_DIM)),
        'w_o': nrm((nb, D_MODEL, D_MODEL), D_MODEL ** -0.5),
    }

def second_block(x, rel_bias, ffn1_norm, ffn1_w_in, ffn1_w_out, mix_norm, ffn2_norm, ffn2_w_in, ffn2_w_out,
              s5_a_re, s5_a_im, s5_log_dt, s5_b_re, s5_b_im, s5_c_re, s5_c_im, s5_d, s5_w_glu,
              kv_norm, w_kv, k_norm_cmp, k_norm_slc, k_norm_win, cmp_pos_k, cmp_pos_v,
              cmp_k_w1, cmp_k_w2, cmp_v_w1, cmp_v_w2, w_qg, q_norm, w_o):
    h = x
    kv = None
    for layer in range(DEPTH):
        h = h + 0.5 * _swiglu(_rmsnorm(h, ffn1_norm[layer]), ffn1_w_in[layer], ffn1_w_out[layer])
        u = _rmsnorm(h, mix_norm[layer])
        if layer < N_A_LAYERS:
            a = layer
            h = h + _s5_mixer(u, s5_a_re[a], s5_a_im[a], s5_log_dt[a], s5_b_re[a], s5_b_im[a],
                              s5_c_re[a], s5_c_im[a], s5_d[a], s5_w_glu[a])
        else:
            b = layer - N_A_LAYERS
            h = h + _nsa_mixer(u, kv, w_qg[b], q_norm[b], w_o[b], rel_bias)
        h = h + 0.5 * _swiglu(_rmsnorm(h, ffn2_norm[layer]), ffn2_w_in[layer], ffn2_w_out[layer])
        if layer == N_A_LAYERS - 1:
            kv = _shared_kv(h, kv_norm, w_kv, k_norm_cmp, k_norm_slc, k_norm_win,
                            cmp_pos_k, cmp_pos_v, cmp_k_w1, cmp_k_w2, cmp_v_w1, cmp_v_w2)
    return h


def setup_inputs(seed=0):
    out = dict(first_inputs(seed))
    for name, value in second_inputs(seed + 1).items():
        if name != "x":
            out[name + "_2"] = value
    return out


def reference(
    x, c, ada_w, ada_b, norm_mix, norm_ffn, w_in, conv_w, dn_a_log, dn_dt_bias, dn_out_norm,
    w_up_dn, w_up_sb, w_out, ffn_w1, ffn_w3, ffn_w2, router_w, router_b, moe_w1, moe_w3, moe_w2,
    final_norm, rel_bias_2, ffn1_norm_2, ffn1_w_in_2, ffn1_w_out_2, mix_norm_2, ffn2_norm_2,
    ffn2_w_in_2, ffn2_w_out_2, s5_a_re_2, s5_a_im_2, s5_log_dt_2, s5_b_re_2, s5_b_im_2,
    s5_c_re_2, s5_c_im_2, s5_d_2, s5_w_glu_2, kv_norm_2, w_kv_2, k_norm_cmp_2, k_norm_slc_2,
    k_norm_win_2, cmp_pos_k_2, cmp_pos_v_2, cmp_k_w1_2, cmp_k_w2_2, cmp_v_w1_2, cmp_v_w2_2,
    w_qg_2, q_norm_2, w_o_2,
):
    x = first_block(
        x, c, ada_w, ada_b, norm_mix, norm_ffn, w_in, conv_w, dn_a_log, dn_dt_bias, dn_out_norm,
        w_up_dn, w_up_sb, w_out, ffn_w1, ffn_w3, ffn_w2, router_w, router_b, moe_w1, moe_w3,
        moe_w2, final_norm,
    )
    return second_block(
        x, rel_bias_2, ffn1_norm_2, ffn1_w_in_2, ffn1_w_out_2, mix_norm_2, ffn2_norm_2,
        ffn2_w_in_2, ffn2_w_out_2, s5_a_re_2, s5_a_im_2, s5_log_dt_2, s5_b_re_2, s5_b_im_2,
        s5_c_re_2, s5_c_im_2, s5_d_2, s5_w_glu_2, kv_norm_2, w_kv_2, k_norm_cmp_2, k_norm_slc_2,
        k_norm_win_2, cmp_pos_k_2, cmp_pos_v_2, cmp_k_w1_2, cmp_k_w2_2, cmp_v_w1_2, cmp_v_w2_2,
        w_qg_2, q_norm_2, w_o_2,
    )


_drawn_inputs = setup_inputs


def setup_inputs(seed=0):
    import zlib

    import numpy as np

    out = dict(_drawn_inputs(seed))
    spreads = {}
    factors = {'dn_out_norm': 4.417,
     'router_b': 4.964,
     'ffn1_norm_2': 4.886,
     'mix_norm_2': 6.028,
     'ffn2_norm_2': 5.365,
     's5_a_re_2': 64.0,
     's5_a_im_2': 2.705,
     's5_log_dt_2': 2.775,
     's5_b_re_2': 3.764,
     's5_b_im_2': 3.806,
     's5_c_re_2': 3.769,
     's5_c_im_2': 3.762,
     'kv_norm_2': 8.0,
     'k_norm_cmp_2': 36.566,
     'k_norm_slc_2': 8.0,
     'k_norm_win_2': 8.0,
     'cmp_pos_k_2': 8.0,
     'q_norm_2': 8.0,
     'cmp_pos_v_2': 8.0}
    for name, (base, spread) in spreads.items():
        noise = np.random.default_rng([zlib.crc32(name.encode()), seed]).standard_normal(out[name].shape)
        drawn = base * np.exp(spread * noise) if base else spread * noise
        out[name] = __import__('jax').numpy.asarray(drawn.astype(out[name].dtype))
    for name, factor in factors.items():
        out[name] = (out[name] * factor).astype(out[name].dtype)
    return out
```

```python
from contextlib import ExitStack

import concourse.bass as bass
from concourse import mybir
import numpy as np

F32 = mybir.dt.float32
U32 = mybir.dt.uint32
ALU = mybir.AluOpType
ACT = mybir.ActivationFunctionType
AX = mybir.AxisListType.X

P = 128
TOK = 256
NT = TOK // P
D = 1024
KT = D // P
LAYERS = 2
HEADS = 8
FF1 = 3584
FF2 = 2816
EXPERTS = 8
BLK1 = FF1 // 256
BLK2 = FF2 // 256
STATES = 64
PAIRS = 32
QH = 16
NCMP = (TOK - 32) // 16 + 1
NEG = -1e30
EPS = 1e-6
RING = 6
UNIT = 2048
TWO_PI = 2 * np.pi


def columns(spec):
    at, out = 0, {}
    for name, width in spec:
        out[name] = at
        at += width
    out["width"] = at
    return out


CC = columns([("ident", 128), ("ones", 128), ("half_ones", 128), ("upper", 128), ("lower_strict", 128),
              ("key_after", 128), ("level0_lower", 128), ("level", 7 * 128), ("stick_mask", 384), ("iota", 8),
              ("cmp_add", NT * NCMP), ("cmp_mul", NT * NCMP), ("onehot", 511)])
PC = columns([("c", 8), ("ada_b", 96), ("norm_mix", 16), ("norm_ffn", 16), ("conv_w", 192), ("dn_out_norm", 2),
              ("dt_bias", 32), ("a_log", 32), ("final_norm", 8), ("router_b", 16), ("ffn1_norm", 16),
              ("mix_norm", 16), ("ffn2_norm", 16), ("s5_d", 8), ("kv_norm", 8), ("k_norm_cmp", 1),
              ("k_norm_slc", 1), ("k_norm_win", 1), ("q_norm", 1), ("a_re", 32), ("a_im", 32), ("log_dt", 32),
              ("pos_k", 32), ("pos_v", 32), ("w_ba", 256), ("router_w", 64), ("w_gate", 384), ("w2_k", 128),
              ("w2_v", 128), ("rel_bias", 16)])
UN = columns([("ada0", 24), ("ada1", 24), ("w_in0", 30), ("up0", 6), ("w_out0", 4), ("ffn", 3 * BLK1),
              ("w_in1", 30), ("up1", 6), ("w_out1", 4), ("moe", 3 * BLK1 * EXPERTS),
              ("ffn1_0", 3 * BLK2), ("glu", 4), ("ffn2_0", 3 * BLK2), ("kv", 6), ("ffn1_1", 3 * BLK2),
              ("q", 4), ("w_o", 4), ("ffn2_1", 3 * BLK2)])
NUNITS = UN["width"]

TOTAL = dict(
    norm_sq=1, norm_sum=1, norm_ln=1, norm_rs=1, norm_scaled=8, normed=8,
    ada_psum=4, ada_out=4,
    evac=30, conv_y=3, conv_out=3,
    ba=1,
    lvl_lt=6,
)


def program(nc, A):
    ctx = ExitStack()
    with ctx:
        def sb(name, cols, dt=F32):
            return ctx.enter_context(nc.sbuf_tensor(name, [P, cols], dt))

        sems = {}

        def sem(name):
            if name not in sems:
                sems[name] = ctx.enter_context(nc.semaphore(name))
            return sems[name]

        def at(name, count, stage=0, total=None):
            return sem(name), stage * (TOTAL[name] if total is None else total) + count

        ring = [sb(f"ring{r}", UNIT) for r in range(RING)]
        X = sb("x", KT * TOK)
        CON = sb("constants", CC["width"])
        PAR = sb("parameters", PC["width"])
        WORK = 28160
        HB, FSB, FGB = WORK, WORK + 2048, WORK + 3072
        BIG = sb("big", WORK + 4096)
        H = BIG[:, HB:HB + KT * TOK]
        FS = BIG[:, FSB:FSB + 1024]
        FG = BIG[:, FGB:FGB + 1024]
        RS = sb("inverse_rms", TOK)
        LNB = sb("log_mean_square", TOK)
        EPSB = sb("epsilon", 2)
        MOD = sb("modulation", 96)
        NSC = sb("norm_scale", 8)
        SM = sb("small", 1280)
        SMU = sb("small_idx", 32, U32)
        PS = ctx.enter_context(nc.psum_tensor("banks", [P, 8 * 512], F32))
        bank = [PS[:, b * 512:(b + 1) * 512] for b in range(8)]

        def view(t, off, dims, p0=0, pn=P):
            a = t if isinstance(t, bass.AP) else t[:, :]
            row = a.ap[0][0]
            return bass.AP(tensor=a.tensor, offset=a.offset + p0 * row + off, ap=[[row, pn]] + dims)

        def con(name, width=128, extra=0, p0=0, pn=P):
            return CON[p0:p0 + pn, CC[name] + extra:CC[name] + extra + width]

        def par(name, width, extra=0, p0=0, pn=P):
            return PAR[p0:p0 + pn, PC[name] + extra:PC[name] + extra + width]

        ident = con("ident")
        ones = con("ones")
        half_ones = con("half_ones")
        upper = con("upper")

        PROJ, CONV, SC = 0, 15360, 21504
        Z_, SBQ, SBK, SBV, GATES = 24 * TOK, 32 * TOK, 36 * TOK, 40 * TOK, 44 * TOK
        SLOT = dict(A=0, B=2048, C=4096, D=SC, E=SC + 2048, F=SC + 4096)
        SQ0 = FSB
        EG, WT, ST = FSB, FGB, HB
        LTS, UBUF = (SLOT["A"], HB), SLOT["D"]
        OD, OSB = SLOT["E"], SLOT["F"]
        ZB, SP, VT = 0, 3072, SLOT["D"]
        GR, YE, YT, SELT, HG, YS = 0, 2048, 4096, 6144, 8192, 16384
        GD, HN, SEL, SELG, SLOTS = YE, YT, 24576, FSB, 26624
        GATE, MASK, PLACE, COUNT = 88, 104, 120, 136
        TC, TS, S5P, BBX, BBT, CX, PT1 = 0, 8192, 16384, 18432, 20480, 22528, 25600
        VR, VI, YR, YI, YB = 25600, 26624, BBX, BBX + 1024, S5P
        ROT = (VR, VI, FSB, FGB)
        KV, W1, SRC, KSQ, KRS, KT2 = 0, 3072, 11264, 13824, 14848, 15872
        KD, VN, BTAB, CB, BT, CP = 16896, 18944, 19968, 20352, 20832, 24928
        GT, KC, VC = 27700, 27800, 27864
        QB, OB, LG, PT, CPT = 0, 2048, 4096, 10240, HB

        def big(off, width, p0=0, pn=P):
            return BIG[p0:p0 + pn, off:off + width]

        tab_dram = A["tab"]
        HID = (6 * 512, 7 * 512 + 384)

        steps = {}

        def link(eng, name, ins):
            steps[name] = steps.get(name, 0) + 1
            ins.then_inc(sem(name), 1)
            eng.wait_ge(sem(name), steps[name])

        stage_no = {}

        def stage_end(eng, who):
            stage_no[who] = stage_no.get(who, 0) + 1
            eng.drain().then_inc(sem("stage_done"), 1)
            eng.wait_ge(sem("stage_done"), 4 * stage_no[who])

        stage = ctx.enter_context(nc.Block())

        @stage.sync
        def _(sp):
            sp.dma_start(PAR[:, :], A["par"]).then_inc(sem("inputs"), 16)
            for r in range(RING):
                sp.dma_start(ring[r][:, :], A["wall"][r]).then_inc(sem(f"loaded{r}"), 16)
            sp.dma_start(X[:, :], A["x"]).then_inc(sem("inputs"), 16)
            sp.dma_start(CON[:, :], A["con"]).then_inc(sem("inputs"), 16)
            whole = NUNITS // RING
            with sp.Fori(1, whole) as m:
                for r in range(RING):
                    sp.wait_ge(sem("unit_done"), m * RING + (r + 1 - RING))
                    sp.dma_start(ring[r][:, :], A["wall"][m * RING + r]).then_inc(sem(f"loaded{r}"), 16)
            for n in range(whole * RING, NUNITS):
                sp.wait_ge(sem("unit_done"), n - RING + 1)
                sp.dma_start(ring[n % RING][:, :], A["wall"][n]).then_inc(sem(f"loaded{n % RING}"), 16)
            sp.wait_ge(sem("result"), 1)
            sp.dma_start(A["out"], X[:, :]).then_inc(sem("stored"), 16)
            sp.wait_ge(sem("stored"), 16)

        @stage.tensor
        def _(pe):
            def arrived(n, more=0):
                pe.wait_ge(sem(f"loaded{n % RING}"), more * 16 + 16 * (n // RING + 1))

            def tile(n, k):
                return ring[n % RING][:, k * P:(k + 1) * P]

            def cols_unit(n, dst, kt=KT, tiles=2, src=H, rounds=0, width=TOK, src_off=0):
                arrived(n, rounds)
                for t in range(tiles):
                    for k in range(kt):
                        mm = pe.matmul(dst(t), tile(n, k * tiles + t),
                                       src[:, src_off + k * width:src_off + (k + 1) * width],
                                       start=(k == 0), stop=(k == kt - 1))
                mm.then_inc(sem("unit_done"), 1)

            def half(b, t):
                return bank[b][:, t * TOK:(t + 1) * TOK]

            def norm(i):
                pe.wait_ge(*at("norm_sq", 1, i))
                for t in range(KT):
                    mm = pe.matmul(half(7, 0), ones, big(SQ0 + t * TOK, TOK), start=(t == 0), stop=(t == KT - 1))
                mm.then_inc(sem("norm_sum"), 1)
                pe.wait_ge(*at("normed", 8, i))

            def ada(l):
                with pe.Fori(0, 4) as i:
                    pe.wait_ge(sem("ada_free"), l * 4 + 1 + i)
                    for u in range(RING):
                        n = UN[f"ada{l}"] + u
                        cols_unit(n, lambda t: bank[0][:, 2 * u + t:2 * u + t + 1], src=SM, width=1, rounds=i)

            def project(l):
                with pe.Fori(0, 5) as i:
                    for u in range(RING):
                        pe.wait_ge(sem("evac"), l * 30 + i * RING + u + 1)
                        cols_unit(UN[f"w_in{l}"] + u, lambda t: half(u, t), rounds=i)
                for n in range(NT):
                    for k in range(KT):
                        mm = pe.matmul(bank[6][:, n * 16:n * 16 + 16], H[:, k * TOK + n * P:k * TOK + (n + 1) * P],
                                       par("w_ba", 16, l * 128 + k * 16), start=(k == 0), stop=(k == KT - 1))
                mm.then_inc(sem("ba"), 1)

            def qkc(which, h, n):
                return big(CONV + (which * HEADS + h) * TOK + n * P, P)

            def delta(l):
                pe.wait_ge(*at("qk_sq", 1, l, 1))
                pe.wait_ge(*at("beta_exp", 1, l, 1))
                pe.wait_ge(*at("a_abs", 1, l, 1))
                for b in range(8):
                    mm = pe.matmul(bank[b][:, :], ones, big(SLOT["D"] + b * 512, 512), start=True, stop=True)
                mm.then_inc(sem("qk_sum"), 1)
                pe.wait_ge(*at("gu", 1, l, 1))
                pe.wait_ge(*at("qk_normed", 1, l, 1))
                for b in range(4):
                    pe.matmul(bank[b][:, :], ones, big(SLOT["A"] + b * 512, 512), start=True, stop=True)
                pe.matmul(bank[4][:, 0:16], upper, SM[:, 64:80], start=True, stop=True)
                pe.matmul(bank[4][:, 16:32], ones, SM[:, 64:80], start=True, stop=True).then_inc(sem("cum"), 1)
                stage_end(pe, "pe")
                for which in (1, 0):
                    for n in range(NT):
                        for h in range(HEADS):
                            b = 4 * (1 - which) + n * 2 + h // 4
                            mm = pe.matmul(bank[b][:, (h % 4) * P:(h % 4 + 1) * P], qkc(1, h, n), qkc(which, h, n),
                                           start=True, stop=True)
                    mm.then_inc(sem("kk"), 1)
                pe.wait_ge(*at("lmat", 1, l, 1))
                for c in range(16):
                    mm = pe.transpose(bank[c // 4][:, (c % 4) * P:(c % 4 + 1) * P], big(SLOT["D"] + c * P, P), ident)
                mm.then_inc(sem("lt"), 1)
                stage_end(pe, "pe")
                for s in range(6):
                    for q in range(4):
                        pe.wait_ge(*at("level_mask", 4 * s + q + 1, l, 24))
                        if s:
                            pe.wait_ge(*at("level_t", 4 * (s - 1) + q + 1, l, 24))
                        for c in range(4):
                            x = (4 * q + c) * P
                            mm = pe.matmul(bank[q][:, c * P:(c + 1) * P], big(LTS[s % 2] + x, P), big(SLOT["E"] + x, P),
                                           start=True, stop=True)
                        mm.then_inc(sem("level_u"), 1)
                    for q in range(4):
                        pe.wait_ge(*at("level_uc", 4 * s + q + 1, l, 24))
                        if 4 * s + q >= 2:
                            pe.wait_ge(*at("level_t", 4 * s + q - 1, l, 24))
                        for c in range(4):
                            x = (4 * q + c) * P
                            pe.matmul(bank[4 + q % 2][:, c * P:(c + 1) * P], big(SLOT["F"] + x, P), big(UBUF + x, P),
                                      start=True, stop=True)
                            mm = pe.matmul(bank[6 + q % 2][:, c * P:(c + 1) * P], big(UBUF + x, P),
                                           big(SLOT["F"] + x, P), start=True, stop=True)
                        mm.then_inc(sem("level_p"), 1)
                stage_end(pe, "pe")
                for which in (1, 2):
                    for n in range(NT):
                        for h in range(HEADS):
                            b = 4 * (which - 1) + n * 2 + h // 4
                            mm = pe.transpose(bank[b][:, (h % 4) * P:(h % 4 + 1) * P], qkc(which, h, n), ident)
                mm.then_inc(sem("kvt"), 1)
                stage_end(pe, "pe")
                for h in range(HEADS):
                    pe.matmul(bank[h // 4][:, (h % 4) * P:(h % 4 + 1) * P], big(SLOT["F"] + h * P, P),
                              big(SLOT["D"] + h * P, P), start=True, stop=True)
                for h in range(HEADS):
                    mm = pe.matmul(bank[2 + h // 4][:, (h % 4) * P:(h % 4 + 1) * P], big(SLOT["C"] + (8 + h) * P, P),
                                   big(SLOT["F"] + (8 + h) * P, P), start=True, stop=True)
                mm.then_inc(sem("vnew_ps"), 1)
                pe.wait_ge(*at("vnew0", 1, l, 1))
                for h in range(HEADS):
                    mm = pe.matmul(bank[4 + h // 4][:, (h % 4) * P:(h % 4 + 1) * P], big(SLOT["C"] + h * P, P),
                                   big(SLOT["A"] + h * P, P), start=True, stop=True)
                mm.then_inc(sem("state_ps"), 1)
                pe.wait_ge(*at("state", 1, l, 1))
                pe.wait_ge(*at("w_neg", 1, l, 1))
                for h in range(HEADS):
                    o = bank[6 + h // 4][:, (h % 4) * P:(h % 4 + 1) * P]
                    pe.matmul(o, big(SLOT["F"] + (8 + h) * P, P), big(SLOT["D"] + (8 + h) * P, P), start=True, stop=False)
                    mm = pe.matmul(o, big(WT + h * P, P), big(ST + h * P, P), start=False, stop=True)
                mm.then_inc(sem("vnew_ps1"), 1)
                pe.wait_ge(*at("vnew1", 1, l, 1))
                pe.wait_ge(*at("q_dec", 1, l, 1))
                for h in range(HEADS):
                    o = bank[h // 2]
                    c = (h % 2) * TOK
                    pe.matmul(o[:, c:c + P], big(SLOT["A"] + h * P, P), big(SLOT["B"] + h * P, P), start=True, stop=True)
                    pe.matmul(o[:, c + P:c + 2 * P], big(ST + h * P, P), qkc(0, h, 1), start=True, stop=False)
                    mm = pe.matmul(o[:, c + P:c + 2 * P], big(SLOT["A"] + (8 + h) * P, P), big(SLOT["B"] + (8 + h) * P, P),
                                   start=False, stop=True)
                mm.then_inc(sem("o_ps"), 1)
                pe.wait_ge(*at("o_sq", 1, l, 1))
                for b in range(4):
                    mm = pe.matmul(bank[4 + b][:, :], ones, big(SLOT["E"] + b * 512, 512), start=True, stop=True)
                mm.then_inc(sem("o_sum"), 1)
                stage_end(pe, "pe")

            def stick(l):
                for h in range(HEADS):
                    p0 = 64 * (h % 2)
                    j = (h // 2) * TOK
                    q = BIG[p0:p0 + 64, SBQ + j:SBQ + j + TOK]
                    pe.matmul(bank[h][:, 0:TOK], BIG[p0:p0 + 64, SBK + j:SBK + j + P], q, start=True, stop=True)
                    mm = pe.matmul(bank[h][:, TOK:TOK + P], BIG[p0:p0 + 64, SBK + j + P:SBK + j + 2 * P],
                                   BIG[p0:p0 + 64, SBQ + j + P:SBQ + j + 2 * P], start=True, stop=True)
                mm.then_inc(sem("z_ps"), 1)
                pe.wait_ge(*at("z_out", 8, l, 8))
                for n in range(NT):
                    for j in range(4):
                        mm = pe.transpose(bank[n][:, j * P:(j + 1) * P], big(SBV + j * TOK + n * P, P), ident)
                mm.then_inc(sem("vt_ps"), 1)
                pe.wait_ge(*at("vt_out", 1, l, 1))
                pe.wait_ge(*at("sp_out", 1, l, 1))
                for h in range(HEADS):
                    s0 = SP + h * 384
                    pe.matmul(bank[h][:, 0:TOK], con("key_after"), big(s0, TOK), start=True, stop=False)
                    pe.matmul(bank[h][:, P:TOK], ones, big(s0 + TOK, P), start=False, stop=True)
                    mm = pe.matmul(bank[h][:, TOK:TOK + P], con("key_after"), big(s0 + TOK, P), start=True, stop=True)
                mm.then_inc(sem("rem_ps"), 1)
                pe.wait_ge(*at("stick_p", 1, l, 1))
                for h in range(HEADS):
                    p0 = 64 * (h % 2)
                    o = bank[h // 4][p0:p0 + 64, ((h // 2) % 2) * TOK:((h // 2) % 2 + 1) * TOK]
                    pe.matmul(o, big(VT + h * 64, 64), big(ZB + h * 384, TOK), start=True, stop=False)
                    mm = pe.matmul(bank[h // 4][p0:p0 + 64, ((h // 2) % 2) * TOK + P:((h // 2) % 2 + 1) * TOK],
                                   big(VT + 512 + h * 64, 64), big(ZB + h * 384 + TOK, P), start=False, stop=True)
                mm.then_inc(sem("stick_ps"), 1)
                stage_end(pe, "pe")

            def combine(l):
                n = UN[f"up{l}"]
                for u in range(4):
                    cols_unit(n + u, lambda t: half(u, t), src=BIG, src_off=OD)
                for u in range(2):
                    cols_unit(n + 4 + u, lambda t: half(4 + 2 * u + t // 2, t % 2), kt=4, tiles=4, src=BIG, src_off=OSB)
                pe.wait_ge(*at("mixed", 1, l, 1))
                n = UN[f"w_out{l}"]
                for u in range(4):
                    cols_unit(n + u, lambda t: half(u, t), src=BIG, src_off=SLOT["D"])
                stage_end(pe, "pe")

            def up_all(n, par2, rounds=0):
                cols_unit(n, lambda t: half(2 * par2, t), rounds=rounds)
                cols_unit(n + 1, lambda t: half(2 * par2 + 1, t), rounds=rounds)

            def down_all(n, par2, first=False, rounds=0):
                arrived(n, rounds)
                for f in range(2):
                    for o in range(KT):
                        mm = pe.matmul(half(4 + o // 2, o % 2), ring[n % RING][:, (f * KT + o) * P:(f * KT + o + 1) * P],
                                       FG[:, par2 * 512 + f * TOK:par2 * 512 + (f + 1) * TOK],
                                       start=(first and f == 0 and o % 2 == 0), stop=True, skip_group_check=True)
                mm.then_inc(sem("unit_done"), 1)

            def up_slots(n, par2, rounds, e):
                for which in range(2):
                    arrived(n + which, rounds)
                    for t in range(2):
                        for k in range(KT):
                            mm = pe.matmul(bank[2 * par2 + which][:, t * P:(t + 1) * P], tile(n + which, k * 2 + t),
                                           BIG[:, bass.ds(e * 1024 + (HG + k * P), P)], start=(k == 0), stop=(k == KT - 1))
                    mm.then_inc(sem("unit_done"), 1)

            def down_slots(n, par2, first, rounds, e):
                arrived(n, rounds)
                for f in range(2):
                    for b in range(2):
                        mm = pe.matmul(bank[4 + b][:, :], FG[:, par2 * 512 + f * P:par2 * 512 + (f + 1) * P],
                                       ring[n % RING][:, f * 1024 + b * 512:f * 1024 + (b + 1) * 512],
                                       start=(first and f == 0), stop=True, skip_group_check=True)
                mm.then_inc(sem("unit_done"), 1)

            def ffn(n, blocks, base, expert=None, slots=False):
                up = (lambda m, p, r=0: up_slots(m, p, r, expert)) if slots else up_all
                down = (lambda m, p, f=False, r=0: down_slots(m, p, f, r, expert)) if slots else down_all
                e_units = 0 if expert is None else expert * (3 * blocks // RING)
                b0 = base if expert is None else expert * blocks + base
                e2 = expert

                def gated(count):
                    if isinstance(count, int) and count <= 0:
                        return
                    pe.wait_ge(sem("gated"), count)

                gated(b0)
                up(n, 0, e_units)
                up(n + 2, 1, e_units)
                gated(b0 + 1)
                if expert is not None:
                    pe.wait_ge(sem("expert_out"), e2 + 1)
                down(n + 4, 0, True, e_units)
                steps_left = blocks - 2
                with pe.Fori(0, steps_left // 2) as i:
                    r = i + e_units
                    for half_step in range(2):
                        m = n + 5 + 3 * half_step
                        gated(i * 2 + (b0 + 1 + half_step))
                        up(m, half_step, r)
                        gated(i * 2 + (b0 + 2 + half_step))
                        down(m + 2, 1 - half_step, False, r)
                done = steps_left // 2 * 2
                m = n + 5 + 3 * done
                if steps_left % 2:
                    gated(b0 + 1 + done)
                    up(m, 0, e_units)
                    gated(b0 + 2 + done)
                    down(m + 2, 1, False, e_units)
                    m += 3
                gated(b0 + blocks)
                down(m, (blocks - 1) % 2, False, e_units)
                assert m + 1 == n + 3 * blocks

            pe.wait_ge(sem("inputs"), 48)
            pe.wait_ge(sem("c_act"), 1)
            ada(0)
            ada(1)
            stage_end(pe, "pe")
            norms = 0
            for l in range(LAYERS):
                norm(norms)
                norms += 1
                project(l)
                stage_end(pe, "pe")
                delta(l)
                stick(l)
                combine(l)
                norm(norms)
                norms += 1
                if l == 0:
                    ffn(UN["ffn"], BLK1, 0)
                    stage_end(pe, "pe")
                    continue
                for n in range(NT):
                    for k in range(KT):
                        mm = pe.transpose(bank[4 + 2 * n + k // 4][:, (k % 4) * P:(k % 4 + 1) * P],
                                          H[:, k * TOK + n * P:k * TOK + (n + 1) * P], ident)
                mm.then_inc(sem("hn_ps"), 1)
                for n in range(NT):
                    for k in range(KT):
                        mm = pe.matmul(bank[0][:, n * 8:n * 8 + 8], H[:, k * TOK + n * P:k * TOK + (n + 1) * P],
                                       par("router_w", 8, k * 8), start=(k == 0), stop=(k == KT - 1))
                mm.then_inc(sem("logits"), 1)
                pe.wait_ge(sem("hn_out"), 1)
                pe.wait_ge(sem("masks"), 1)
                pe.matmul(bank[5][:, 0:8], upper, SM[:, MASK:MASK + 8], start=True, stop=True)
                pe.matmul(bank[5][:, 8:16], ones, SM[:, MASK:MASK + 8], start=True, stop=False)
                pe.matmul(bank[5][:, 8:16], upper, SM[:, MASK + 8:MASK + 16], start=False, stop=True)
                for n in range(NT):
                    pe.matmul(bank[5][:, 16:24], ones, SM[:, MASK + 8 * n:MASK + 8 * n + 8], start=(n == 0), stop=(n == NT - 1))
                pe.matmul(bank[5][:, 128:256], ones, upper, start=True, stop=True).then_inc(sem("places"), 1)
                for half_e in range(2):
                    pe.wait_ge(sem("gate_diag"), half_e + 1)
                    for b in range(2):
                        mm = pe.matmul(bank[1 + 2 * half_e + b][:, :], ones, big(GD + half_e * 1024 + b * 512, 512), start=True, stop=True)
                    mm.then_inc(sem("gate_ps"), 1)
                stage_end(pe, "pe")
                for c in range(16):
                    mm = pe.transpose(bank[c // 4][:, (c % 4) * P:(c % 4 + 1) * P], big(SELG + c * P, P), ident)
                mm.then_inc(sem("selt_ps"), 1)
                with pe.Fori(0, EXPERTS // 2) as i:
                    for j in range(2):
                        pe.wait_ge(sem("gather_low"), i * 2 + (j + 1))
                        pe.wait_ge(sem("gather_high"), i * 2 + (j + 1))
                        for k in range(KT):
                            for n in range(NT):
                                mm = pe.matmul(bank[4 + 2 * j + k // 4][:, (k % 4) * P:(k % 4 + 1) * P],
                                               big(HN + n * 1024 + k * P, P), BIG[:, bass.ds(i * 512 + (SEL + j * 256 + n * P), P)],
                                               start=(n == 0), stop=(n == NT - 1))
                        mm.then_inc(sem("gather_ps"), 1)
                stage_end(pe, "pe")
                with pe.Fori(0, EXPERTS) as e:
                    count = pe.value_load(SMU[0:1, bass.ds(e + 16, 1)], min_val=0, max_val=TOK)
                    with pe.If(count <= P):
                        ffn(UN["moe"], BLK1, BLK1, e, slots=True)
                    with pe.Else():
                        ffn(UN["moe"], BLK1, BLK1, e)
                stage_end(pe, "pe")
                for t in range(KT):
                    for e in range(EXPERTS):
                        mm = pe.matmul(half(t // 2, t % 2), big(YS + e * 1024 + t * P, P), big(SELT + e * TOK, TOK),
                                       start=(e == 0), stop=(e == EXPERTS - 1))
                    if t % 2:
                        mm.then_inc(sem("scatter"), 1)
                stage_end(pe, "pe")
            norm(norms)
            stage_end(pe, "pe")
            norms += 1
            done_blocks = BLK1 * (1 + EXPERTS)

            def ffn2(name):
                nonlocal norms, done_blocks
                norm(norms)
                norms += 1
                ffn(UN[name], BLK2, done_blocks)
                done_blocks += BLK2
                if name != "ffn2_1":
                    stage_end(pe, "pe")

            ffn2("ffn1_0")
            norm(norms)
            norms += 1
            pe.wait_ge(sem("bb"), 1)
            for i in range(2):
                for k in range(KT):
                    mm = pe.transpose(bank[4 * i + k // 4][:, (k % 4) * P:(k % 4 + 1) * P], big(BBX + i * 1024 + k * P, P), ident)
            mm.then_inc(sem("bt_ps"), 1)
            pe.wait_ge(sem("bt"), 1)
            for k in range(KT + 1):
                if k < KT:
                    if k:
                        pe.wait_ge(sem("bu_read"), k)
                    for i in range(2):
                        for j in range(4):
                            mm = pe.matmul(half(j, i), BIG[32 * j:32 * j + 32, BBT + i * 1024 + k * P:BBT + i * 1024 + (k + 1) * P],
                                           H[32 * j:32 * j + 32, k * TOK:(k + 1) * TOK], start=True, stop=True)
                    mm.then_inc(sem("bu"), 1)
                if k:
                    kk = k - 1
                    pe.wait_ge(sem("rotated"), k)
                    if kk > 1:
                        pe.wait_ge(sem("y_out"), kk - 1)
                    for j in range(4):
                        pr = 4 * kk + j
                        for q, c in enumerate((0, 1, 2, 2)):
                            mm = pe.matmul(bank[4 + kk % 2][32 * j:32 * j + 32, 0:TOK], big(CX + c * 1024 + pr * 32, 32),
                                           big(ROT[q] + j * TOK, TOK), start=(q == 0), stop=(q == 3))
                    mm.then_inc(sem("y_ps"), 1)
            pe.wait_ge(sem("y_gelu"), 1)
            stage_end(pe, "pe")
            for u in range(4):
                cols_unit(UN["glu"] + u, lambda t: half(u, t), src=BIG, src_off=YB)
            stage_end(pe, "pe")
            ffn2("ffn2_0")
            norm(norms)
            norms += 1
            for u in range(6):
                cols_unit(UN["kv"] + u, lambda t: half(u, t))
            stage_end(pe, "pe")
            pe.wait_ge(sem("kv_sq"), 1)
            for i in range(2):
                mm = pe.matmul(bank[i][:, :], half_ones, big(KSQ + i * 512, 512), start=True, stop=True)
            mm.then_inc(sem("kv_sum"), 1)
            for i, t0 in enumerate((6, 10)):
                for n in range(NT):
                    for m in range(2):
                        mm = pe.transpose(bank[2 + i][:, (n * 2 + m) * P:(n * 2 + m + 1) * P],
                                          big(KV + (t0 + m) * TOK + n * P, P), ident)
            mm.then_inc(sem("kv_vt"), 1)
            pe.matmul(bank[4][0:QH, 0:256], par("rel_bias", 16, pn=32), con("onehot", 256, 255, pn=32), start=True, stop=True)
            for n in range(NT):
                for c in range(NCMP):
                    x = 255 + n * P - 16 * c - 31
                    mm = pe.matmul(bank[5][:, (n * NCMP + c) * QH:(n * NCMP + c + 1) * QH], con("onehot", P, x, pn=32),
                                   par("rel_bias", 16, pn=32), start=True, stop=True)
            mm.then_inc(sem("bias_ps"), 1)
            pe.wait_ge(sem("w1_here"), 32)
            pe.wait_ge(sem("cmp_src"), 1)
            for i in range(2):
                for hf in range(2):
                    for s in range(32):
                        off = SRC + i * 1024 + (s // 16) * 512
                        mm = pe.matmul(PS[:, HID[hf] + i * 2 * NCMP:HID[hf] + (i + 1) * 2 * NCMP],
                                       BIG[64 * hf:64 * hf + 64, W1 + i * 4096 + s * P:W1 + i * 4096 + (s + 1) * P],
                                       view(BIG, off + s, [[TOK, 2], [16, NCMP]], 64 * hf, 64),
                                       start=(s == 0), stop=(s == 31))
            mm.then_inc(sem("hid_ps"), 1)
            pe.wait_ge(sem("hid"), 1)
            pe.matmul(bank[7][:, 0:4 * NCMP], par("w2_k", 128), SM[:, 0:4 * NCMP], start=True, stop=True)
            for g in range(4):
                x = (2 + g % 2) * 2 * NCMP + (g // 2) * NCMP
                mm = pe.matmul(bank[7][0:NCMP, 128 + g * 64:128 + (g + 1) * 64], SM[:, x:x + NCMP], par("w2_v", 64),
                               start=True, stop=True)
            mm.then_inc(sem("cmp_ps"), 1)
            pe.wait_ge(sem("kc_sq"), 1)
            pe.matmul(bank[7][:, 64:64 + 4 * NCMP], half_ones, SM[:, 128:128 + 4 * NCMP], start=True, stop=True)\
                .then_inc(sem("kc_sum"), 1)
            stage_end(pe, "pe")
            ffn2("ffn1_1")
            norm(norms)
            norms += 1
            for u in range(4):
                cols_unit(UN["q"] + u, lambda t: half(u, t))
            for n in range(NT):
                for k in range(KT):
                    mm = pe.matmul(bank[4][:, n * 48:n * 48 + 48], H[:, k * TOK + n * P:k * TOK + (n + 1) * P],
                                   par("w_gate", 48, k * 48), start=(k == 0), stop=(k == KT - 1))
            mm.then_inc(sem("gate_logits"), 1)
            stage_end(pe, "pe")
            pe.wait_ge(sem("q_sq"), 1)
            for b in range(4):
                mm = pe.matmul(bank[b][:, :], half_ones, big(PT + b * 512, 512), start=True, stop=True)
            mm.then_inc(sem("q_sum"), 1)
            stage_end(pe, "pe")

            def qhead(h, n):
                p0 = 64 * (h % 2)
                return BIG[p0:p0 + 64, QB + (h // 2) * TOK + n * P:QB + (h // 2) * TOK + (n + 1) * P]

            for n in range(NT):
                for h in range(QH):
                    g = h // 4
                    p0 = 64 * (h % 2)
                    mm = pe.matmul(bank[h % 2][:, (n * QH + h) * NCMP:(n * QH + h + 1) * NCMP], qhead(h, n),
                                   BIG[p0:p0 + 64, KC + g * NCMP:KC + (g + 1) * NCMP], start=True, stop=True)
            mm.then_inc(sem("cmp_logits"), 1)
            pe.wait_ge(sem("cmp_p"), 1)
            stage_end(pe, "pe")
            for h in range(QH):
                for n in range(NT):
                    mm = pe.transpose(bank[h // 2][0:NCMP, (h % 2) * TOK + n * P:(h % 2) * TOK + (n + 1) * P],
                                      big(CP + (n * QH + h) * NCMP, NCMP), ident)
            mm.then_inc(sem("cmp_pt"), 1)
            stage_end(pe, "pe")
            for br in range(2):
                for h in range(QH):
                    g = h // 4
                    p0 = 64 * (h % 2)
                    b = bank[h % 8]
                    if h >= 8:
                        pe.wait_ge(sem("logits_out"), br * 16 + h - 7)
                    kk = KD + br * 1024 + g * TOK
                    pe.matmul(b[:, 0:P], qhead(h, 0), BIG[p0:p0 + 64, kk:kk + P], start=True, stop=True)
                    pe.matmul(b[:, P:3 * P], qhead(h, 1), BIG[p0:p0 + 64, kk:kk + TOK], start=True, stop=True)\
                        .then_inc(sem("logits_ps"), 1)
                pe.wait_ge(sem("probs"), br + 1)
                for h in range(QH):
                    b = bank[h % 8]
                    if h >= 8:
                        pe.wait_ge(sem("pt_out"), br * 16 + h - 7)
                    for i in range(3):
                        mm = pe.transpose(b[:, i * P:(i + 1) * P], big(LG + h * 384 + i * P, P), ident)
                    mm.then_inc(sem("pt_ps"), 1)
                pe.wait_ge(sem("pt_out"), br * 16 + 16)
                for h in range(QH):
                    g = h // 4
                    p0 = 64 * (h % 2)
                    o = bank[h // 4][p0:p0 + 64, (h // 2 % 2) * TOK:(h // 2 % 2 + 1) * TOK]
                    o1 = bank[h // 4][p0:p0 + 64, (h // 2 % 2) * TOK + P:(h // 2 % 2 + 1) * TOK]
                    pe.matmul(o, big(VN + br * 512 + g * 64, 64), big(PT + h * 384, TOK), start=True, stop=False)
                    if br == 0:
                        pe.matmul(o, BIG[0:NCMP, VC + g * 64:VC + (g + 1) * 64], BIG[0:NCMP, CPT + h * TOK:CPT + (h + 1) * TOK],
                                  start=False, stop=False)
                    mm = pe.matmul(o1, big(VN + br * 512 + 256 + g * 64, 64), big(PT + h * 384 + TOK, P), start=False, stop=True)
                mm.then_inc(sem("o_branch"), 1)
                stage_end(pe, "pe")
            for u in range(4):
                cols_unit(UN["w_o"] + u, lambda t: half(u, t), src=BIG, src_off=OB)
            stage_end(pe, "pe")
            ffn2("ffn2_1")

        @stage.vector
        def _(ve):
            def lk(ins):
                link(ve, "vector_step", ins)

            def tt(out, a, b, op):
                return ve.tensor_tensor(out, a, b, op)

            def norm_v(i, scale_off, shift, dst=None):
                dst = H if dst is None else dst
                tt(big(SQ0, 2048), X[:, :], X[:, :], ALU.mult).then_inc(sem("norm_sq"), 1)
                ve.wait_ge(*at("norm_rs", 1, i))
                for t in range(KT):
                    w = NSC[:, t:t + 1] if scale_off is None else par(scale_off[0], 1, scale_off[1] + t)
                    ve.scalar_tensor_tensor(dst[:, t * TOK:(t + 1) * TOK], X[:, t * TOK:(t + 1) * TOK], w, RS[:, :],
                                            ALU.mult, ALU.mult).then_inc(sem("norm_scaled" if shift else "normed"), 1)

            def ffn_loop(blocks, base, units0, expert=None, width=2 * TOK):
                b0 = base if expert is None else expert * blocks + base
                u0 = units0 if expert is None else expert * (3 * blocks) + units0

                def gate(par2, count, units):
                    ve.wait_ge(sem("silu"), count + 1)
                    ve.wait_ge(sem("unit_done"), units)
                    tt(FG[:, par2 * 512:par2 * 512 + width], FS[:, par2 * 512:par2 * 512 + width],
                       bank[2 * par2 + 1][:, 0:width], ALU.mult).then_inc(sem("gated"), 1)

                gate(0, b0, u0 + 2)
                gate(1, b0 + 1, u0 + 4)
                steps_left = blocks - 2
                with ve.Fori(0, steps_left // 2) as i:
                    for hs in range(2):
                        gate(hs, i * 2 + (b0 + 2 + hs), i * 6 + (u0 + 7 + 3 * hs))
                done = steps_left // 2 * 2
                if steps_left % 2:
                    gate(0, b0 + 2 + done, u0 + 7 + 3 * done)

            ve.wait_ge(sem("inputs"), 48)
            for l in range(LAYERS):
                with ve.Fori(0, 4) as i:
                    ve.wait_ge(sem("unit_done"), i * RING + (UN[f"ada{l}"] + RING))
                    ve.tensor_tensor(MOD[:, bass.ds(i * 12 + l * 48, 12)], bank[0][:, 0:12],
                                     PAR[:, bass.ds(i * 12 + (PC["ada_b"] + l * 48), 12)], ALU.add).then_inc(sem("ada_free"), 1)
            stage_end(ve, "ve")
            norms = 0

            def mod(l, part, t=0, w=8):
                return MOD[:, l * 48 + part * 8 + t:l * 48 + part * 8 + t + w]

            for l in range(LAYERS):
                ve.wait_ge(sem("ada_free"), 9)
                lk(ve.scalar_tensor_tensor(NSC[:, :], mod(l, 1), 1.0, par("norm_mix", 8, l * 8), ALU.add, ALU.mult))
                norm_v(norms, None, True)
                norms += 1
                with ve.Fori(0, 3) as i:
                    ve.wait_ge(sem("evac"), i * 4 + (l * 30 + 6 + 4))
                    for j in range(4):
                        for t in range(KT):
                            x0 = i * 2048 + (PROJ + t * TOK)
                            y0 = i * 2048 + (CONV + t * TOK)
                            wj = PAR[:, bass.ds(i * 32 + (PC["conv_w"] + l * 96 + t * 4 + 3 - j), 1)]
                            if j == 0:
                                ins = ve.tensor_scalar(BIG[:, bass.ds(y0, TOK)], BIG[:, bass.ds(x0, TOK)], wj, None, ALU.mult)
                            else:
                                ins = ve.scalar_tensor_tensor(BIG[:, bass.ds(y0 + j, TOK - j)], BIG[:, bass.ds(x0, TOK - j)], wj,
                                                              BIG[:, bass.ds(y0 + j, TOK - j)], ALU.mult, ALU.add)
                            if t == KT - 1:
                                ins.then_inc(sem("conv_tap"), 1)
                        if j < 3:
                            ve.wait_ge(sem("conv_tap"), i * 4 + (l * 12 + j + 1))
                stage_end(ve, "ve")
                tt(big(SLOT["D"], 4096), big(CONV, 4096), big(CONV, 4096), ALU.mult).then_inc(sem("qk_sq"), 1)
                ve.wait_ge(*at("beta_exp", 1, l, 1))
                lk(ve.tensor_scalar(SM[:, 0:16], SM[:, 0:16], 1.0, None, ALU.add))
                lk(ve.reciprocal(SM[:, 0:16], SM[:, 0:16]))
                lk(tt(view(SM, 16, [[8, 2], [1, 8]]), view(bank[6], 8, [[16, 2], [1, 8]]),
                      view(PAR, PC["dt_bias"] + l * 16, [[8, 2], [1, 8]]), ALU.add))
                ve.scalar_tensor_tensor(SM[:, 32:48], SM[:, 16:32], -1.0, SM[:, 16:32], ALU.mult, ALU.max).then_inc(sem("a_abs"), 1)
                ve.wait_ge(*at("a_ln", 1, l, 1))
                lk(ve.scalar_tensor_tensor(SM[:, 32:48], SM[:, 16:32], 0.0, SM[:, 32:48], ALU.max, ALU.add))
                lk(ve.scalar_tensor_tensor(SM[:, 64:80], SM[:, 32:48], -1.0, SM[:, 48:64], ALU.mult, ALU.mult))
                tt(view(BIG, SLOT["A"], [[P, 16], [1, P]]), view(CON, CC["upper"], [[0, 16], [1, P]]),
                   view(SM, 64, [[1, 16], [0, P]]), ALU.mult).then_inc(sem("gu"), 1)
                ve.wait_ge(*at("qk_rs", 1, l, 1))
                tt(big(CONV, 4096), big(CONV, 4096), big(SLOT["D"], 4096), ALU.mult).then_inc(sem("qk_normed"), 1)
                ve.wait_ge(*at("cum", 1, l, 1))
                lk(ve.tensor_copy(SM[:, 80:112], bank[4][:, 0:32]))
                for c in range(16):
                    gr = bank[c // 4][:, (c % 4) * P:(c % 4 + 1) * P]
                    gc = SM[:, 80 + c:81 + c]
                    ve.tensor_scalar(big(SLOT["B"] + c * P, P), gr, gc, 0.0, ALU.subtract, ALU.min)
                    ins = ve.tensor_scalar(big(SLOT["C"] + c * P, P), gr, gc, 0.0, ALU.subtract, ALU.max)
                ins.then_inc(sem("decay_arg"), 1)
                tt(SM[:, 112:128], SM[:, 96:112], SM[:, 80:96], ALU.subtract).then_inc(sem("kd_arg"), 1)
                ve.wait_ge(*at("decay_exp", 1, l, 1))
                tt(SM[:, 144:160], SM[:, 144:160], SM[:, 0:16], ALU.mult)
                tt(view(BIG, SLOT["B"], [[P, 16], [1, P]]), view(BIG, SLOT["B"], [[P, 16], [1, P]]),
                   view(CON, CC["upper"], [[0, 16], [1, P]]), ALU.mult)
                tt(view(BIG, SLOT["C"], [[P, 16], [1, P]]), view(BIG, SLOT["C"], [[P, 16], [1, P]]),
                   view(CON, CC["lower_strict"], [[0, 16], [1, P]]), ALU.mult)
                stage_end(ve, "ve")
                ve.wait_ge(*at("kk", 1, l, 2))
                for c in range(16):
                    ins = ve.scalar_tensor_tensor(big(SLOT["D"] + c * P, P), bank[c // 4][:, (c % 4) * P:(c % 4 + 1) * P],
                                                  SM[:, c:c + 1], big(SLOT["C"] + c * P, P), ALU.mult, ALU.mult)
                lk(ins)
                ve.nop().then_inc(sem("lmat"), 1)
                ve.wait_ge(*at("kk", 2, l, 2))
                for b in range(4):
                    tt(big(SLOT["B"] + b * 512, 512), bank[4 + b][:, :], big(SLOT["B"] + b * 512, 512), ALU.mult)
                lk(tt(view(BIG, SLOT["E"], [[P, 16], [1, P]]), view(BIG, SLOT["D"], [[P, 16], [1, P]]),
                      view(CON, CC["level0_lower"], [[0, 16], [1, P]]), ALU.mult))
                tt(view(BIG, SLOT["E"], [[P, 16], [1, P]]), view(CON, CC["ident"], [[0, 16], [1, P]]),
                   view(BIG, SLOT["E"], [[P, 16], [1, P]]), ALU.subtract)
                ve.wait_ge(*at("lt_out", 1, l, 1))
                lk(tt(view(BIG, SLOT["F"], [[P, 16], [1, P]]), view(BIG, SLOT["C"], [[P, 16], [1, P]]),
                      view(CON, CC["level"], [[0, 16], [1, P]]), ALU.mult))
                tt(view(BIG, SLOT["F"], [[P, 16], [1, P]]), view(CON, CC["ident"], [[0, 16], [1, P]]),
                   view(BIG, SLOT["F"], [[P, 16], [1, P]]), ALU.subtract)
                stage_end(ve, "ve")
                for s in range(6):
                    for q in range(4):
                        ve.wait_ge(*at("level_p", 4 * s + q + 1, l, 24))
                        x = q * 512
                        tt(big(SLOT["E"] + x, 512), big(SLOT["E"] + x, 512), bank[4 + q % 2][:, :], ALU.subtract)
                        lk(tt(big(SLOT["F"] + x, 512), big(SLOT["F"] + x, 512), bank[6 + q % 2][:, :], ALU.subtract))
                        ve.nop().then_inc(sem("level_t"), 1)
                stage_end(ve, "ve")
                ve.wait_ge(*at("kvt", 1, l, 1))
                for b in range(4):
                    s = view(SM, (128 if b < 2 else 144) + b * 4, [[1, 4], [0, P]])
                    tt(view(BIG, SLOT["C"] + b * 512, [[P, 4], [1, P]]), view(bank[b], 0, [[P, 4], [1, P]]), s, ALU.mult)
                for b in range(4):
                    tt(view(BIG, SLOT["D"] + b * 512, [[P, 4], [1, P]]), view(bank[4 + b], 0, [[P, 4], [1, P]]),
                       view(SM, b * 4, [[1, 4], [0, P]]), ALU.mult)
                qv = view(BIG, CONV + P, [[TOK, 8], [1, P]])
                tt(qv, qv, view(BIG, EG, [[P, 8], [1, P]]), ALU.mult).then_inc(sem("q_dec"), 1)
                stage_end(ve, "ve")
                ve.wait_ge(*at("vnew_ps", 1, l, 1))
                lk(ve.tensor_copy(big(SLOT["A"], 512), bank[0][:, :]))
                lk(ve.tensor_copy(big(SLOT["A"] + 512, 512), bank[1][:, :]))
                ve.nop().then_inc(sem("vnew0"), 1)
                ve.wait_ge(*at("state_ps", 1, l, 1))
                lk(ve.tensor_copy(big(ST, 512), bank[4][:, :]))
                lk(ve.tensor_copy(big(ST + 512, 512), bank[5][:, :]))
                ve.nop().then_inc(sem("state"), 1)
                ve.wait_ge(*at("vnew_ps1", 1, l, 1))
                lk(ve.tensor_copy(big(SLOT["A"] + 1024, 512), bank[6][:, :]))
                lk(ve.tensor_copy(big(SLOT["A"] + 1536, 512), bank[7][:, :]))
                ve.nop().then_inc(sem("vnew1"), 1)
                ve.wait_ge(*at("o_rs", 1, l, 1))
                for b in range(4):
                    x = b * 512
                    ins = tt(big(SLOT["E"] + x, 512), bank[b][:, :], big(SLOT["E"] + x, 512), ALU.mult)
                lk(ins)
                ve.scalar_tensor_tensor(big(OD, 2048), big(SLOT["E"], 2048), par("dn_out_norm", 1, l), big(Z_, 2048),
                                        ALU.mult, ALU.mult)
                stage_end(ve, "ve")
                ve.wait_ge(*at("z_ps", 1, l, 1))
                for h in range(HEADS):
                    ve.scalar_tensor_tensor(big(ZB + h * 384, 384), bank[h][:, 0:384], 0.125, con("stick_mask", 384),
                                            ALU.mult, ALU.add).then_inc(sem("z_out"), 1)
                ve.wait_ge(*at("vt_ps", 1, l, 1))
                ve.tensor_copy(big(VT, 512), bank[0][:, :])
                lk(ve.tensor_copy(big(VT + 512, 512), bank[1][:, :]))
                ve.nop().then_inc(sem("vt_out"), 1)
                ve.wait_ge(*at("sp_ln", 1, l, 1))
                ve.scalar_tensor_tensor(big(SP, 3072), big(ZB, 3072), 0.0, big(SP, 3072), ALU.max, ALU.add)\
                    .then_inc(sem("sp_out"), 1)
                ve.wait_ge(*at("rem_ps", 1, l, 1))
                for h in range(HEADS):
                    ins = tt(big(ZB + h * 384, 384), big(ZB + h * 384, 384), bank[h][:, 0:384], ALU.subtract)
                ins.then_inc(sem("stick_arg"), 1)
                ve.wait_ge(*at("stick_ps", 1, l, 1))
                ve.tensor_copy(big(OSB, 512), bank[0][:, :])
                ve.tensor_copy(big(OSB + 512, 512), bank[1][:, :])
                stage_end(ve, "ve")
                n = UN[f"up{l}"]
                for b in range(4):
                    ve.wait_ge(sem("unit_done"), n + b + 1)
                    tt(big(SLOT["D"] + b * 512, 512), bank[b][:, :], big(GATES + b * 512, 512), ALU.mult)
                ve.wait_ge(sem("unit_done"), n + 6)
                for b in range(4):
                    ins = tt(big(SLOT["E"] + b * 512, 512), bank[4 + b][:, :], big(GATES + 2048 + b * 512, 512), ALU.mult)
                lk(ins)
                tt(big(SLOT["D"], 2048), big(SLOT["D"], 2048), big(SLOT["E"], 2048), ALU.add).then_inc(sem("mixed"), 1)
                n = UN[f"w_out{l}"]
                for t in range(KT):
                    ve.wait_ge(sem("unit_done"), n + t // 2 + 1)
                    ve.scalar_tensor_tensor(X[:, t * TOK:(t + 1) * TOK], bank[t // 2][:, (t % 2) * TOK:(t % 2 + 1) * TOK],
                                            mod(l, 2, t, 1), X[:, t * TOK:(t + 1) * TOK], ALU.mult, ALU.add)
                stage_end(ve, "ve")
                lk(ve.scalar_tensor_tensor(NSC[:, :], mod(l, 4), 1.0, par("norm_ffn", 8, l * 8), ALU.add, ALU.mult))
                norm_v(norms, None, True)
                norms += 1
                if l == 0:
                    ffn_loop(BLK1, 0, UN["ffn"])
                    ve.wait_ge(sem("unit_done"), UN["ffn"] + 3 * BLK1)
                    for t in range(KT):
                        ve.scalar_tensor_tensor(X[:, t * TOK:(t + 1) * TOK], bank[4 + t // 2][:, (t % 2) * TOK:(t % 2 + 1) * TOK],
                                                mod(l, 5, t, 1), X[:, t * TOK:(t + 1) * TOK], ALU.mult, ALU.add)
                    stage_end(ve, "ve")
                    continue
                ve.wait_ge(sem("logits"), 1)
                lk(tt(SM[:, 0:16], bank[0][:, 0:16], par("router_b", 16), ALU.add))
                for n in range(NT):
                    lk(ve.max(SM[:, 16 + 8 * n:24 + 8 * n], SM[:, 8 * n:8 * n + 8]))
                    lk(ve.max_index(SMU[:, 8 * n:8 * n + 8], SM[:, 16 + 8 * n:24 + 8 * n], SM[:, 8 * n:8 * n + 8]))
                lk(ve.tensor_copy(SM[:, 32:48], SMU[:, 0:16]))
                tt(view(SM, 48, [[1, 2]]), view(SM, 17, [[8, 2]]), view(SM, 16, [[8, 2]]), ALU.subtract).then_inc(sem("route_arg"), 1)
                ve.wait_ge(sem("route_exp"), 1)
                lk(ve.tensor_scalar(SM[:, 50:52], SM[:, 48:50], 1.0, None, ALU.add))
                lk(ve.reciprocal(SM[:, 50:52], SM[:, 50:52]))
                lk(tt(SM[:, 52:54], SM[:, 48:50], SM[:, 50:52], ALU.mult))
                for n in range(NT):
                    lk(ve.tensor_scalar(SM[:, 56 + 8 * n:64 + 8 * n], con("iota", 8), SM[:, 32 + 8 * n:33 + 8 * n],
                                        SM[:, 50 + n:51 + n], ALU.is_equal, ALU.mult))
                    lk(ve.tensor_scalar(SM[:, 72 + 8 * n:80 + 8 * n], con("iota", 8), SM[:, 33 + 8 * n:34 + 8 * n],
                                        SM[:, 52 + n:53 + n], ALU.is_equal, ALU.mult))
                lk(tt(SM[:, GATE:GATE + 16], SM[:, 56:72], SM[:, 72:88], ALU.add))
                for n in range(NT):
                    ve.tensor_scalar(SM[:, PLACE + 8 * n:PLACE + 8 * n + 8], con("iota", 8), SM[:, 32 + 8 * n:33 + 8 * n],
                                     None, ALU.is_equal)
                    lk(ve.tensor_scalar(SM[:, MASK + 8 * n:MASK + 8 * n + 8], con("iota", 8), SM[:, 33 + 8 * n:34 + 8 * n],
                                        None, ALU.is_equal))
                tt(SM[:, MASK:MASK + 16], SM[:, MASK:MASK + 16], SM[:, PLACE:PLACE + 16], ALU.add).then_inc(sem("masks"), 1)
                for half_e in range(2):
                    tt(view(BIG, GD + half_e * 1024, [[TOK, 4], [1, P]]), view(CON, CC["ident"], [[0, 4], [1, P]]),
                       view(SM, GATE + half_e * 4, [[1, 4], [0, P]]), ALU.mult)
                    lk(tt(view(BIG, GD + half_e * 1024 + P, [[TOK, 4], [1, P]]), view(CON, CC["ident"], [[0, 4], [1, P]]),
                          view(SM, GATE + 8 + half_e * 4, [[1, 4], [0, P]]), ALU.mult))
                    ve.nop().then_inc(sem("gate_diag"), 1)
                for half_e in range(2):
                    ve.wait_ge(sem("gate_ps"), half_e + 1)
                    ve.tensor_copy(big(GR + half_e * 1024, 512), bank[1 + 2 * half_e][:, :])
                    ve.tensor_copy(big(GR + half_e * 1024 + 512, 512), bank[2 + 2 * half_e][:, :])
                ve.memset(big(YE, 2048), 0.0)
                ve.wait_ge(sem("places"), 1)
                ve.tensor_copy(SM[:, PLACE:PLACE + 16], bank[5][:, 0:16])
                ve.tensor_copy(SMU[:, 16:24], bank[5][:, 16:24])
                lk(ve.tensor_copy(big(SLOTS, P), bank[5][:, 128:256]))
                for e in range(EXPERTS):
                    for n in range(NT):
                        c = 8 * n + e
                        place = SM[:, PLACE + c:PLACE + c + 1]
                        ve.tensor_scalar(big(SEL + (2 * e + n) * P, P), big(SLOTS, P), place, SM[:, MASK + c:MASK + c + 1],
                                         ALU.is_equal, ALU.mult)
                        ve.tensor_scalar(big(SELG + (2 * e + n) * P, P), big(SLOTS, P), place, SM[:, GATE + c:GATE + c + 1],
                                         ALU.is_equal, ALU.mult)
                stage_end(ve, "ve")
                ve.nop().then_inc(sem("gather_low"), 2)
                with ve.Fori(0, EXPERTS // 2) as i:
                    for j in range(2):
                        ve.wait_ge(sem("gather_ps"), i * 2 + (j + 1))
                        ve.tensor_copy(BIG[:, bass.ds(i * 2048 + (HG + j * 1024), 512)], bank[4 + 2 * j][:, :])\
                            .then_inc(sem("gather_low"), 1)
                ve.nop().then_inc(sem("expert_out"), 1)
                stage_end(ve, "ve")

                def dense_expert(e):
                    ffn_loop(BLK1, BLK1, UN["moe"], e)
                    ve.wait_ge(sem("unit_done"), e * (3 * BLK1) + (UN["moe"] + 3 * BLK1))
                    for b in range(4):
                        g = BIG[:, bass.ds(e * TOK + GR, TOK)]
                        for t in range(2):
                            ins = tt(big(YT + b * 512 + t * TOK, TOK), bank[4 + b][:, t * TOK:(t + 1) * TOK], g, ALU.mult)
                    ins.then_inc(sem("expert_out"), 1)
                    ve.wait_ge(sem("expert_out"), e + 2)
                    tt(big(YE, 2048), big(YE, 2048), big(YT, 2048), ALU.add).then_inc(sem("expert_sum"), 1)

                with ve.Fori(0, EXPERTS) as e:
                    count = ve.value_load(SMU[0:1, bass.ds(e + 16, 1)], min_val=0, max_val=TOK)
                    with ve.If(count <= P):
                        ffn_loop(BLK1, BLK1, UN["moe"], e, width=2 * P)
                        ve.nop().then_inc(sem("expert_sum"), 1)
                    with ve.Else():
                        dense_expert(e)
                    ve.wait_ge(sem("expert_sum"), e + 1)
                stage_end(ve, "ve")
                for b in range(4):
                    ve.wait_ge(sem("scatter"), b + 1)
                    ins = tt(big(YE + b * 512, 512), big(YE + b * 512, 512), bank[b][:, :], ALU.add)
                lk(ins)
                for t in range(KT):
                    ve.scalar_tensor_tensor(X[:, t * TOK:(t + 1) * TOK], big(YE + t * TOK, TOK), mod(l, 5, t, 1),
                                            X[:, t * TOK:(t + 1) * TOK], ALU.mult, ALU.add)
                stage_end(ve, "ve")
            norm_v(norms, ("final_norm", 0), False, X)
            stage_end(ve, "ve")
            norms += 1
            done_blocks = BLK1 * (1 + EXPERTS)

            def ffn2(name, l, last=False):
                nonlocal norms, done_blocks
                which = name[:4] + "_norm"
                norm_v(norms, (which, l * 8), False)
                norms += 1
                ffn_loop(BLK2, done_blocks, UN[name])
                done_blocks += BLK2
                ve.wait_ge(sem("unit_done"), UN[name] + 3 * BLK2)
                for b in range(4):
                    ins = ve.scalar_tensor_tensor(X[:, b * 512:(b + 1) * 512], bank[4 + b][:, :], 0.5, X[:, b * 512:(b + 1) * 512],
                                                  ALU.mult, ALU.add)
                if last:
                    lk(ins)
                    ve.nop().then_inc(sem("result"), 1)
                else:
                    stage_end(ve, "ve")

            a_re, a_im = par("a_re", 32), par("a_im", 32)
            dt, mag, th = SM[:, 0:32], SM[:, 32:64], SM[:, 64:96]
            ve.wait_ge(sem("s5_dt"), 1)
            tt(mag, a_re, dt, ALU.mult).then_inc(sem("s5_mag_arg"), 1)
            lk(tt(th, a_im, dt, ALU.mult))
            PH, RN = 256, 512
            for k in range(8):
                ins = ve.tensor_scalar(SM[:, PH + 32 * k:PH + 32 * (k + 1)], th, float(2 ** k), None, ALU.mult)
            lk(ins)
            magic = 1.5 * 2.0 ** 23
            lk(ve.tensor_scalar(SM[:, RN:RN + 256], SM[:, PH:PH + 256], float(1 / TWO_PI), magic, ALU.mult, ALU.add))
            lk(ve.tensor_scalar(SM[:, RN:RN + 256], SM[:, RN:RN + 256], magic, None, ALU.subtract))
            p1 = 6.28125
            p2 = float(np.float32(np.round((TWO_PI - p1) * 2 ** 22) / 2 ** 22))
            p3 = float(np.float32(TWO_PI - p1 - p2))
            for part in (p1, p2, p3):
                lk(ve.scalar_tensor_tensor(SM[:, PH:PH + 256], SM[:, RN:RN + 256], -part, SM[:, PH:PH + 256], ALU.mult, ALU.add))
            PI = 3.1415925
            lk(ve.tensor_scalar(SM[:, PH:PH + 256], SM[:, PH:PH + 256], PI, -PI, ALU.min, ALU.max))
            lk(ve.scalar_tensor_tensor(SM[:, RN:RN + 256], SM[:, PH:PH + 256], -1.0, SM[:, PH:PH + 256], ALU.mult, ALU.max))
            ve.tensor_scalar(SM[:, RN:RN + 256], SM[:, RN:RN + 256], -1.0, float(np.pi / 2), ALU.mult, ALU.add)\
                .then_inc(sem("angles"), 1)
            ve.wait_ge(sem("s5_trig"), 1)
            cr, ci, den, zr, zi, t1 = (SM[:, 768 + 32 * k:800 + 32 * k] for k in range(6))
            lk(tt(cr, mag, SM[:, RN:RN + 32], ALU.mult))
            lk(ve.tensor_scalar(cr, cr, -1.0, None, ALU.add))
            lk(tt(ci, mag, SM[:, PH:PH + 32], ALU.mult))
            lk(tt(den, a_re, a_re, ALU.mult))
            lk(tt(t1, a_im, a_im, ALU.mult))
            lk(tt(den, den, t1, ALU.add))
            lk(ve.reciprocal(den, den))
            lk(tt(zr, cr, a_re, ALU.mult))
            lk(tt(t1, ci, a_im, ALU.mult))
            lk(tt(zr, zr, t1, ALU.add))
            lk(tt(zr, zr, den, ALU.mult))
            lk(tt(zi, ci, a_re, ALU.mult))
            lk(tt(t1, cr, a_im, ALU.mult))
            lk(tt(zi, zi, t1, ALU.subtract))
            lk(tt(zi, zi, den, ALU.mult))
            ve.wait_ge(sem("s5_here"), 64)
            lk(ve.memset(big(BBX, 2048), 0.0))
            lk(ve.memset(big(CX, 3072), 0.0))
            for g in range(2):
                p0 = 64 * g

                def src(i):
                    return view(BIG, S5P + i * 512, [[16, 32], [1, 16]], p0, 64)

                def bc(off):
                    return view(SM, off, [[1, 32], [0, 16]], p0, 64)

                def dst(off):
                    return view(BIG, off + 16 * g, [[32, 32], [1, 16]], p0, 64)

                tmp = view(BIG, BBT, [[16, 32], [1, 16]], p0, 64)
                zro, zio = 768 + 96, 768 + 128
                tt(dst(BBX), src(0), bc(zro), ALU.mult)
                lk(tt(tmp, src(1), bc(zio), ALU.mult))
                lk(tt(dst(BBX), dst(BBX), tmp, ALU.subtract))
                tt(dst(BBX + 1024), src(1), bc(zro), ALU.mult)
                lk(tt(tmp, src(0), bc(zio), ALU.mult))
                lk(tt(dst(BBX + 1024), dst(BBX + 1024), tmp, ALU.add))
                lk(ve.tensor_copy(dst(CX), src(2)))
                lk(ve.tensor_scalar(dst(CX + 1024), src(2), -1.0, None, ALU.mult))
                lk(ve.tensor_scalar(dst(CX + 2048), src(3), -1.0, None, ALU.mult))
            ve.nop().then_inc(sem("bb"), 1)
            ffn2("ffn1_0", 0)
            norm_v(norms, ("mix_norm", 0), False)
            norms += 1
            ve.wait_ge(sem("bt_ps"), 1)
            for b in range(4):
                ins = ve.tensor_copy(big(BBT + b * 512, 512), bank[(0, 1, 4, 5)[b]][:, :])
            lk(ins)
            ve.nop().then_inc(sem("bt"), 1)
            ve.wait_ge(sem("tables"), 1)
            for k in range(KT):
                ve.wait_ge(sem("bu"), k + 1)

                vr, vi, t1, t2 = VR, VI, YR, YI
                if k:
                    ve.wait_ge(sem("rotated"), k)
                    ve.wait_ge(sem("y_ps"), k)
                pairs = [[TOK, 4], [1, TOK]]
                c, s = view(BIG, TC + k * 1024, pairs), view(BIG, TS + k * 1024, pairs)
                re, im = view(PS, 0, [[512, 4], [1, TOK]]), view(PS, TOK, [[512, 4], [1, TOK]])
                tt(view(BIG, vr, pairs), re, c, ALU.mult)
                tt(view(BIG, t1, pairs), im, s, ALU.mult)
                tt(view(BIG, vi, pairs), im, c, ALU.mult)
                tt(view(BIG, t2, pairs), re, s, ALU.mult).then_inc(sem("bu_read"), 1)
                ve.wait_ge(sem("bu_read"), k + 1)
                lk(tt(big(vr, 1024), big(vr, 1024), big(t1, 1024), ALU.add))
                lk(tt(big(vi, 1024), big(vi, 1024), big(t2, 1024), ALU.subtract))
                for j in range(4):
                    m = view(SM, 32 + 4 * k + j, [[0, TOK]])
                    ve.tensor_tensor_scan(big(YR + j * TOK, TOK), m, big(vr + j * TOK, TOK), 0.0, ALU.mult, ALU.add)
                    ins = ve.tensor_tensor_scan(big(YI + j * TOK, TOK), m, big(vi + j * TOK, TOK), 0.0, ALU.mult, ALU.add)
                ins.then_inc(sem("scanned"), 1)
                if k:
                    kk = k - 1
                    ve.wait_ge(sem("y_ps"), k)
                    ve.scalar_tensor_tensor(big(YB + kk * TOK, TOK), H[:, kk * TOK:(kk + 1) * TOK], par("s5_d", 1, kk),
                                            bank[4 + kk % 2][:, 0:TOK], ALU.mult, ALU.add).then_inc(sem("y_out"), 1)
            ve.wait_ge(sem("y_ps"), KT)
            kk = KT - 1
            ve.scalar_tensor_tensor(big(YB + kk * TOK, TOK), H[:, kk * TOK:(kk + 1) * TOK], par("s5_d", 1, kk),
                                    bank[4 + kk % 2][:, 0:TOK], ALU.mult, ALU.add).then_inc(sem("y_out"), 1)
            stage_end(ve, "ve")
            ve.wait_ge(sem("glu_sig"), 4)
            lk(tt(big(SLOT["D"], 2048), big(SLOT["D"], 2048), big(YB, 2048), ALU.mult))
            tt(X[:, :], X[:, :], big(SLOT["D"], 2048), ALU.add)
            stage_end(ve, "ve")
            ffn2("ffn2_0", 0)
            norm_v(norms, ("kv_norm", 0), False)
            norms += 1
            for u in range(6):
                ve.wait_ge(sem("unit_done"), UN["kv"] + u + 1)
                ve.tensor_copy(big(KV + u * 512, 512), bank[u][:, :])
            stage_end(ve, "ve")
            tt(big(KSQ, 512), big(KV + 4 * TOK, 512), big(KV + 4 * TOK, 512), ALU.mult)
            lk(tt(big(KSQ + 512, 512), big(KV + 8 * TOK, 512), big(KV + 8 * TOK, 512), ALU.mult))
            ve.nop().then_inc(sem("kv_sq"), 1)
            for i, pos in enumerate(("pos_k", "pos_v")):
                for hf in range(2):
                    ins = tt(view(BIG, SRC + i * 1024 + hf * 512, [[16, 32], [1, 16]]),
                             view(BIG, KV + i * 512, [[16, 32], [1, 16]]),
                             view(PAR, PC[pos] + 16 * hf, [[0, 32], [1, 16]]), ALU.add)
            lk(ins)
            ve.nop().then_inc(sem("cmp_src"), 1)
            ve.wait_ge(sem("kv_sum"), 1)

            def refine(y, m, t):
                lk(tt(t, y, y, ALU.mult))
                lk(tt(t, t, m, ALU.mult))
                lk(ve.tensor_scalar(t, t, -0.5, 1.5, ALU.mult, ALU.add))
                lk(tt(y, y, t, ALU.mult))

            lk(ve.tensor_scalar(big(KSQ, 512), bank[0][:, :], 1 / 64, EPS, ALU.mult, ALU.add))
            lk(ve.tensor_scalar(big(KSQ + 512, 512), bank[1][:, :], 1 / 64, EPS, ALU.mult, ALU.add))
            ve.nop().then_inc(sem("kv_ms"), 1)
            ve.wait_ge(sem("kv_rs"), 1)
            refine(big(KRS, 1024), big(KSQ, 1024), big(KT2, 1024))
            for i, (t0, w) in enumerate(((4, "k_norm_slc"), (8, "k_norm_win"))):
                k = big(KV + t0 * TOK, 512)
                lk(ve.scalar_tensor_tensor(k, k, par(w, 1), big(KRS + i * 512, 512), ALU.mult, ALU.mult))
            ve.nop().then_inc(sem("k_normed"), 1)
            ve.wait_ge(sem("kv_vt"), 1)
            ve.tensor_copy(big(VN, 512), bank[2][:, :])
            ve.tensor_copy(big(VN + 512, 512), bank[3][:, :])
            ve.wait_ge(sem("bias_ps"), 1)
            lk(ve.memset(BIG[0:QH, BTAB:BTAB + 384], NEG))
            lk(ve.tensor_copy(BIG[0:QH, BTAB + 127:BTAB + 383], bank[4][0:QH, 0:256]))
            ve.nop().then_inc(sem("bias_tab"), 1)
            for n in range(NT):
                tt(view(BIG, CB + n * QH * NCMP, [[NCMP, QH], [1, NCMP]]), view(bank[5], n * QH * NCMP, [[1, QH], [QH, NCMP]]),
                   view(CON, CC["cmp_add"] + n * NCMP, [[0, QH], [1, NCMP]]), ALU.add)
            ve.wait_ge(sem("cmp_ps"), 1)
            for hf in range(2):
                ins = ve.tensor_copy(view(BIG, KC + hf * NCMP, [[2 * NCMP, 2], [1, NCMP]]),
                                     view(bank[7], hf * 2 * NCMP, [[NCMP, 2], [1, NCMP]]))
            lk(ins)
            ve.tensor_copy(BIG[0:NCMP, VC:VC + 256], bank[7][0:NCMP, 128:384])
            kc = big(KC, 4 * NCMP)
            lk(tt(SM[:, 128:128 + 4 * NCMP], kc, kc, ALU.mult))
            ve.nop().then_inc(sem("kc_sq"), 1)
            ve.wait_ge(sem("kc_sum"), 1)
            lk(ve.tensor_scalar(SM[:, 192:192 + 4 * NCMP], bank[7][:, 64:64 + 4 * NCMP], 1 / 64, EPS, ALU.mult, ALU.add))
            ve.nop().then_inc(sem("kc_ms"), 1)
            ve.wait_ge(sem("kc_rs"), 1)
            refine(SM[:, 256:256 + 4 * NCMP], SM[:, 192:192 + 4 * NCMP], SM[:, 320:320 + 4 * NCMP])
            ve.scalar_tensor_tensor(kc, kc, par("k_norm_cmp", 1), SM[:, 256:256 + 4 * NCMP], ALU.mult, ALU.mult)
            stage_end(ve, "ve")
            ffn2("ffn1_1", 1)
            norm_v(norms, ("mix_norm", 8), False)
            norms += 1
            for u in range(4):
                ve.wait_ge(sem("unit_done"), UN["q"] + u + 1)
                lk(ve.tensor_copy(big(QB + u * 512, 512), bank[u][:, :]))
            stage_end(ve, "ve")
            tt(big(PT, 2048), big(QB, 2048), big(QB, 2048), ALU.mult).then_inc(sem("q_sq"), 1)
            ve.wait_ge(sem("gate_exp"), 1)
            lk(ve.tensor_scalar(big(GT, 96), big(GT, 96), 1.0, None, ALU.add))
            ve.reciprocal(big(GT, 96), big(GT, 96))
            ve.wait_ge(sem("q_sum"), 1)
            for b in range(4):
                ins = ve.tensor_scalar(big(PT + b * 512, 512), bank[b][:, :], 1 / 64, EPS, ALU.mult, ALU.add)
            lk(ins)
            ve.nop().then_inc(sem("q_ms"), 1)
            ve.wait_ge(sem("q_rs"), 1)
            refine(big(PT + 2048, 2048), big(PT, 2048), big(PT + 4096, 2048))
            ve.scalar_tensor_tensor(big(QB, 2048), big(QB, 2048), par("q_norm", 1), big(PT + 2048, 2048), ALU.mult, ALU.mult)
            stage_end(ve, "ve")
            W_ = QH * NCMP
            ve.wait_ge(sem("cmp_logits"), 1)
            for b in range(2):
                every = [[2 * NCMP, QH], [1, NCMP]]
                lk(ve.scalar_tensor_tensor(view(BIG, CP + b * NCMP, every), view(bank[b], b * NCMP, every), 0.125,
                                           view(BIG, CB + b * NCMP, every), ALU.mult, ALU.add))
            c3 = view(BIG, CP, [[NCMP, 2 * QH], [1, NCMP]])
            lk(ve.tensor_reduce(SM[:, 0:32], c3, AX, ALU.max))
            lk(tt(c3, c3, view(SM, 0, [[1, 32], [0, NCMP]]), ALU.subtract))
            ve.nop().then_inc(sem("cmp_arg"), 1)
            ve.wait_ge(sem("cmp_exp"), 1)
            lk(ve.tensor_reduce(SM[:, 32:64], c3, AX, ALU.add))
            lk(ve.reciprocal(SM[:, 32:64], SM[:, 32:64]))
            lk(tt(SM[:, 32:64], SM[:, 32:64], view(BIG, GT, [[3, 32]]), ALU.mult))
            lk(tt(c3, c3, view(SM, 32, [[1, 32], [0, NCMP]]), ALU.mult))
            for n in range(NT):
                cn = view(BIG, CP + n * W_, [[NCMP, QH], [1, NCMP]])
                ins = tt(cn, cn, view(CON, CC["cmp_mul"] + n * NCMP, [[0, QH], [1, NCMP]]), ALU.mult)
            lk(ins)
            ve.nop().then_inc(sem("cmp_p"), 1)
            stage_end(ve, "ve")
            ve.wait_ge(sem("cmp_pt"), 1)
            for b in range(8):
                ve.tensor_copy(BIG[0:NCMP, CPT + b * 512:CPT + (b + 1) * 512], bank[b][0:NCMP, :])
            stage_end(ve, "ve")
            ve.wait_ge(sem("bias_here"), 16)
            for br in range(2):
                for h in range(QH):
                    b = bank[h % 8]
                    ve.wait_ge(sem("logits_ps"), br * 16 + h + 1)
                    two = [[P, 2], [1, P]]
                    ve.scalar_tensor_tensor(view(BIG, LG + h * 384, two), view(b, 0, two), 0.125,
                                            view(BIG, BT + h * 256 + P - 1, [[P, 2], [-1, P]]), ALU.mult, ALU.add)
                    ve.scalar_tensor_tensor(big(LG + h * 384 + 256, 128), b[:, 256:384], 0.125,
                                            view(BIG, BT + h * 256 + P - 1, [[-1, P]]),
                                            ALU.mult, ALU.add).then_inc(sem("logits_out"), 1)
                ve.wait_ge(sem("logits_out"), br * 16 + 16)
                lk(ve.tensor_reduce(SM[:, 0:16], view(BIG, LG, [[384, QH], [1, P]]), AX, ALU.max))
                lk(ve.tensor_reduce(SM[:, 16:32], view(BIG, LG + P, [[384, QH], [1, TOK]]), AX, ALU.max))
                lk(ve.tensor_scalar(SM[:, 32:64], SM[:, 0:32], -1.0, None, ALU.mult))
                ve.nop().then_inc(sem("row_max"), 1)
                ve.wait_ge(sem("row_exp"), br + 1)
                lk(ve.reciprocal(SM[:, 64:96], SM[:, 64:96]))
                lk(tt(SM[:, 64:96], SM[:, 64:96], view(BIG, GT + 1 + br, [[3, 32]]), ALU.mult))
                a0 = view(BIG, LG, [[384, QH], [1, P]])
                a1 = view(BIG, LG + P, [[384, QH], [1, TOK]])
                tt(a0, a0, view(SM, 64, [[1, 16], [0, P]]), ALU.mult)
                lk(tt(a1, a1, view(SM, 80, [[1, 16], [0, TOK]]), ALU.mult))
                ve.nop().then_inc(sem("probs"), 1)
                for h in range(QH):
                    ve.wait_ge(sem("pt_ps"), br * 16 + h + 1)
                    ve.tensor_copy(big(PT + h * 384, 384), bank[h % 8][:, 0:384]).then_inc(sem("pt_out"), 1)
                ve.wait_ge(sem("o_branch"), br + 1)
                for b in range(4):
                    if br == 0:
                        ve.tensor_copy(big(OB + b * 512, 512), bank[b][:, :])
                    else:
                        tt(big(OB + b * 512, 512), big(OB + b * 512, 512), bank[b][:, :], ALU.add)
                stage_end(ve, "ve")
            for b in range(4):
                ve.wait_ge(sem("unit_done"), UN["w_o"] + b + 1)
                tt(X[:, b * 512:(b + 1) * 512], X[:, b * 512:(b + 1) * 512], bank[b][:, :], ALU.add)
            stage_end(ve, "ve")
            ffn2("ffn2_1", 1, last=True)

        @stage.scalar
        def _(se):
            act = se.activation

            def lk(ins):
                link(se, "scalar_step", ins)

            def norm_s(i, shift=None):
                se.wait_ge(*at("norm_sum", 1, i))
                lk(act(LNB[:, :], bank[7][:, 0:TOK], ACT.Ln, bias=EPSB[:, 0:1], scale=1 / D))
                act(RS[:, :], LNB[:, :], ACT.Exp, scale=-0.5).then_inc(sem("norm_rs"), 1)
                if shift is not None:
                    l, part = shift
                    for t in range(KT):
                        se.wait_ge(sem("norm_scaled"), counts["scaled"] + t + 1)
                        act(H[:, t * TOK:(t + 1) * TOK], H[:, t * TOK:(t + 1) * TOK], ACT.Identity,
                            bias=MOD[:, l * 48 + part * 8 + t:l * 48 + part * 8 + t + 1]).then_inc(sem("normed"), 1)
                    counts["scaled"] += KT

            counts = {"scaled": 0}

            def ffn_s(blocks, base, units0, expert=None, width=2 * TOK):
                b0 = base if expert is None else expert * blocks + base
                u0 = units0 if expert is None else expert * (3 * blocks) + units0

                def silu(par2, count, units):
                    se.wait_ge(sem("unit_done"), units)
                    c = count - 1
                    if not (isinstance(c, int) and c <= 0):
                        se.wait_ge(sem("gated"), c)
                    act(FS[:, par2 * 512:par2 * 512 + width], bank[2 * par2][:, 0:width], ACT.Silu).then_inc(sem("silu"), 1)

                silu(0, b0, u0 + 1)
                silu(1, b0 + 1, u0 + 3)
                steps_left = blocks - 2
                with se.Fori(0, steps_left // 2) as i:
                    for hs in range(2):
                        silu(hs, i * 2 + (b0 + 2 + hs), i * 6 + (u0 + 6 + 3 * hs))
                done = steps_left // 2 * 2
                if steps_left % 2:
                    silu(0, b0 + 2 + done, u0 + 6 + 3 * done)

            se.wait_ge(sem("eps_set"), 1)
            se.wait_ge(sem("inputs"), 48)
            act(SM[:, 0:8], par("c", 8), ACT.Silu).then_inc(sem("c_act"), 1)
            se.nop().then_inc(sem("evac"), 6)
            se.nop().then_inc(sem("ada_free"), 1)
            stage_end(se, "se")
            norms = 0
            for l in range(LAYERS):
                norm_s(norms, (l, 0))
                norms += 1

                with se.Fori(0, 2) as i:
                    for u in range(RING):
                        se.wait_ge(sem("unit_done"), i * RING + (UN[f"w_in{l}"] + u + 1))
                        act(BIG[:, bass.ds(i * 3072 + (PROJ + u * 512), 512)], bank[u][:, :], ACT.Copy).then_inc(sem("evac"), 1)
                with se.Fori(0, 3) as i:
                    for u in range(RING):
                        se.wait_ge(sem("unit_done"), i * RING + (UN[f"w_in{l}"] + 12 + u + 1))
                        act(BIG[:, bass.ds(i * 3072 + (PROJ + 6144 + u * 512), 512)], bank[u][:, :], ACT.Copy).then_inc(sem("evac"), 1)
                    se.wait_ge(sem("conv_tap"), i * 4 + (l * 12 + 4))
                    c = BIG[:, bass.ds(i * 2048 + CONV, 2048)]
                    act(c, c, ACT.Silu)
                se.wait_ge(sem("evac"), l * 30 + 36)
                lk(act(big(Z_, 2048), big(Z_, 2048), ACT.Silu))
                act(big(GATES, 4096), big(GATES, 4096), ACT.Sigmoid)
                stage_end(se, "se")
                act(view(SM, 0, [[8, 2], [1, 8]]), view(bank[6], 0, [[16, 2], [1, 8]]), ACT.Exp, scale=-1.0).then_inc(sem("beta_exp"), 1)
                lk(act(SM[:, 48:64], par("a_log", 16, l * 16), ACT.Exp))
                se.wait_ge(*at("a_abs", 1, l, 1))
                lk(act(SM[:, 32:48], SM[:, 32:48], ACT.Exp, scale=-1.0))
                act(SM[:, 32:48], SM[:, 32:48], ACT.Ln, bias=1.0).then_inc(sem("a_ln"), 1)
                se.wait_ge(*at("qk_sum", 1, l, 1))
                for b in range(8):
                    ins = act(big(SLOT["D"] + b * 512, 512), bank[b][:, :], ACT.Ln, bias=EPSB[:, 0:1])
                lk(ins)
                lk(act(big(SLOT["D"], 2048), big(SLOT["D"], 2048), ACT.Exp, scale=-0.5, bias=EPSB[:, 1:2]))
                act(big(SLOT["E"], 2048), big(SLOT["E"], 2048), ACT.Exp, scale=-0.5).then_inc(sem("qk_rs"), 1)
                se.wait_ge(*at("decay_arg", 1, l, 1))
                act(big(EG, 512), bank[2][:, :], ACT.Exp)
                act(big(EG + 512, 512), bank[3][:, :], ACT.Exp)
                act(big(SLOT["B"], 2048), big(SLOT["B"], 2048), ACT.Exp)
                act(big(SLOT["C"], 2048), big(SLOT["C"], 2048), ACT.Exp, scale=-1.0)
                se.wait_ge(*at("kd_arg", 1, l, 1))
                act(SM[:, 128:144], SM[:, 112:128], ACT.Exp)
                lk(act(SM[:, 144:160], SM[:, 80:96], ACT.Exp))
                se.nop().then_inc(sem("decay_exp"), 1)
                stage_end(se, "se")
                se.wait_ge(*at("lt", 1, l, 1))
                for b in range(4):
                    ins = act(big(SLOT["C"] + b * 512, 512), bank[b][:, :], ACT.Copy)
                ins.then_inc(sem("lt_out"), 1)
                stage_end(se, "se")
                for s in range(6):
                    for q in range(4):
                        se.wait_ge(*at("level_u", 4 * s + q + 1, l, 24))
                        act(big(UBUF + q * 512, 512), bank[q][:, :], ACT.Copy).then_inc(sem("level_uc"), 1)
                stage_end(se, "se")
                stage_end(se, "se")
                se.wait_ge(*at("vnew_ps", 1, l, 1))
                act(big(WT, 512), bank[2][:, :], ACT.Copy, scale=-1.0)
                act(big(WT + 512, 512), bank[3][:, :], ACT.Copy, scale=-1.0).then_inc(sem("w_neg"), 1)
                se.wait_ge(*at("o_ps", 1, l, 1))
                for b in range(4):
                    ins = act(big(SLOT["E"] + b * 512, 512), bank[b][:, :], ACT.Square)
                ins.then_inc(sem("o_sq"), 1)
                se.wait_ge(*at("o_sum", 1, l, 1))
                for b in range(4):
                    ins = act(big(SLOT["E"] + b * 512, 512), bank[4 + b][:, :], ACT.Ln, bias=EPSB[:, 0:1], scale=1 / P)
                lk(ins)
                act(big(SLOT["E"], 2048), big(SLOT["E"], 2048), ACT.Exp, scale=-0.5).then_inc(sem("o_rs"), 1)
                stage_end(se, "se")
                se.wait_ge(*at("z_out", 8, l, 8))
                lk(act(big(SP, 3072), big(ZB, 3072), ACT.Abs))
                lk(act(big(SP, 3072), big(SP, 3072), ACT.Exp, scale=-1.0))
                act(big(SP, 3072), big(SP, 3072), ACT.Ln, bias=1.0).then_inc(sem("sp_ln"), 1)
                se.wait_ge(*at("stick_arg", 1, l, 1))
                act(big(ZB, 3072), big(ZB, 3072), ACT.Exp).then_inc(sem("stick_p"), 1)
                stage_end(se, "se")
                stage_end(se, "se")
                norm_s(norms, (l, 3))
                norms += 1
                if l == 0:
                    ffn_s(BLK1, 0, UN["ffn"])
                    stage_end(se, "se")
                    continue
                se.wait_ge(sem("hn_ps"), 1)
                for b in range(4):
                    ins = act(big(HN + b * 512, 512), bank[4 + b][:, :], ACT.Copy)
                ins.then_inc(sem("hn_out"), 1)
                se.wait_ge(sem("route_arg"), 1)
                act(SM[:, 48:50], SM[:, 48:50], ACT.Exp).then_inc(sem("route_exp"), 1)
                stage_end(se, "se")
                se.nop().then_inc(sem("gather_high"), 2)
                with se.Fori(0, EXPERTS // 2) as i:
                    for j in range(2):
                        se.wait_ge(sem("gather_ps"), i * 2 + (j + 1))
                        act(BIG[:, bass.ds(i * 2048 + (HG + j * 1024 + 512), 512)], bank[5 + 2 * j][:, :], ACT.Copy)\
                            .then_inc(sem("gather_high"), 1)
                se.wait_ge(sem("selt_ps"), 1)
                for b in range(4):
                    act(big(SELT + b * 512, 512), bank[b][:, :], ACT.Copy)
                stage_end(se, "se")
                with se.Fori(0, EXPERTS) as e:
                    count = se.value_load(SMU[0:1, bass.ds(e + 16, 1)], min_val=0, max_val=TOK)
                    with se.If(count <= P):
                        ffn_s(BLK1, BLK1, UN["moe"], e, width=2 * P)
                        se.wait_ge(sem("unit_done"), e * (3 * BLK1) + (UN["moe"] + 3 * BLK1))
                        act(BIG[:, bass.ds(e * 1024 + YS, 512)], bank[4][:, :], ACT.Copy)
                        act(BIG[:, bass.ds(e * 1024 + (YS + 512), 512)], bank[5][:, :], ACT.Copy).then_inc(sem("expert_out"), 1)
                    with se.Else():
                        ffn_s(BLK1, BLK1, UN["moe"], e)
                stage_end(se, "se")
                stage_end(se, "se")
            norm_s(norms)
            stage_end(se, "se")
            norms += 1
            done_blocks = BLK1 * (1 + EXPERTS)

            def ffn2(name):
                nonlocal norms, done_blocks
                norm_s(norms)
                norms += 1
                ffn_s(BLK2, done_blocks, UN[name])
                done_blocks += BLK2
                if name != "ffn2_1":
                    stage_end(se, "se")

            act(SM[:, 0:32], par("log_dt", 32), ACT.Exp).then_inc(sem("s5_dt"), 1)
            se.wait_ge(sem("s5_mag_arg"), 1)
            lk(act(SM[:, 32:64], SM[:, 32:64], ACT.Exp))
            se.wait_ge(sem("angles"), 1)
            lk(act(SM[:, 256:768], SM[:, 256:768], ACT.Sin))
            se.nop().then_inc(sem("s5_trig"), 1)
            ffn2("ffn1_0")
            norm_s(norms)
            norms += 1
            se.wait_ge(sem("y_out"), KT)
            act(big(YB, 2048), big(YB, 2048), ACT.Gelu_apprx_tanh).then_inc(sem("y_gelu"), 1)
            stage_end(se, "se")
            for u in range(4):
                se.wait_ge(sem("unit_done"), UN["glu"] + u + 1)
                act(big(SLOT["D"] + u * 512, 512), bank[u][:, :], ACT.Sigmoid).then_inc(sem("glu_sig"), 1)
            stage_end(se, "se")
            ffn2("ffn2_0")
            norm_s(norms)
            norms += 1
            stage_end(se, "se")
            se.wait_ge(sem("kv_ms"), 1)
            lk(act(big(KRS, 1024), big(KSQ, 1024), ACT.Ln))
            act(big(KRS, 1024), big(KRS, 1024), ACT.Exp, scale=-0.5).then_inc(sem("kv_rs"), 1)
            se.wait_ge(sem("k_normed"), 1)
            for br, t0 in enumerate((4, 8)):
                for g in range(4):
                    s0 = 64 * (g % 2)
                    for d0 in (0, 64):
                        se.dma_start(BIG[d0:d0 + 64, KD + br * 1024 + g * TOK:KD + br * 1024 + (g + 1) * TOK],
                                     BIG[s0:s0 + 64, KV + (t0 + g // 2) * TOK:KV + (t0 + g // 2 + 1) * TOK]).then_inc(sem("k_dup"), 16)
            se.wait_ge(sem("bias_tab"), 1)
            se.dma_start(tab_dram, BIG[0:QH, BTAB:BTAB + 384]).then_inc(sem("tab_out"), 16)
            se.wait_ge(sem("tab_out"), 16)
            for blk in range(2):
                se.dma_start(view(BIG, BT + blk * P, [[TOK, QH], [1, P]]),
                             bass.AP(tensor=tab_dram.tensor, offset=P * blk, ap=[[1, P], [384, QH], [1, P]]))\
                    .then_inc(sem("bias_here"), 16)
            se.wait_ge(sem("hid_ps"), 1)
            for hf in range(2):
                ins = act(view(SM, hf * 2 * NCMP, [[4 * NCMP, 2], [1, 2 * NCMP]]), view(PS, HID[hf], [[2 * NCMP, 2], [1, 2 * NCMP]]),
                          ACT.Gelu_apprx_tanh)
            ins.then_inc(sem("hid"), 1)
            se.wait_ge(sem("kc_ms"), 1)
            lk(act(SM[:, 256:256 + 4 * NCMP], SM[:, 192:192 + 4 * NCMP], ACT.Ln))
            act(SM[:, 256:256 + 4 * NCMP], SM[:, 256:256 + 4 * NCMP], ACT.Exp, scale=-0.5).then_inc(sem("kc_rs"), 1)
            se.wait_ge(sem("k_dup"), 16 * 16)
            se.wait_ge(sem("bias_here"), 32)
            stage_end(se, "se")
            ffn2("ffn1_1")
            norm_s(norms)
            norms += 1
            stage_end(se, "se")
            se.wait_ge(sem("gate_logits"), 1)
            act(big(GT, 96), bank[4][:, 0:96], ACT.Exp, scale=-1.0).then_inc(sem("gate_exp"), 1)
            se.wait_ge(sem("q_ms"), 1)
            lk(act(big(PT + 2048, 2048), big(PT, 2048), ACT.Ln))
            act(big(PT + 2048, 2048), big(PT + 2048, 2048), ACT.Exp, scale=-0.5).then_inc(sem("q_rs"), 1)
            stage_end(se, "se")
            se.wait_ge(sem("cmp_arg"), 1)
            act(big(CP, 2 * QH * NCMP), big(CP, 2 * QH * NCMP), ACT.Exp).then_inc(sem("cmp_exp"), 1)
            stage_end(se, "se")
            stage_end(se, "se")
            for br in range(2):
                se.wait_ge(sem("row_max"), br + 1)
                for h in range(QH):
                    for n in range(NT):
                        r = big(LG + h * 384 + n * P, P * (n + 1))
                        ins = act(r, r, ACT.Exp, bias=SM[:, 32 + n * 16 + h:33 + n * 16 + h],
                                  accum_out=SM[:, 64 + n * 16 + h:65 + n * 16 + h])
                lk(ins)
                se.nop().then_inc(sem("row_exp"), 1)
                stage_end(se, "se")
            stage_end(se, "se")
            ffn2("ffn2_1")

        @stage.gpsimd
        def _(po):
            def lk(ins):
                link(po, "pool_step", ins)

            po.memset(EPSB[:, 0:1], EPS)
            po.memset(EPSB[:, 1:2], float(-0.5 * np.log(P))).then_inc(sem("eps_set"), 1)
            po.wait_ge(sem("inputs"), 48)
            stage_end(po, "po")
            for l in range(LAYERS):
                stage_end(po, "po")
                stage_end(po, "po")
                stage_end(po, "po")
                for s in range(6):
                    if s >= 2:
                        po.wait_ge(*at("level_u", 4 * (s - 1), l, 24))
                    for q in range(4):
                        po.tensor_tensor(view(BIG, LTS[s % 2] + q * 512, [[P, 4], [1, P]]), view(BIG, SLOT["C"] + q * 512, [[P, 4], [1, P]]),
                                         view(CON, CC["level"] + (s + 1) * P, [[0, 4], [1, P]]), ALU.mult).then_inc(sem("level_mask"), 1)
                stage_end(po, "po")
                stage_end(po, "po")
                stage_end(po, "po")
                stage_end(po, "po")
                stage_end(po, "po")
                if l == 0:
                    stage_end(po, "po")
            stage_end(po, "po")
            for e in range(EXPERTS):
                po.memset(big(YS + e * 1024, 1024), 0.0)
            stage_end(po, "po")
            stage_end(po, "po")
            stage_end(po, "po")
            stage_end(po, "po")
            for i, name in enumerate(("b_re", "b_im", "c_re", "c_im")):
                po.dma_start(big(S5P + i * 512, 512), A[name]).then_inc(sem("s5_here"), 16)
            for q in range(4):
                po.memset(view(BIG, TC + q * 2048, [[TOK, 8], [1, 1]]), 1.0)
                ins = po.memset(view(BIG, TS + q * 2048, [[TOK, 8], [1, 1]]), 0.0)
            lk(ins)
            po.wait_ge(sem("s5_trig"), 1)
            for q in range(4):
                c0, s0 = TC + q * 2048, TS + q * 2048
                for k in range(8):
                    n = 2 ** k

                    def old(b):
                        return view(BIG, b, [[TOK, 8], [1, n]])

                    def new(b):
                        return view(BIG, b + n, [[TOK, 8], [1, n]])

                    cw = view(SM, 512 + 32 * k + 8 * q, [[1, 8], [0, n]])
                    sw = view(SM, 256 + 32 * k + 8 * q, [[1, 8], [0, n]])
                    t1 = view(BIG, PT1, [[n, 8], [1, n]])
                    t2 = view(BIG, PT1 + 1024, [[n, 8], [1, n]])
                    po.tensor_tensor(new(c0), old(c0), cw, ALU.mult)
                    po.tensor_tensor(t1, old(s0), sw, ALU.mult)
                    po.tensor_tensor(new(s0), old(s0), cw, ALU.mult)
                    lk(po.tensor_tensor(t2, old(c0), sw, ALU.mult))
                    po.tensor_tensor(new(c0), new(c0), t1, ALU.subtract)
                    lk(po.tensor_tensor(new(s0), new(s0), t2, ALU.add))
            po.nop().then_inc(sem("tables"), 1)
            stage_end(po, "po")
            for k in range(KT):
                po.wait_ge(sem("scanned"), k + 1)
                c, s = big(TC + k * 1024, 1024), big(TS + k * 1024, 1024)
                po.tensor_tensor(big(ROT[0], 1024), c, big(YR, 1024), ALU.mult)
                po.tensor_tensor(big(ROT[1], 1024), s, big(YI, 1024), ALU.mult)
                po.tensor_tensor(big(ROT[2], 1024), s, big(YR, 1024), ALU.mult)
                lk(po.tensor_tensor(big(ROT[3], 1024), c, big(YI, 1024), ALU.mult))
                po.nop().then_inc(sem("rotated"), 1)
            stage_end(po, "po")
            stage_end(po, "po")
            stage_end(po, "po")
            for i, name in enumerate(("w1_k", "w1_v")):
                po.dma_start(big(W1 + i * 4096, 4096), A[name]).then_inc(sem("w1_here"), 16)
            stage_end(po, "po")
            stage_end(po, "po")
            stage_end(po, "po")
            stage_end(po, "po")
            stage_end(po, "po")
            stage_end(po, "po")
            stage_end(po, "po")
            stage_end(po, "po")
            stage_end(po, "po")
            stage_end(po, "po")


def laid_out(inputs):
    a = {k: np.asarray(v) for k, v in inputs.items()}

    def cols(w, kt=KT, tiles=2):
        k, n = w.shape
        return w.reshape(kt, P, n // (tiles * P), tiles * P).transpose(2, 1, 0, 3).reshape(-1, P, UNIT)

    def rows(w):
        return w.reshape(w.shape[0] // 256, 2, P, D).transpose(0, 2, 1, 3).reshape(-1, P, UNIT)

    def swiglu(w1, w3, w2):
        u1, u3, u2 = cols(w1), cols(w3), rows(w2)
        n = len(u1)
        out = [u1[0], u3[0]]
        for b in range(1, n):
            out += [u1[b], u3[b], u2[b - 1]]
        return out + [u2[n - 1]]

    wall = np.empty((NUNITS, P, UNIT), np.float32)
    at = 0

    def put(units):
        nonlocal at
        for u in units:
            wall[at] = u
            at += 1

    b0, b1 = 3072 + D, 3072 + D + 16
    for l in range(LAYERS):
        put(cols(a["ada_w"][l]))
    for l in range(LAYERS):
        w = a["w_in"][l]
        put(cols(np.concatenate([w[:, :b0], w[:, b1:]], 1)))
        put(cols(a["w_up_dn"][l]))
        put(cols(a["w_up_sb"][l], 4, 4))
        put(cols(a["w_out"][l]))
        if l == 0:
            put(swiglu(a["ffn_w1"][0], a["ffn_w3"][0], a["ffn_w2"][0]))
        else:
            for e in range(EXPERTS):
                put(swiglu(a["moe_w1"][0, e], a["moe_w3"][0, e], a["moe_w2"][0, e]))

    def ffn2(i, l):
        w = a[f"ffn{i}_w_in_2"][l]
        put(swiglu(w[:, :FF2], w[:, FF2:], a[f"ffn{i}_w_out_2"][l]))

    ffn2(1, 0)
    put(cols(a["s5_w_glu_2"][0]))
    ffn2(2, 0)
    put(cols(a["w_kv_2"]))
    ffn2(1, 1)
    put(cols(a["w_qg_2"][0][:, :D]))
    put(cols(a["w_o_2"][0]))
    ffn2(2, 1)
    assert at == NUNITS

    def chan(v):
        return v.reshape(-1, P).T

    def narrow(w):
        return w.reshape(KT, P, -1).transpose(1, 0, 2).reshape(P, -1)

    def spread(v):
        return np.broadcast_to(v, (P, v.size))

    def twice(v):
        return np.concatenate([v, v], 0)

    def by_state(v):
        return v.reshape(PAIRS, P).T

    def by_state3(v):
        return np.ascontiguousarray(v.reshape(PAIRS, P, 16).transpose(1, 0, 2).reshape(P, 512))

    par = np.zeros((P, PC["width"]), np.float32)

    def small(name, v):
        par[:v.shape[0], PC[name]:PC[name] + v.shape[1]] = v

    small("c", chan(a["c"][0]))
    small("ada_b", np.concatenate([chan(a["ada_b"][l]) for l in range(LAYERS)], 1))
    for name, key in (("norm_mix", "norm_mix"), ("norm_ffn", "norm_ffn"), ("ffn1_norm", "ffn1_norm_2"),
                      ("mix_norm", "mix_norm_2"), ("ffn2_norm", "ffn2_norm_2")):
        small(name, np.concatenate([chan(a[key][l]) for l in range(LAYERS)], 1))
    small("conv_w", a["conv_w"].reshape(LAYERS, 4, 24, P).transpose(3, 0, 2, 1).reshape(P, -1))
    small("dn_out_norm", a["dn_out_norm"].T)
    small("dt_bias", spread(np.concatenate([v for l in range(LAYERS) for v in (a["dn_dt_bias"][l],) * NT])))
    small("a_log", spread(np.concatenate([v for l in range(LAYERS) for v in (a["dn_a_log"][l],) * NT])))
    small("final_norm", chan(a["final_norm"]))
    small("router_b", spread(np.concatenate([a["router_b"][0]] * NT)))
    small("s5_d", chan(a["s5_d_2"][0].reshape(-1)))
    small("kv_norm", chan(a["kv_norm_2"]))
    for name in ("k_norm_cmp", "k_norm_slc", "k_norm_win"):
        small(name, twice(a[name + "_2"])[:, None])
    small("q_norm", twice(a["q_norm_2"][0])[:, None])
    small("a_re", by_state(a["s5_a_re_2"][0]))
    small("a_im", by_state(a["s5_a_im_2"][0]))
    small("log_dt", by_state(np.repeat(a["s5_log_dt_2"][0][:, None], STATES, 1)))
    small("pos_k", twice(a["cmp_pos_k_2"].T))
    small("pos_v", twice(a["cmp_pos_v_2"].T))
    small("w_ba", np.concatenate([narrow(a["w_in"][l][:, b0:b1]) for l in range(LAYERS)], 1))
    small("router_w", narrow(a["router_w"][0]))
    small("w_gate", narrow(a["w_qg_2"][0][:, D:]))
    small("w2_k", np.concatenate([a["cmp_k_w2_2"]] * 2, 1))
    small("w2_v", np.concatenate([a["cmp_v_w2_2"]] * 2, 1))
    small("rel_bias", a["rel_bias_2"])

    def first(w):
        return np.ascontiguousarray(twice(w.transpose(1, 0, 2).reshape(64, -1)))

    return {
        "wall": wall, "par": par, "con": constants(),
        "x": np.ascontiguousarray(a["x"][0].reshape(TOK, KT, P).transpose(2, 1, 0).reshape(P, -1)),
        "b_re": by_state3(a["s5_b_re_2"][0]), "b_im": by_state3(a["s5_b_im_2"][0]),
        "c_re": by_state3(a["s5_c_re_2"][0].transpose(0, 2, 1)), "c_im": by_state3(a["s5_c_im_2"][0].transpose(0, 2, 1)),
        "w1_k": first(a["cmp_k_w1_2"]), "w1_v": first(a["cmp_v_w1_2"]),
    }


def constants():
    con = np.zeros((P, CC["width"]), np.float32)
    i, j = np.arange(P)[:, None], np.arange(P)[None, :]

    def put(name, v, extra=0):
        con[:v.shape[0], CC[name] + extra:CC[name] + extra + v.shape[1]] = v

    put("ident", i == j)
    put("ones", np.ones((P, P)))
    put("half_ones", i // 64 == j // 64)
    put("upper", i <= j)
    put("lower_strict", j < i)
    put("key_after", i >= j)
    for s in range(7):
        b = 2 ** s
        put("level", (i // b % 2 == 0) & (j // b == i // b + 1), s * P)
    put("level0_lower", (i % 2 == 1) & (j == i - 1))
    diag = np.where(i >= j, NEG, 0.0)
    put("stick_mask", np.concatenate([diag, np.zeros((P, P)), diag], 1))
    put("iota", np.broadcast_to(np.arange(8), (P, 8)))
    for n in range(NT):
        dist = (n * P + i) - (16 * np.arange(NCMP)[None, :] + 31)
        put("cmp_add", np.where(dist >= 0, 0.0, NEG), n * NCMP)
        put("cmp_mul", dist >= 0, n * NCMP)
    dist = np.arange(TOK)
    far = np.log(np.maximum(dist, 1).astype(np.float32) / np.float32(16)) / np.float32(np.log(128 / 16))
    bucket = np.where(dist < 16, dist, np.minimum(16 + (far * 16).astype(np.int32), 31))
    onehot = (np.arange(32)[:, None] == bucket[None, :]).astype(np.float32)
    put("onehot", onehot, 255)
    return con


def build(nc):
    A = {}
    for name, shape in (("wall", (NUNITS, P, UNIT)), ("par", (P, PC["width"])), ("con", (P, CC["width"])), ("x", (P, 2048)),
                        ("b_re", (P, 512)), ("b_im", (P, 512)), ("c_re", (P, 512)), ("c_im", (P, 512)),
                        ("w1_k", (P, 4096)), ("w1_v", (P, 4096))):
        A[name] = nc.dram_tensor(f"in_{name}", shape, F32, kind="ExternalInput").ap()
    A["tab"] = nc.dram_tensor("bias_table", (QH, 384), F32, kind="Internal").ap()
    A["out"] = nc.dram_tensor("out", (P, 2048), F32, kind="ExternalOutput").ap()
    program(nc, A)


def kernel(**inputs):
    import concourse.bacc as _bacc
    from concourse.bass_utils import run_bass_kernel_spmd as _run

    nc = _bacc.Bacc("TRN2", target_bir_lowering=False, num_devices=1)
    arrays = {f"in_{k}": v for k, v in laid_out(inputs).items()}
    build(nc)
    r = _run(nc, [arrays], core_ids=[0])
    got = np.asarray(r.results[0]["out"])
    return np.ascontiguousarray(got.reshape(P, KT, TOK).transpose(2, 1, 0).reshape(1, TOK, D))
```

```python
from contextlib import ExitStack

import concourse.bass as bass
from concourse import mybir
import numpy as np

F32 = mybir.dt.float32
U32 = mybir.dt.uint32
F32R = mybir.dt.float32r
ALU = mybir.AluOpType
ACT = mybir.ActivationFunctionType
AX = mybir.AxisListType.X

P = 128
TOK = 256
NT = TOK // P
D = 1024
KT = D // P
LAYERS = 2
HEADS = 8
FF1 = 3584
FF2 = 2816
EXPERTS = 8
BLK1 = FF1 // 256
BLK2 = FF2 // 256
STATES = 64
PAIRS = 32
QH = 16
NCMP = (TOK - 32) // 16 + 1
NEG = -1e30
EPS = 1e-6
RING = 6
UNIT = 2048
TWO_PI = 2 * np.pi


def columns(spec):
    at, out = 0, {}
    for name, width in spec:
        out[name] = at
        at += width
    out["width"] = at
    return out


CC = columns([("ident", 128), ("ones", 128), ("half_ones", 128), ("upper", 128), ("lower_strict", 128),
              ("key_after", 128), ("level0_lower", 128), ("level", 7 * 128), ("stick_mask", 384), ("iota", 8),
              ("cmp_add", NT * NCMP), ("cmp_mul", NT * NCMP), ("onehot", 511)])
PC = columns([("c", 8), ("ada_b", 96), ("norm_mix", 16), ("norm_ffn", 16), ("conv_w", 192), ("dn_out_norm", 2),
              ("dt_bias", 32), ("a_log", 32), ("final_norm", 8), ("router_b", 16), ("ffn1_norm", 16),
              ("mix_norm", 16), ("ffn2_norm", 16), ("s5_d", 8), ("kv_norm", 8), ("k_norm_cmp", 1),
              ("k_norm_slc", 1), ("k_norm_win", 1), ("q_norm", 1), ("a_re", 32), ("a_im", 32), ("log_dt", 32),
              ("pos_k", 32), ("pos_v", 32), ("w_ba", 256), ("router_w", 64), ("w_gate", 384), ("w2_k", 128),
              ("w2_v", 128), ("rel_bias", 16)])
UN = columns([("ada0", 24), ("ada1", 24), ("w_in0", 30), ("up0", 6), ("w_out0", 4), ("ffn", 3 * BLK1),
              ("w_in1", 30), ("up1", 6), ("w_out1", 4), ("moe", 3 * BLK1 * EXPERTS),
              ("ffn1_0", 3 * BLK2), ("glu", 4), ("ffn2_0", 3 * BLK2), ("kv", 6), ("ffn1_1", 3 * BLK2),
              ("q", 4), ("w_o", 4), ("ffn2_1", 3 * BLK2)])
NUNITS = UN["width"]

TOTAL = dict(norm_sq=1, norm_sum=1, norm_rs=1, normed=8)


def program(nc, A):
    ctx = ExitStack()
    with ctx:
        def sb(name, cols, dt=F32):
            return ctx.enter_context(nc.sbuf_tensor(name, [P, cols], dt))

        sems = {}

        def sem(name):
            if name not in sems:
                sems[name] = ctx.enter_context(nc.semaphore(name))
            return sems[name]

        def at(name, count, stage=0, total=None):
            return sem(name), stage * (TOTAL[name] if total is None else total) + count

        with ExitStack() as plain:
            ring = [plain.enter_context(nc.sbuf_tensor(f"ring{r}", [P, UNIT], F32)) for r in range(RING)]
        ring_low = [sb(f"ring_low{r}", UNIT, F32R) for r in range(RING)]
        X = sb("x", KT * TOK)
        CON = sb("constants", CC["width"])
        PAR = sb("parameters", PC["width"])
        WORK = 28160
        HB, FSB, FGB = WORK, WORK + 2048, WORK + 3072
        with nc.sbuf_tensor("before_gathered", [P, 8192], F32), nc.sbuf_tensor("gathered", [P, 8192], F32) as GATHERED:
            pass
        with nc.sbuf_tensor("big", [P, WORK], F32) as BIG, nc.sbuf_tensor("tail", [P, 4096], F32) as TAIL:
            pass
        PARTS = sb("parts", WORK, F32R)
        TAIL_PARTS = sb("tail_parts", 4096, F32R)
        H = TAIL[:, 0:KT * TOK]
        FS = TAIL[:, 2048:3072]
        FG = TAIL[:, 3072:4096]
        RS = sb("inverse_rms", TOK)
        LNB = sb("log_mean_square", TOK)
        EPSB = sb("epsilon", 2)
        MOD = sb("modulation", 96)
        NSC = sb("norm_scale", 8)
        SM = sb("small", 1280)
        SMU = sb("small_idx", 32, U32)
        PS = ctx.enter_context(nc.psum_tensor("banks", [P, 8 * 512], F32))
        bank = [PS[:, b * 512:(b + 1) * 512] for b in range(8)]

        def view(t, off, dims, p0=0, pn=P):
            if t is BIG and off >= WORK:
                t, off = TAIL, off - WORK
            a = t if isinstance(t, bass.AP) else t[:, :]
            row = a.ap[0][0]
            return bass.AP(tensor=a.tensor, offset=a.offset + p0 * row + off, ap=[[row, pn]] + dims)

        def con(name, width=128, extra=0, p0=0, pn=P):
            return CON[p0:p0 + pn, CC[name] + extra:CC[name] + extra + width]

        def par(name, width, extra=0, p0=0, pn=P):
            return PAR[p0:p0 + pn, PC[name] + extra:PC[name] + extra + width]

        ident = con("ident")
        ones = con("ones")
        half_ones = con("half_ones")
        upper = con("upper")

        PROJ, CONV, SC = 0, 15360, 21504
        Z_, SBQ, SBK, SBV, GATES = 24 * TOK, 32 * TOK, 36 * TOK, 40 * TOK, 44 * TOK
        SLOT = dict(A=0, B=2048, C=4096, D=SC, E=SC + 2048, F=SC + 4096)
        SQ0 = FSB
        EG, WT, ST = FSB, FGB, HB
        LTS, UBUF = (SLOT["A"], HB), SLOT["D"]
        OD, OSB = SLOT["E"], SLOT["F"]
        ZB, SP, VT = 0, 3072, SLOT["D"]
        GR, YE, YT, SELT, XW, XH, XL = 0, 2048, 4096, 6144, 16384, 22528, 23552
        GD, HN, SEL, SELG, SLOTS = YE, YT, 24576, FSB, 26624
        ZEROS = SEL
        ACC = 0
        GATE, MASK, PLACE, COUNT = 88, 104, 120, 136
        TC, TS, S5P, BBX, BBT, CX, PT1 = 0, 8192, 16384, 18432, 20480, 22528, 25600
        VR, VI, YR, YI, YB = 25600, 26624, BBX, BBX + 1024, S5P

        def rot(k):
            return (TC + (k - 1) * 1024, TS + (k - 1) * 1024, FSB, FGB) if k else (YB, YB + 1024, FSB, FGB)

        KV, W1, SRC, KSQ, KRS, KT2 = 0, 3072, 11264, 13824, 14848, 15872
        KD, VN, BTAB, CB, BT, CP = 16896, 18944, 19968, 20352, 20832, 24928
        GT, KC, VC = 27700, 27800, 27864
        QB, OB, LG, PT, CPT = 0, 2048, 4096, 10240, HB

        def big(off, width, p0=0, pn=P):
            if off >= WORK:
                return TAIL[p0:p0 + pn, off - WORK:off - WORK + width]
            return BIG[p0:p0 + pn, off:off + width]

        def parts(off, width):
            if off >= WORK:
                return TAIL_PARTS[:, off - WORK:off - WORK + width]
            return PARTS[:, off:off + width]

        def w_high(room, n):
            return room[n % 2]

        def h_high(room):
            return room[2]

        ROOM = (18432, 20480, 22528)
        ROOM_MIX = (SLOT["D"], SLOT["E"], SLOT["F"])
        ROOM_S5 = (S5P, BBT, 26112)
        ROOM_KV = (3072, 5120, 7168)
        PROJECTIONS = 30
        SPLITS, SPLIT_BLOCKS = {}, {}
        splits = blocks_before = 0
        for name, count in (("w_in0", 0), ("ffn", BLK1), ("w_in1", 0), ("ffn1_0", BLK2), ("ffn2_0", BLK2), ("ffn1_1", BLK2),
                            ("ffn2_1", BLK2)):
            SPLITS[name], SPLIT_BLOCKS[name] = splits, blocks_before
            splits += 3 * count if count else PROJECTIONS
            blocks_before += count
        INPUTS = {name: i for i, name in enumerate(SPLITS)}

        def unit_role(p):
            return (p % 2, p // 2) if p < 4 else (2, 0) if p == 4 else ((p - 5) % 3, 2 + (p - 5) // 3)

        def slot_high(n):
            return parts(XW + n % 3 * UNIT, UNIT)

        def turned(area, b):
            return parts(area + b % 2 * 512 + TOK, TOK)

        EXPERT_ROUNDS = 3 * BLK1 // RING

        def loop_rounds(blocks):
            return (blocks - 3) // 2

        tab_dram = A["tab"]
        HID = (6 * 512, 7 * 512 + 384)

        steps = {}

        def link(eng, name, ins):
            steps[name] = steps.get(name, 0) + 1
            ins.then_inc(sem(name), 1)
            eng.wait_ge(sem(name), steps[name])

        stage_no = {}

        def stage_end(eng, who):
            stage_no[who] = stage_no.get(who, 0) + 1
            eng.drain().then_inc(sem("stage_done"), 1)
            eng.wait_ge(sem("stage_done"), 4 * stage_no[who])

        stage = ctx.enter_context(nc.Block())

        @stage.sync
        def _(sp):
            sp.dma_start(PAR[:, :], A["par"]).then_inc(sem("inputs"), 16)
            sp.dma_start(CON[:, :], A["con"]).then_inc(sem("inputs"), 16)
            sp.dma_start(X[:, :], A["x"]).then_inc(sem("inputs"), 16)
            for r in range(RING):
                sp.dma_start(ring[r][:, :], A["wall"][r]).then_inc(sem(f"loaded{r}"), 16)
            whole = NUNITS // RING
            with sp.Fori(1, whole) as m:
                for r in range(RING):
                    sp.wait_ge(sem("unit_done"), m * RING + (r + 1 - RING))
                    sp.dma_start(ring[r][:, :], A["wall"][m * RING + r]).then_inc(sem(f"loaded{r}"), 16)
            for n in range(whole * RING, NUNITS):
                sp.wait_ge(sem("unit_done"), n - RING + 1)
                sp.dma_start(ring[n % RING][:, :], A["wall"][n]).then_inc(sem(f"loaded{n % RING}"), 16)
            sp.wait_ge(sem("result"), 1)
            sp.dma_start(A["out"], X[:, :]).then_inc(sem("stored"), 16)
            sp.wait_ge(sem("stored"), 16)

        @stage.tensor
        def _(pe):
            def arrived(n, more=0):
                pe.wait_ge(sem(f"loaded{n % RING}"), more * 16 + 16 * (n // RING + 1))

            def tile(n, k):
                return ring[n % RING][:, k * P:(k + 1) * P]

            def cols_unit(n, dst, kt=KT, tiles=2, src=H, rounds=0, width=TOK, src_off=0):
                arrived(n, rounds)
                for t in range(tiles):
                    for k in range(kt):
                        mm = pe.matmul(dst(t), tile(n, k * tiles + t),
                                       src[:, src_off + k * width:src_off + (k + 1) * width],
                                       start=(k == 0), stop=(k == kt - 1))
                mm.then_inc(sem("unit_done"), 1)

            def half(b, t):
                return bank[b][:, t * TOK:(t + 1) * TOK]

            def norm(i):
                pe.wait_ge(*at("norm_sq", 1, i))
                for t in range(KT):
                    mm = pe.matmul(half(7, 0), ones, big(SQ0 + t * TOK, TOK), start=(t == 0), stop=(t == KT - 1))
                mm.then_inc(sem("norm_sum"), 1)
                pe.wait_ge(*at("normed", 8, i))

            def ada(l):
                with pe.Fori(0, 4) as i:
                    for u in range(RING):
                        n = UN[f"ada{l}"] + u
                        pe.wait_ge(sem("weighted"), i * (RING * KT) + (n + 1) * KT)
                        for t in range(2):
                            for chain in range(2):
                                mm = pe.matmul(PS[:, bass.ds(i * 12 + (l * 48 + 2 * u + t), 1)],
                                               big(ACC + (2 * (u % 2) + chain) * TOK + t * P, P), ones[:, 0:1],
                                               start=(chain == 0), stop=(chain == 1))
                        mm.then_inc(sem("unit_done"), 1)

            def product(o, high, low, in_high, in_low, start, stop, **kw):
                pe.matmul(o, high, in_high, start=start, stop=False, **kw)
                pe.matmul(o, high, in_low, start=False, stop=False, **kw)
                return pe.matmul(o, low, in_high, start=False, stop=stop, **kw)

            def cols_split(n, dst, room):
                for t in range(2):
                    for k in range(KT):
                        c = (k * 2 + t) * P
                        mm = product(dst(t), parts(w_high(room, n) + c, P), ring_low[n % RING][:, c:c + P],
                                     parts(h_high(room) + k * TOK, TOK), parts(HB + k * TOK, TOK), k == 0, k == KT - 1)
                mm.then_inc(sem("unit_done"), 1)

            def project(l):
                for n in range(NT):
                    for k in range(KT):
                        mm = pe.matmul(bank[6][:, n * 16:n * 16 + 16], H[:, k * TOK + n * P:k * TOK + (n + 1) * P],
                                       par("w_ba", 16, l * 128 + k * 16), start=(k == 0), stop=(k == KT - 1))
                mm.then_inc(sem("ba"), 1)
                pe.wait_ge(sem("h_low"), INPUTS[f"w_in{l}"] + 1)
                with pe.Fori(0, PROJECTIONS // RING) as i:
                    for u in range(RING):
                        pe.wait_ge(sem("evac"), l * 30 + i * RING + u + 1)
                        pe.wait_ge(sem("w_low"), i * RING + (SPLITS[f"w_in{l}"] + u + 1))
                        cols_split(UN[f"w_in{l}"] + u, lambda t: half(u, t), ROOM_MIX)

            def qkc(which, h, n):
                return big(CONV + (which * HEADS + h) * TOK + n * P, P)

            def delta(l):
                pe.wait_ge(*at("qk_sq", 1, l, 1))
                pe.wait_ge(*at("beta_exp", 1, l, 1))
                pe.wait_ge(*at("a_abs", 1, l, 1))
                for b in range(8):
                    mm = pe.matmul(bank[b][:, :], ones, big(SLOT["D"] + b * 512, 512), start=True, stop=True)
                mm.then_inc(sem("qk_sum"), 1)
                pe.wait_ge(*at("gu", 1, l, 1))
                pe.wait_ge(*at("qk_normed", 1, l, 1))
                for b in range(4):
                    pe.matmul(bank[b][:, :], ones, big(SLOT["A"] + b * 512, 512), start=True, stop=True)
                pe.matmul(bank[4][:, 0:16], upper, SM[:, 64:80], start=True, stop=True)
                pe.matmul(bank[4][:, 16:32], ones, SM[:, 64:80], start=True, stop=True).then_inc(sem("cum"), 1)
                stage_end(pe, "pe")
                for which in (1, 0):
                    for n in range(NT):
                        for h in range(HEADS):
                            b = 4 * (1 - which) + n * 2 + h // 4
                            mm = pe.matmul(bank[b][:, (h % 4) * P:(h % 4 + 1) * P], qkc(1, h, n), qkc(which, h, n),
                                           start=True, stop=True)
                    mm.then_inc(sem("kk"), 1)
                pe.wait_ge(*at("lmat", 1, l, 1))
                for c in range(16):
                    mm = pe.transpose(bank[c // 4][:, (c % 4) * P:(c % 4 + 1) * P], big(SLOT["D"] + c * P, P), ident)
                mm.then_inc(sem("lt"), 1)
                stage_end(pe, "pe")
                for s in range(6):
                    for q in range(4):
                        pe.wait_ge(*at("level_mask", 4 * s + q + 1, l, 24))
                        if s:
                            pe.wait_ge(*at("level_t", 4 * (s - 1) + q + 1, l, 24))
                        for c in range(4):
                            x = (4 * q + c) * P
                            mm = pe.matmul(bank[q][:, c * P:(c + 1) * P], big(LTS[s % 2] + x, P), big(SLOT["E"] + x, P),
                                           start=True, stop=True)
                        mm.then_inc(sem("level_u"), 1)
                    for q in range(4):
                        pe.wait_ge(*at("level_uc", 4 * s + q + 1, l, 24))
                        if 4 * s + q >= 2:
                            pe.wait_ge(*at("level_t", 4 * s + q - 1, l, 24))
                        for c in range(4):
                            x = (4 * q + c) * P
                            pe.matmul(bank[4 + q % 2][:, c * P:(c + 1) * P], big(SLOT["F"] + x, P), big(UBUF + x, P),
                                      start=True, stop=True)
                            mm = pe.matmul(bank[6 + q % 2][:, c * P:(c + 1) * P], big(UBUF + x, P),
                                           big(SLOT["F"] + x, P), start=True, stop=True)
                        mm.then_inc(sem("level_p"), 1)
                stage_end(pe, "pe")
                for which in (1, 2):
                    for n in range(NT):
                        for h in range(HEADS):
                            b = 4 * (which - 1) + n * 2 + h // 4
                            mm = pe.transpose(bank[b][:, (h % 4) * P:(h % 4 + 1) * P], qkc(which, h, n), ident)
                mm.then_inc(sem("kvt"), 1)
                stage_end(pe, "pe")
                for h in range(HEADS):
                    pe.matmul(bank[h // 4][:, (h % 4) * P:(h % 4 + 1) * P], big(SLOT["F"] + h * P, P),
                              big(SLOT["D"] + h * P, P), start=True, stop=True)
                for h in range(HEADS):
                    mm = pe.matmul(bank[2 + h // 4][:, (h % 4) * P:(h % 4 + 1) * P], big(SLOT["C"] + (8 + h) * P, P),
                                   big(SLOT["F"] + (8 + h) * P, P), start=True, stop=True)
                mm.then_inc(sem("vnew_ps"), 1)
                pe.wait_ge(*at("vnew0", 1, l, 1))
                for h in range(HEADS):
                    mm = pe.matmul(bank[4 + h // 4][:, (h % 4) * P:(h % 4 + 1) * P], big(SLOT["C"] + h * P, P),
                                   big(SLOT["A"] + h * P, P), start=True, stop=True)
                mm.then_inc(sem("state_ps"), 1)
                pe.wait_ge(*at("state", 1, l, 1))
                pe.wait_ge(*at("w_neg", 1, l, 1))
                for h in range(HEADS):
                    o = bank[6 + h // 4][:, (h % 4) * P:(h % 4 + 1) * P]
                    pe.matmul(o, big(SLOT["F"] + (8 + h) * P, P), big(SLOT["D"] + (8 + h) * P, P), start=True, stop=False)
                    mm = pe.matmul(o, big(WT + h * P, P), big(ST + h * P, P), start=False, stop=True)
                mm.then_inc(sem("vnew_ps1"), 1)
                pe.wait_ge(*at("vnew1", 1, l, 1))
                pe.wait_ge(*at("q_dec", 1, l, 1))
                for h in range(HEADS):
                    o = bank[h // 2]
                    c = (h % 2) * TOK
                    pe.matmul(o[:, c:c + P], big(SLOT["A"] + h * P, P), big(SLOT["B"] + h * P, P), start=True, stop=True)
                    pe.matmul(o[:, c + P:c + 2 * P], big(ST + h * P, P), qkc(0, h, 1), start=True, stop=False)
                    mm = pe.matmul(o[:, c + P:c + 2 * P], big(SLOT["A"] + (8 + h) * P, P), big(SLOT["B"] + (8 + h) * P, P),
                                   start=False, stop=True)
                mm.then_inc(sem("o_ps"), 1)
                pe.wait_ge(*at("o_sq", 1, l, 1))
                for b in range(4):
                    mm = pe.matmul(bank[4 + b][:, :], ones, big(SLOT["E"] + b * 512, 512), start=True, stop=True)
                mm.then_inc(sem("o_sum"), 1)
                stage_end(pe, "pe")

            def stick(l):
                for h in range(HEADS):
                    p0 = 64 * (h % 2)
                    j = (h // 2) * TOK
                    q = BIG[p0:p0 + 64, SBQ + j:SBQ + j + TOK]
                    pe.matmul(bank[h][:, 0:TOK], BIG[p0:p0 + 64, SBK + j:SBK + j + P], q, start=True, stop=True)
                    mm = pe.matmul(bank[h][:, TOK:TOK + P], BIG[p0:p0 + 64, SBK + j + P:SBK + j + 2 * P],
                                   BIG[p0:p0 + 64, SBQ + j + P:SBQ + j + 2 * P], start=True, stop=True)
                mm.then_inc(sem("z_ps"), 1)
                pe.wait_ge(*at("z_out", 8, l, 8))
                for n in range(NT):
                    for j in range(4):
                        mm = pe.transpose(bank[n][:, j * P:(j + 1) * P], big(SBV + j * TOK + n * P, P), ident)
                mm.then_inc(sem("vt_ps"), 1)
                pe.wait_ge(*at("vt_out", 1, l, 1))
                pe.wait_ge(*at("sp_out", 1, l, 1))
                for h in range(HEADS):
                    s0 = SP + h * 384
                    pe.matmul(bank[h][:, 0:TOK], con("key_after"), big(s0, TOK), start=True, stop=False)
                    pe.matmul(bank[h][:, P:TOK], ones, big(s0 + TOK, P), start=False, stop=True)
                    mm = pe.matmul(bank[h][:, TOK:TOK + P], con("key_after"), big(s0 + TOK, P), start=True, stop=True)
                mm.then_inc(sem("rem_ps"), 1)
                pe.wait_ge(*at("stick_p", 1, l, 1))
                for h in range(HEADS):
                    p0 = 64 * (h % 2)
                    o = bank[h // 4][p0:p0 + 64, ((h // 2) % 2) * TOK:((h // 2) % 2 + 1) * TOK]
                    pe.matmul(o, big(VT + h * 64, 64), big(ZB + h * 384, TOK), start=True, stop=False)
                    mm = pe.matmul(bank[h // 4][p0:p0 + 64, ((h // 2) % 2) * TOK + P:((h // 2) % 2 + 1) * TOK],
                                   big(VT + 512 + h * 64, 64), big(ZB + h * 384 + TOK, P), start=False, stop=True)
                mm.then_inc(sem("stick_ps"), 1)
                stage_end(pe, "pe")

            def combine(l):
                n = UN[f"up{l}"]
                for u in range(4):
                    cols_unit(n + u, lambda t: half(u, t), src=BIG, src_off=OD)
                for u in range(2):
                    cols_unit(n + 4 + u, lambda t: half(4 + 2 * u + t // 2, t % 2), kt=4, tiles=4, src=BIG, src_off=OSB)
                pe.wait_ge(*at("mixed", 1, l, 1))
                n = UN[f"w_out{l}"]
                for u in range(4):
                    cols_unit(n + u, lambda t: half(u, t), src=BIG, src_off=SLOT["D"])
                stage_end(pe, "pe")

            def up(n, par2, rounds=0):
                cols_unit(n, lambda t: half(2 * par2, t), rounds=rounds)
                cols_unit(n + 1, lambda t: half(2 * par2 + 1, t), rounds=rounds)

            def down(n, par2, first=False, rounds=0):
                arrived(n, rounds)
                for f in range(2):
                    for o in range(KT):
                        mm = pe.matmul(half(4 + o // 2, o % 2), ring[n % RING][:, (f * KT + o) * P:(f * KT + o + 1) * P],
                                       FG[:, par2 * 512 + f * TOK:par2 * 512 + (f + 1) * TOK],
                                       start=(first and f == 0 and o % 2 == 0), stop=True, skip_group_check=True)
                mm.then_inc(sem("unit_done"), 1)

            def ffn_slots(n, blocks, base, e):
                def turn(b, i):
                    pe.wait_ge(sem("gated"), i * 2 + (base + b + 1))
                    for f in range(2):
                        mm = pe.transpose(bank[6 + b % 2][:, f * P:(f + 1) * P],
                                          FG[:, b % 2 * 512 + f * P:b % 2 * 512 + (f + 1) * P], ident)
                    mm.then_inc(sem("x_turned"), 1)

                def step(p, i):
                    which, b = unit_role(p)
                    if p == 3 * blocks - 1:
                        which, b = 2, blocks - 1
                        turn(b, i)
                    elif which == 2 and p > 4:
                        b = b - 1
                    r = (n + p) % RING
                    high = slot_high(n + p)
                    pe.wait_ge(sem("x_low"), i * RING + (p + 1))
                    if which < 2:
                        if b > 1:
                            pe.wait_ge(sem("gated"), i * 2 + (base + b - 1))
                        for k in range(KT):
                            mm = product(bank[2 * (b % 2) + which][:, 0:TOK], parts(XH + k * P, P), parts(XL + k * P, P),
                                         high[:, k * TOK:(k + 1) * TOK], ring_low[r][:, k * TOK:(k + 1) * TOK],
                                         k == 0, k == KT - 1)
                        mm.then_inc(sem("unit_done"), 1)
                        if which == 0 and b:
                            turn(b - 1, i)
                    else:
                        pe.wait_ge(sem("x_turned_low"), i * 2 + (b + 1))
                        if p == 4:
                            pe.wait_ge(sem("expert_out"), e + 1)
                        for f in range(2):
                            for c in range(2):
                                w = slice(f * 1024 + c * 512, f * 1024 + (c + 1) * 512)
                                mm = product(bank[4 + c][:, :], turned(FSB, b)[:, f * P:(f + 1) * P],
                                             turned(FGB, b)[:, f * P:(f + 1) * P], high[:, w], ring_low[r][:, w],
                                             p == 4 and f == 0, True, skip_group_check=True)
                        mm.then_inc(sem("unit_done"), 1)

                pe.wait_ge(sem("xh_low"), e + 1)
                for p in range(5):
                    step(p, e * EXPERT_ROUNDS)
                with pe.Fori(0, loop_rounds(blocks)) as i:
                    for p in range(5, 11):
                        step(p, i + e * EXPERT_ROUNDS)
                for p in range(5 + 6 * loop_rounds(blocks), 3 * blocks):
                    step(p, e * EXPERT_ROUNDS)

            def ffn_split(name, blocks, base, room):
                n, sp0, b0 = UN[name], SPLITS[name], SPLIT_BLOCKS[name]

                def step(p, i=0):
                    which, b = unit_role(p)
                    if p == 3 * blocks - 1:
                        which, b = 2, blocks - 1
                    elif which == 2 and p > 4:
                        b = b - 1
                    r = (n + p) % RING
                    pe.wait_ge(sem("w_low"), i * RING + (sp0 + p + 1))
                    if which < 2:
                        if b > 1:
                            pe.wait_ge(sem("gated"), i * 2 + (base + b - 1))
                        cols_split(n + p, lambda t: half(2 * (b % 2) + which, t), room)
                    else:
                        pe.wait_ge(sem("g_low"), i * 2 + (b0 + b + 1))
                        for f in range(2):
                            for o in range(KT):
                                c = (f * KT + o) * P
                                g = (b % 2) * 512 + f * TOK
                                mm = product(half(4 + o // 2, o % 2), parts(w_high(room, n + p) + c, P),
                                             ring_low[r][:, c:c + P], parts(FSB + g, TOK), parts(FGB + g, TOK),
                                             p == 4 and f == 0 and o % 2 == 0, True, skip_group_check=True)
                        mm.then_inc(sem("unit_done"), 1)

                pe.wait_ge(sem("h_low"), INPUTS[name] + 1)
                for p in range(5):
                    step(p)
                with pe.Fori(0, loop_rounds(blocks)) as i:
                    for p in range(5, 11):
                        step(p, i)
                for p in range(5 + 6 * loop_rounds(blocks), 3 * blocks):
                    step(p)

            def ffn(n, blocks, base, expert=None):
                e_units = 0 if expert is None else expert * (3 * blocks // RING)
                b0 = base if expert is None else expert * blocks + base
                e2 = expert

                def gated(count):
                    if isinstance(count, int) and count <= 0:
                        return
                    pe.wait_ge(sem("gated"), count)

                gated(b0)
                up(n, 0, e_units)
                up(n + 2, 1, e_units)
                gated(b0 + 1)
                if expert is not None:
                    pe.wait_ge(sem("expert_out"), e2 + 1)
                down(n + 4, 0, True, e_units)
                steps_left = blocks - 2
                with pe.Fori(0, steps_left // 2) as i:
                    r = i + e_units
                    for half_step in range(2):
                        m = n + 5 + 3 * half_step
                        gated(i * 2 + (b0 + 1 + half_step))
                        up(m, half_step, r)
                        gated(i * 2 + (b0 + 2 + half_step))
                        down(m + 2, 1 - half_step, False, r)
                done = steps_left // 2 * 2
                m = n + 5 + 3 * done
                if steps_left % 2:
                    gated(b0 + 1 + done)
                    up(m, 0, e_units)
                    gated(b0 + 2 + done)
                    down(m + 2, 1, False, e_units)
                    m += 3
                gated(b0 + blocks)
                down(m, (blocks - 1) % 2, False, e_units)
                assert m + 1 == n + 3 * blocks

            pe.wait_ge(sem("inputs"), 48)
            ada(0)
            ada(1)
            stage_end(pe, "pe")
            norms = 0
            for l in range(LAYERS):
                norm(norms)
                norms += 1
                project(l)
                stage_end(pe, "pe")
                delta(l)
                stick(l)
                combine(l)
                norm(norms)
                norms += 1
                if l == 0:
                    ffn_split("ffn", BLK1, 0, ROOM)
                    stage_end(pe, "pe")
                    continue
                for n in range(NT):
                    for k in range(KT):
                        mm = pe.transpose(bank[4 + 2 * n + k // 4][:, (k % 4) * P:(k % 4 + 1) * P],
                                          H[:, k * TOK + n * P:k * TOK + (n + 1) * P], ident)
                mm.then_inc(sem("hn_ps"), 1)
                for n in range(NT):
                    for k in range(KT):
                        mm = pe.matmul(bank[0][:, n * 8:n * 8 + 8], H[:, k * TOK + n * P:k * TOK + (n + 1) * P],
                                       par("router_w", 8, k * 8), start=(k == 0), stop=(k == KT - 1))
                mm.then_inc(sem("logits"), 1)
                pe.wait_ge(sem("hn_out"), 1)
                pe.wait_ge(sem("masks"), 1)
                pe.matmul(bank[5][:, 0:8], upper, SM[:, MASK:MASK + 8], start=True, stop=True)
                pe.matmul(bank[5][:, 8:16], ones, SM[:, MASK:MASK + 8], start=True, stop=False)
                pe.matmul(bank[5][:, 8:16], upper, SM[:, MASK + 8:MASK + 16], start=False, stop=True)
                for n in range(NT):
                    pe.matmul(bank[5][:, 16:24], ones, SM[:, MASK + 8 * n:MASK + 8 * n + 8], start=(n == 0), stop=(n == NT - 1))
                pe.matmul(bank[5][:, 128:256], ones, upper, start=True, stop=True).then_inc(sem("places"), 1)
                for half_e in range(2):
                    pe.wait_ge(sem("gate_diag"), half_e + 1)
                    for b in range(2):
                        mm = pe.matmul(bank[1 + 2 * half_e + b][:, :], ones, big(GD + half_e * 1024 + b * 512, 512), start=True, stop=True)
                    mm.then_inc(sem("gate_ps"), 1)
                stage_end(pe, "pe")
                for c in range(16):
                    mm = pe.transpose(bank[c // 4][:, (c % 4) * P:(c % 4 + 1) * P], big(SELG + c * P, P), ident)
                mm.then_inc(sem("selt_ps"), 1)
                with pe.Fori(0, EXPERTS // 2) as i:
                    for j in range(2):
                        pe.wait_ge(sem("gather_low"), i * 2 + (j + 1))
                        pe.wait_ge(sem("gather_high"), i * 2 + (j + 1))
                        for k in range(KT):
                            for n in range(NT):
                                mm = pe.matmul(bank[4 + 2 * j + k // 4][:, (k % 4) * P:(k % 4 + 1) * P],
                                               big(HN + n * 1024 + k * P, P), BIG[:, bass.ds(i * 512 + (SEL + j * 256 + n * P), P)],
                                               start=(n == 0), stop=(n == NT - 1))
                        mm.then_inc(sem("gather_ps"), 1)
                stage_end(pe, "pe")
                with pe.Fori(0, EXPERTS) as e:
                    count = pe.value_load(SMU[0:1, bass.ds(e + 16, 1)], min_val=0, max_val=TOK)
                    with pe.If(count <= P):
                        ffn_slots(UN["moe"], BLK1, BLK1, e)
                    with pe.Else():
                        ffn(UN["moe"], BLK1, BLK1, e)
                        pe.nop().then_inc(sem("x_turned"), BLK1)
                stage_end(pe, "pe")
                for t in range(KT):
                    for e in range(EXPERTS):
                        mm = pe.matmul(half(t // 2, t % 2), GATHERED[:, e * 1024 + t * P:e * 1024 + (t + 1) * P], big(SELT + e * TOK, TOK),
                                       start=(e == 0), stop=(e == EXPERTS - 1))
                    if t % 2:
                        mm.then_inc(sem("scatter"), 1)
                stage_end(pe, "pe")
            norm(norms)
            stage_end(pe, "pe")
            norms += 1
            done_blocks = BLK1 * (1 + EXPERTS)

            def ffn2(name):
                nonlocal norms, done_blocks
                norm(norms)
                norms += 1
                ffn_split(name, BLK2, done_blocks, {"ffn1_0": ROOM_S5, "ffn1_1": ROOM_KV}.get(name, ROOM))
                done_blocks += BLK2
                if name != "ffn2_1":
                    stage_end(pe, "pe")

            ffn2("ffn1_0")
            norm(norms)
            norms += 1
            pe.wait_ge(sem("bb"), 1)
            for i in range(2):
                for k in range(KT):
                    mm = pe.transpose(bank[4 * i + k // 4][:, (k % 4) * P:(k % 4 + 1) * P], big(BBX + i * 1024 + k * P, P), ident)
            mm.then_inc(sem("bt_ps"), 1)
            pe.wait_ge(sem("bt"), 1)
            for k in range(KT + 2):
                if k < KT:
                    if k:
                        pe.wait_ge(sem("bu_read"), k)
                    for i in range(2):
                        for j in range(4):
                            mm = pe.matmul(half(j, i), BIG[32 * j:32 * j + 32, BBT + i * 1024 + k * P:BBT + i * 1024 + (k + 1) * P],
                                           H[32 * j:32 * j + 32, k * TOK:(k + 1) * TOK], start=True, stop=True)
                    mm.then_inc(sem("bu"), 1)
                if k > 1:
                    kk = k - 2
                    pe.wait_ge(sem("rotated"), kk + 1)
                    if kk > 1:
                        pe.wait_ge(sem("y_out"), kk - 1)
                    for j in range(4):
                        pr = 4 * kk + j
                        for q, c in enumerate((0, 1, 2, 2)):
                            mm = pe.matmul(bank[4 + kk % 2][32 * j:32 * j + 32, 0:TOK], big(CX + c * 1024 + pr * 32, 32),
                                           big(rot(kk)[q] + j * TOK, TOK), start=(q == 0), stop=(q == 3))
                    mm.then_inc(sem("y_ps"), 1)
            pe.wait_ge(sem("y_gelu"), 1)
            stage_end(pe, "pe")
            for u in range(4):
                cols_unit(UN["glu"] + u, lambda t: half(u, t), src=BIG, src_off=YB)
            stage_end(pe, "pe")
            ffn2("ffn2_0")
            norm(norms)
            norms += 1
            for u in range(6):
                cols_unit(UN["kv"] + u, lambda t: half(u, t))
            stage_end(pe, "pe")
            pe.wait_ge(sem("kv_sq"), 1)
            for i in range(2):
                mm = pe.matmul(bank[i][:, :], half_ones, big(KSQ + i * 512, 512), start=True, stop=True)
            mm.then_inc(sem("kv_sum"), 1)
            for i, t0 in enumerate((6, 10)):
                for n in range(NT):
                    for m in range(2):
                        mm = pe.transpose(bank[2 + i][:, (n * 2 + m) * P:(n * 2 + m + 1) * P],
                                          big(KV + (t0 + m) * TOK + n * P, P), ident)
            mm.then_inc(sem("kv_vt"), 1)
            pe.matmul(bank[4][0:QH, 0:256], par("rel_bias", 16, pn=32), con("onehot", 256, 255, pn=32), start=True, stop=True)
            for n in range(NT):
                for c in range(NCMP):
                    x = 255 + n * P - 16 * c - 31
                    mm = pe.matmul(bank[5][:, (n * NCMP + c) * QH:(n * NCMP + c + 1) * QH], con("onehot", P, x, pn=32),
                                   par("rel_bias", 16, pn=32), start=True, stop=True)
            mm.then_inc(sem("bias_ps"), 1)
            pe.wait_ge(sem("w1_here"), 32)
            pe.wait_ge(sem("cmp_src"), 1)
            for i in range(2):
                for hf in range(2):
                    for s in range(32):
                        off = SRC + i * 1024 + (s // 16) * 512
                        mm = pe.matmul(PS[:, HID[hf] + i * 2 * NCMP:HID[hf] + (i + 1) * 2 * NCMP],
                                       BIG[64 * hf:64 * hf + 64, W1 + i * 4096 + s * P:W1 + i * 4096 + (s + 1) * P],
                                       view(BIG, off + s, [[TOK, 2], [16, NCMP]], 64 * hf, 64),
                                       start=(s == 0), stop=(s == 31))
            mm.then_inc(sem("hid_ps"), 1)
            pe.wait_ge(sem("hid"), 1)
            pe.matmul(bank[7][:, 0:4 * NCMP], par("w2_k", 128), SM[:, 0:4 * NCMP], start=True, stop=True)
            for g in range(4):
                x = (2 + g % 2) * 2 * NCMP + (g // 2) * NCMP
                mm = pe.matmul(bank[7][0:NCMP, 128 + g * 64:128 + (g + 1) * 64], SM[:, x:x + NCMP], par("w2_v", 64),
                               start=True, stop=True)
            mm.then_inc(sem("cmp_ps"), 1)
            pe.wait_ge(sem("kc_sq"), 1)
            pe.matmul(bank[7][:, 64:64 + 4 * NCMP], half_ones, SM[:, 128:128 + 4 * NCMP], start=True, stop=True)\
                .then_inc(sem("kc_sum"), 1)
            stage_end(pe, "pe")
            ffn2("ffn1_1")
            norm(norms)
            norms += 1
            for u in range(4):
                cols_unit(UN["q"] + u, lambda t: half(u, t))
            for n in range(NT):
                for k in range(KT):
                    mm = pe.matmul(bank[4][:, n * 48:n * 48 + 48], H[:, k * TOK + n * P:k * TOK + (n + 1) * P],
                                   par("w_gate", 48, k * 48), start=(k == 0), stop=(k == KT - 1))
            mm.then_inc(sem("gate_logits"), 1)
            stage_end(pe, "pe")
            pe.wait_ge(sem("q_sq"), 1)
            for b in range(4):
                mm = pe.matmul(bank[b][:, :], half_ones, big(PT + b * 512, 512), start=True, stop=True)
            mm.then_inc(sem("q_sum"), 1)
            stage_end(pe, "pe")

            def qhead(h, n):
                p0 = 64 * (h % 2)
                return BIG[p0:p0 + 64, QB + (h // 2) * TOK + n * P:QB + (h // 2) * TOK + (n + 1) * P]

            for n in range(NT):
                for h in range(QH):
                    g = h // 4
                    p0 = 64 * (h % 2)
                    mm = pe.matmul(bank[h % 2][:, (n * QH + h) * NCMP:(n * QH + h + 1) * NCMP], qhead(h, n),
                                   BIG[p0:p0 + 64, KC + g * NCMP:KC + (g + 1) * NCMP], start=True, stop=True)
            mm.then_inc(sem("cmp_logits"), 1)
            pe.wait_ge(sem("cmp_p"), 1)
            stage_end(pe, "pe")
            for h in range(QH):
                for n in range(NT):
                    mm = pe.transpose(bank[h // 2][0:NCMP, (h % 2) * TOK + n * P:(h % 2) * TOK + (n + 1) * P],
                                      big(CP + (n * QH + h) * NCMP, NCMP), ident)
            mm.then_inc(sem("cmp_pt"), 1)
            stage_end(pe, "pe")
            for br in range(2):
                for h in range(QH):
                    g = h // 4
                    p0 = 64 * (h % 2)
                    b = bank[h % 8]
                    if h >= 8:
                        pe.wait_ge(sem("logits_out"), br * 16 + h - 7)
                    kk = KD + br * 1024 + g * TOK
                    pe.matmul(b[:, 0:P], qhead(h, 0), BIG[p0:p0 + 64, kk:kk + P], start=True, stop=True)
                    pe.matmul(b[:, P:3 * P], qhead(h, 1), BIG[p0:p0 + 64, kk:kk + TOK], start=True, stop=True)\
                        .then_inc(sem("logits_ps"), 1)
                pe.wait_ge(sem("probs"), br + 1)
                for h in range(QH):
                    b = bank[h % 8]
                    if h >= 8:
                        pe.wait_ge(sem("pt_out"), br * 16 + h - 7)
                    for i in range(3):
                        mm = pe.transpose(b[:, i * P:(i + 1) * P], big(LG + h * 384 + i * P, P), ident)
                    mm.then_inc(sem("pt_ps"), 1)
                pe.wait_ge(sem("pt_out"), br * 16 + 16)
                for h in range(QH):
                    g = h // 4
                    p0 = 64 * (h % 2)
                    o = bank[h // 4][p0:p0 + 64, (h // 2 % 2) * TOK:(h // 2 % 2 + 1) * TOK]
                    o1 = bank[h // 4][p0:p0 + 64, (h // 2 % 2) * TOK + P:(h // 2 % 2 + 1) * TOK]
                    pe.matmul(o, big(VN + br * 512 + g * 64, 64), big(PT + h * 384, TOK), start=True, stop=False)
                    if br == 0:
                        pe.matmul(o, BIG[0:NCMP, VC + g * 64:VC + (g + 1) * 64], big(CPT + h * TOK, TOK, 0, NCMP),
                                  start=False, stop=False)
                    mm = pe.matmul(o1, big(VN + br * 512 + 256 + g * 64, 64), big(PT + h * 384 + TOK, P), start=False, stop=True)
                mm.then_inc(sem("o_branch"), 1)
                stage_end(pe, "pe")
            for u in range(4):
                cols_unit(UN["w_o"] + u, lambda t: half(u, t), src=BIG, src_off=OB)
            stage_end(pe, "pe")
            ffn2("ffn2_1")

        @stage.vector
        def _(ve):
            def lk(ins):
                link(ve, "vector_step", ins)

            def tt(out, a, b, op):
                return ve.tensor_tensor(out, a, b, op)

            def norm_v(i, scale_off, shift, dst=None, split=None, room=ROOM):
                dst = H if dst is None else dst
                tt(big(SQ0, 2048), X[:, :], X[:, :], ALU.mult).then_inc(sem("norm_sq"), 1)
                if split is not None:
                    w_low(UN[split], SPLITS[split] + 1, room)
                ve.wait_ge(*at("norm_rs", 1, i))
                for t in range(KT):
                    w = NSC[:, t:t + 1] if scale_off is None else par(scale_off[0], 1, scale_off[1] + t)
                    ve.scalar_tensor_tensor(dst[:, t * TOK:(t + 1) * TOK], X[:, t * TOK:(t + 1) * TOK], w, RS[:, :],
                                            ALU.mult, ALU.mult).then_inc(sem("norm_scaled" if shift else "normed"), 1)

            def w_low(n, count, room, i=0):
                ve.wait_ge(sem("w_high"), i * RING + count)
                r = n % RING
                tt(ring_low[r][:, :], ring[r][:, :], parts(w_high(room, n), UNIT).bitcast(F32), ALU.subtract)\
                    .then_inc(sem("w_low"), 1)

            def h_low(name, room):
                ve.wait_ge(sem("h_high"), INPUTS[name] + 1)
                tt(parts(HB, 2048), H, parts(h_high(room), 2048).bitcast(F32), ALU.subtract).then_inc(sem("h_low"), 1)
                w_low(UN[name] + 1, SPLITS[name] + 2, room)

            def ffn_split_v(name, blocks, base, room):
                n, sp0, b0 = UN[name], SPLITS[name], SPLIT_BLOCKS[name]

                def step(p, i=0):
                    which, b = unit_role(p)
                    g = (b % 2) * 512
                    if which == 1:
                        ve.wait_ge(sem("silu"), i * 2 + (base + b + 1))
                        ve.wait_ge(sem("unit_done"), i * RING + (n + p + 1))
                        tt(FG[:, g:g + 512], FS[:, g:g + 512], bank[2 * (b % 2) + 1][:, :], ALU.mult)\
                            .then_inc(sem("gated"), 1)
                    if p + 2 < 3 * blocks:
                        w_low(n + p + 2, sp0 + p + 3, room, i)
                    if which == 1:
                        ve.wait_ge(sem("g_high"), i * 2 + (b0 + b + 1))
                        tt(parts(FGB + g, 512), FG[:, g:g + 512], parts(FSB + g, 512).bitcast(F32), ALU.subtract)\
                            .then_inc(sem("g_low"), 1)

                h_low(name, room)
                for p in range(5):
                    step(p)
                with ve.Fori(0, loop_rounds(blocks)) as i:
                    for p in range(5, 11):
                        step(p, i)
                for p in range(5 + 6 * loop_rounds(blocks), 3 * blocks - 1):
                    step(p)

            def ffn_slots_v(n, blocks, base, e):
                def x_low(p, i):
                    ve.wait_ge(sem("x_high"), i * RING + (p + 1))
                    r = (n + p) % RING
                    tt(ring_low[r][:, :], ring[r][:, :], slot_high(n + p).bitcast(F32), ALU.subtract).then_inc(sem("x_low"), 1)

                def turned_low(b, i):
                    ve.wait_ge(sem("x_turned_high"), i * 2 + (b + 1))
                    tt(turned(FGB, b), bank[6 + b % 2][:, 0:TOK], turned(FSB, b).bitcast(F32), ALU.subtract)\
                        .then_inc(sem("x_turned_low"), 1)

                def step(p, i):
                    which, b = unit_role(p)
                    if which == 0 and b:
                        turned_low(b - 1, i)
                    if p + 3 < 3 * blocks:
                        x_low(p + 3, i)
                    if which == 1:
                        g = (b % 2) * 512
                        ve.wait_ge(sem("silu"), i * 2 + (base + b + 1))
                        ve.wait_ge(sem("unit_done"), i * RING + (n + p + 1))
                        tt(FG[:, g:g + TOK], FS[:, g:g + TOK], bank[2 * (b % 2) + 1][:, 0:TOK], ALU.mult)\
                            .then_inc(sem("gated"), 1)

                ve.wait_ge(sem("xh_high"), e + 1)
                tt(parts(XL, 1024), GATHERED[:, bass.ds(e * 1024, 1024)], parts(XH, 1024).bitcast(F32), ALU.subtract)\
                    .then_inc(sem("xh_low"), 1)
                for p in range(3):
                    x_low(p, e * EXPERT_ROUNDS)
                for p in range(5):
                    step(p, e * EXPERT_ROUNDS)
                with ve.Fori(0, loop_rounds(blocks)) as i:
                    for p in range(5, 11):
                        step(p, i + e * EXPERT_ROUNDS)
                for p in range(5 + 6 * loop_rounds(blocks), 3 * blocks - 1):
                    step(p, e * EXPERT_ROUNDS)
                turned_low(blocks - 1, e * EXPERT_ROUNDS)
                ve.wait_ge(sem("unit_done"), e * (3 * BLK1) + (n + 3 * BLK1))
                ve.tensor_scalar(GATHERED[:, bass.ds(e * 1024, 512)], bank[4][:, :], 1.0, None, ALU.mult)
                ve.tensor_scalar(GATHERED[:, bass.ds(e * 1024 + 512, 512)], bank[5][:, :], 1.0, None, ALU.mult)\
                    .then_inc(sem("expert_out"), 1)

            def ffn_loop(blocks, base, units0, expert=None):
                b0 = base if expert is None else expert * blocks + base
                u0 = units0 if expert is None else expert * (3 * blocks) + units0

                def gate(par2, count, units):
                    ve.wait_ge(sem("silu"), count + 1)
                    ve.wait_ge(sem("unit_done"), units)
                    tt(FG[:, par2 * 512:(par2 + 1) * 512], FS[:, par2 * 512:(par2 + 1) * 512],
                       bank[2 * par2 + 1][:, :], ALU.mult).then_inc(sem("gated"), 1)

                gate(0, b0, u0 + 2)
                gate(1, b0 + 1, u0 + 4)
                steps_left = blocks - 2
                with ve.Fori(0, steps_left // 2) as i:
                    for hs in range(2):
                        gate(hs, i * 2 + (b0 + 2 + hs), i * 6 + (u0 + 7 + 3 * hs))
                done = steps_left // 2 * 2
                if steps_left % 2:
                    gate(0, b0 + 2 + done, u0 + 7 + 3 * done)

            ve.wait_ge(sem("inputs"), 48)
            ve.wait_ge(sem("c_act"), 1)

            def weigh(u, done, rounds):
                ve.wait_ge(sem(f"loaded{u}"), rounds * 16 + 16 * (done // RING + 1))
                if not (isinstance(rounds, int) and done < 2):
                    ve.wait_ge(sem("unit_done"), rounds * RING + (done - 1))
                for k in range(KT):
                    acc = big(ACC + (2 * (u % 2) + k % 2) * TOK, TOK)
                    w = ring[u][:, k * TOK:(k + 1) * TOK]
                    if k < 2:
                        ve.tensor_scalar(acc, w, SM[:, k:k + 1], None, ALU.mult).then_inc(sem("weighted"), 1)
                    else:
                        ve.wait_ge(sem("weighted"), rounds * (RING * KT) + (done * KT + k - 1))
                        ve.scalar_tensor_tensor(acc, w, SM[:, k:k + 1], acc, ALU.mult, ALU.add).then_inc(sem("weighted"), 1)

            for u in range(RING):
                weigh(u, u, 0)
            with ve.Fori(0, 7) as i:
                for u in range(RING):
                    weigh(u, RING + u, i)
            ve.wait_ge(sem("unit_done"), UN["ada1"] + 24)
            lk(ve.tensor_tensor(MOD[:, :], PS[:, 0:96], par("ada_b", 96), ALU.add))
            stage_end(ve, "ve")
            norms = 0

            def mod(l, part, t=0, w=8):
                return MOD[:, l * 48 + part * 8 + t:l * 48 + part * 8 + t + w]

            for l in range(LAYERS):
                lk(ve.scalar_tensor_tensor(NSC[:, :], mod(l, 1), 1.0, par("norm_mix", 8, l * 8), ALU.add, ALU.mult))
                name = f"w_in{l}"
                norm_v(norms, None, True, split=name, room=ROOM_MIX)
                norms += 1
                ve.wait_ge(*at("ba", 1, l, 1))
                h_low(name, ROOM_MIX)
                for p in range(2, 8):
                    w_low(UN[name] + p, SPLITS[name] + p + 1, ROOM_MIX)

                def tap(i, j):
                    if j == 0:
                        ve.wait_ge(sem("evac"), i * 4 + (l * 30 + 6 + 4))
                    else:
                        ve.wait_ge(sem("conv_tap"), i * 4 + (l * 12 + j))
                    for t in range(KT):
                        x0 = i * 2048 + (PROJ + t * TOK)
                        y0 = i * 2048 + (CONV + t * TOK)
                        wj = PAR[:, bass.ds(i * 32 + (PC["conv_w"] + l * 96 + t * 4 + 3 - j), 1)]
                        if j == 0:
                            ins = ve.tensor_scalar(BIG[:, bass.ds(y0, TOK)], BIG[:, bass.ds(x0, TOK)], wj, None, ALU.mult)
                        else:
                            ins = ve.scalar_tensor_tensor(BIG[:, bass.ds(y0 + j, TOK - j)], BIG[:, bass.ds(x0, TOK - j)], wj,
                                                          BIG[:, bass.ds(y0 + j, TOK - j)], ALU.mult, ALU.add)
                    ins.then_inc(sem("conv_tap"), 1)

                with ve.Fori(0, 3) as i:
                    for u in range(RING):
                        w_low(UN[name] + 8 + u, SPLITS[name] + 9 + u, ROOM_MIX, i)
                        if u % 3 < 2:
                            tap(i, u // 3 * 2 + u % 3)
                for p in range(26, PROJECTIONS):
                    w_low(UN[name] + p, SPLITS[name] + p + 1, ROOM_MIX)
                stage_end(ve, "ve")
                tt(big(SLOT["D"], 4096), big(CONV, 4096), big(CONV, 4096), ALU.mult).then_inc(sem("qk_sq"), 1)
                ve.wait_ge(*at("beta_exp", 1, l, 1))
                lk(ve.tensor_scalar(SM[:, 0:16], SM[:, 0:16], 1.0, None, ALU.add))
                lk(ve.reciprocal(SM[:, 0:16], SM[:, 0:16]))
                lk(tt(view(SM, 16, [[8, 2], [1, 8]]), view(bank[6], 8, [[16, 2], [1, 8]]),
                      view(PAR, PC["dt_bias"] + l * 16, [[8, 2], [1, 8]]), ALU.add))
                ve.scalar_tensor_tensor(SM[:, 32:48], SM[:, 16:32], -1.0, SM[:, 16:32], ALU.mult, ALU.max).then_inc(sem("a_abs"), 1)
                ve.wait_ge(*at("a_ln", 1, l, 1))
                lk(ve.scalar_tensor_tensor(SM[:, 32:48], SM[:, 16:32], 0.0, SM[:, 32:48], ALU.max, ALU.add))
                lk(ve.scalar_tensor_tensor(SM[:, 64:80], SM[:, 32:48], -1.0, SM[:, 48:64], ALU.mult, ALU.mult))
                tt(view(BIG, SLOT["A"], [[P, 16], [1, P]]), view(CON, CC["upper"], [[0, 16], [1, P]]),
                   view(SM, 64, [[1, 16], [0, P]]), ALU.mult).then_inc(sem("gu"), 1)
                ve.wait_ge(*at("qk_rs", 1, l, 1))
                tt(big(CONV, 4096), big(CONV, 4096), big(SLOT["D"], 4096), ALU.mult).then_inc(sem("qk_normed"), 1)
                ve.wait_ge(*at("cum", 1, l, 1))
                lk(ve.tensor_copy(SM[:, 80:112], bank[4][:, 0:32]))
                for c in range(16):
                    gr = bank[c // 4][:, (c % 4) * P:(c % 4 + 1) * P]
                    gc = SM[:, 80 + c:81 + c]
                    ve.tensor_scalar(big(SLOT["B"] + c * P, P), gr, gc, 0.0, ALU.subtract, ALU.min)
                    ins = ve.tensor_scalar(big(SLOT["C"] + c * P, P), gr, gc, 0.0, ALU.subtract, ALU.max)
                ins.then_inc(sem("decay_arg"), 1)
                tt(SM[:, 112:128], SM[:, 96:112], SM[:, 80:96], ALU.subtract).then_inc(sem("kd_arg"), 1)
                ve.wait_ge(*at("decay_exp", 1, l, 1))
                tt(SM[:, 144:160], SM[:, 144:160], SM[:, 0:16], ALU.mult)
                tt(view(BIG, SLOT["B"], [[P, 16], [1, P]]), view(BIG, SLOT["B"], [[P, 16], [1, P]]),
                   view(CON, CC["upper"], [[0, 16], [1, P]]), ALU.mult)
                tt(view(BIG, SLOT["C"], [[P, 16], [1, P]]), view(BIG, SLOT["C"], [[P, 16], [1, P]]),
                   view(CON, CC["lower_strict"], [[0, 16], [1, P]]), ALU.mult)
                stage_end(ve, "ve")
                ve.wait_ge(*at("kk", 1, l, 2))
                for c in range(16):
                    ins = ve.scalar_tensor_tensor(big(SLOT["D"] + c * P, P), bank[c // 4][:, (c % 4) * P:(c % 4 + 1) * P],
                                                  SM[:, c:c + 1], big(SLOT["C"] + c * P, P), ALU.mult, ALU.mult)
                lk(ins)
                ve.nop().then_inc(sem("lmat"), 1)
                ve.wait_ge(*at("kk", 2, l, 2))
                for b in range(4):
                    tt(big(SLOT["B"] + b * 512, 512), bank[4 + b][:, :], big(SLOT["B"] + b * 512, 512), ALU.mult)
                lk(tt(view(BIG, SLOT["E"], [[P, 16], [1, P]]), view(BIG, SLOT["D"], [[P, 16], [1, P]]),
                      view(CON, CC["level0_lower"], [[0, 16], [1, P]]), ALU.mult))
                tt(view(BIG, SLOT["E"], [[P, 16], [1, P]]), view(CON, CC["ident"], [[0, 16], [1, P]]),
                   view(BIG, SLOT["E"], [[P, 16], [1, P]]), ALU.subtract)
                ve.wait_ge(*at("lt_out", 1, l, 1))
                lk(tt(view(BIG, SLOT["F"], [[P, 16], [1, P]]), view(BIG, SLOT["C"], [[P, 16], [1, P]]),
                      view(CON, CC["level"], [[0, 16], [1, P]]), ALU.mult))
                tt(view(BIG, SLOT["F"], [[P, 16], [1, P]]), view(CON, CC["ident"], [[0, 16], [1, P]]),
                   view(BIG, SLOT["F"], [[P, 16], [1, P]]), ALU.subtract)
                stage_end(ve, "ve")
                for s in range(6):
                    for q in range(4):
                        ve.wait_ge(*at("level_p", 4 * s + q + 1, l, 24))
                        x = q * 512
                        tt(big(SLOT["E"] + x, 512), big(SLOT["E"] + x, 512), bank[4 + q % 2][:, :], ALU.subtract)
                        lk(tt(big(SLOT["F"] + x, 512), big(SLOT["F"] + x, 512), bank[6 + q % 2][:, :], ALU.subtract))
                        ve.nop().then_inc(sem("level_t"), 1)
                stage_end(ve, "ve")
                ve.wait_ge(*at("kvt", 1, l, 1))
                for b in range(4):
                    s = view(SM, (128 if b < 2 else 144) + b * 4, [[1, 4], [0, P]])
                    tt(view(BIG, SLOT["C"] + b * 512, [[P, 4], [1, P]]), view(bank[b], 0, [[P, 4], [1, P]]), s, ALU.mult)
                for b in range(4):
                    tt(view(BIG, SLOT["D"] + b * 512, [[P, 4], [1, P]]), view(bank[4 + b], 0, [[P, 4], [1, P]]),
                       view(SM, b * 4, [[1, 4], [0, P]]), ALU.mult)
                qv = view(BIG, CONV + P, [[TOK, 8], [1, P]])
                tt(qv, qv, view(BIG, EG, [[P, 8], [1, P]]), ALU.mult).then_inc(sem("q_dec"), 1)
                stage_end(ve, "ve")
                ve.wait_ge(*at("vnew_ps", 1, l, 1))
                lk(ve.tensor_copy(big(SLOT["A"], 512), bank[0][:, :]))
                lk(ve.tensor_copy(big(SLOT["A"] + 512, 512), bank[1][:, :]))
                ve.nop().then_inc(sem("vnew0"), 1)
                ve.wait_ge(*at("state_ps", 1, l, 1))
                lk(ve.tensor_copy(big(ST, 512), bank[4][:, :]))
                lk(ve.tensor_copy(big(ST + 512, 512), bank[5][:, :]))
                ve.nop().then_inc(sem("state"), 1)
                ve.wait_ge(*at("vnew_ps1", 1, l, 1))
                lk(ve.tensor_copy(big(SLOT["A"] + 1024, 512), bank[6][:, :]))
                lk(ve.tensor_copy(big(SLOT["A"] + 1536, 512), bank[7][:, :]))
                ve.nop().then_inc(sem("vnew1"), 1)
                ve.wait_ge(*at("o_rs", 1, l, 1))
                for b in range(4):
                    x = b * 512
                    ins = tt(big(SLOT["E"] + x, 512), bank[b][:, :], big(SLOT["E"] + x, 512), ALU.mult)
                lk(ins)
                ve.scalar_tensor_tensor(big(OD, 2048), big(SLOT["E"], 2048), par("dn_out_norm", 1, l), big(Z_, 2048),
                                        ALU.mult, ALU.mult)
                stage_end(ve, "ve")
                ve.wait_ge(*at("z_ps", 1, l, 1))
                for h in range(HEADS):
                    ve.scalar_tensor_tensor(big(ZB + h * 384, 384), bank[h][:, 0:384], 0.125, con("stick_mask", 384),
                                            ALU.mult, ALU.add).then_inc(sem("z_out"), 1)
                ve.wait_ge(*at("vt_ps", 1, l, 1))
                ve.tensor_copy(big(VT, 512), bank[0][:, :])
                lk(ve.tensor_copy(big(VT + 512, 512), bank[1][:, :]))
                ve.nop().then_inc(sem("vt_out"), 1)
                ve.wait_ge(*at("sp_ln", 1, l, 1))
                ve.scalar_tensor_tensor(big(SP, 3072), big(ZB, 3072), 0.0, big(SP, 3072), ALU.max, ALU.add)\
                    .then_inc(sem("sp_out"), 1)
                ve.wait_ge(*at("rem_ps", 1, l, 1))
                for h in range(HEADS):
                    ins = tt(big(ZB + h * 384, 384), big(ZB + h * 384, 384), bank[h][:, 0:384], ALU.subtract)
                ins.then_inc(sem("stick_arg"), 1)
                ve.wait_ge(*at("stick_ps", 1, l, 1))
                ve.tensor_copy(big(OSB, 512), bank[0][:, :])
                ve.tensor_copy(big(OSB + 512, 512), bank[1][:, :])
                stage_end(ve, "ve")
                n = UN[f"up{l}"]
                for b in range(4):
                    ve.wait_ge(sem("unit_done"), n + b + 1)
                    tt(big(SLOT["D"] + b * 512, 512), bank[b][:, :], big(GATES + b * 512, 512), ALU.mult)
                ve.wait_ge(sem("unit_done"), n + 6)
                for b in range(4):
                    ins = tt(big(SLOT["E"] + b * 512, 512), bank[4 + b][:, :], big(GATES + 2048 + b * 512, 512), ALU.mult)
                lk(ins)
                tt(big(SLOT["D"], 2048), big(SLOT["D"], 2048), big(SLOT["E"], 2048), ALU.add).then_inc(sem("mixed"), 1)
                n = UN[f"w_out{l}"]
                for t in range(KT):
                    ve.wait_ge(sem("unit_done"), n + t // 2 + 1)
                    ve.scalar_tensor_tensor(X[:, t * TOK:(t + 1) * TOK], bank[t // 2][:, (t % 2) * TOK:(t % 2 + 1) * TOK],
                                            mod(l, 2, t, 1), X[:, t * TOK:(t + 1) * TOK], ALU.mult, ALU.add)
                stage_end(ve, "ve")
                lk(ve.scalar_tensor_tensor(NSC[:, :], mod(l, 4), 1.0, par("norm_ffn", 8, l * 8), ALU.add, ALU.mult))
                norm_v(norms, None, True, split="ffn" if l == 0 else None)
                norms += 1
                if l == 0:
                    ffn_split_v("ffn", BLK1, 0, ROOM)
                    ve.wait_ge(sem("unit_done"), UN["ffn"] + 3 * BLK1)
                    for t in range(KT):
                        ve.scalar_tensor_tensor(X[:, t * TOK:(t + 1) * TOK], bank[4 + t // 2][:, (t % 2) * TOK:(t % 2 + 1) * TOK],
                                                mod(l, 5, t, 1), X[:, t * TOK:(t + 1) * TOK], ALU.mult, ALU.add)
                    stage_end(ve, "ve")
                    continue
                ve.wait_ge(sem("logits"), 1)
                lk(tt(SM[:, 0:16], bank[0][:, 0:16], par("router_b", 16), ALU.add))
                for n in range(NT):
                    lk(ve.max(SM[:, 16 + 8 * n:24 + 8 * n], SM[:, 8 * n:8 * n + 8]))
                    lk(ve.max_index(SMU[:, 8 * n:8 * n + 8], SM[:, 16 + 8 * n:24 + 8 * n], SM[:, 8 * n:8 * n + 8]))
                lk(ve.tensor_copy(SM[:, 32:48], SMU[:, 0:16]))
                tt(view(SM, 48, [[1, 2]]), view(SM, 17, [[8, 2]]), view(SM, 16, [[8, 2]]), ALU.subtract).then_inc(sem("route_arg"), 1)
                ve.wait_ge(sem("route_exp"), 1)
                lk(ve.tensor_scalar(SM[:, 50:52], SM[:, 48:50], 1.0, None, ALU.add))
                lk(ve.reciprocal(SM[:, 50:52], SM[:, 50:52]))
                lk(tt(SM[:, 52:54], SM[:, 48:50], SM[:, 50:52], ALU.mult))
                for n in range(NT):
                    lk(ve.tensor_scalar(SM[:, 56 + 8 * n:64 + 8 * n], con("iota", 8), SM[:, 32 + 8 * n:33 + 8 * n],
                                        SM[:, 50 + n:51 + n], ALU.is_equal, ALU.mult))
                    lk(ve.tensor_scalar(SM[:, 72 + 8 * n:80 + 8 * n], con("iota", 8), SM[:, 33 + 8 * n:34 + 8 * n],
                                        SM[:, 52 + n:53 + n], ALU.is_equal, ALU.mult))
                lk(tt(SM[:, GATE:GATE + 16], SM[:, 56:72], SM[:, 72:88], ALU.add))
                for n in range(NT):
                    ve.tensor_scalar(SM[:, PLACE + 8 * n:PLACE + 8 * n + 8], con("iota", 8), SM[:, 32 + 8 * n:33 + 8 * n],
                                     None, ALU.is_equal)
                    lk(ve.tensor_scalar(SM[:, MASK + 8 * n:MASK + 8 * n + 8], con("iota", 8), SM[:, 33 + 8 * n:34 + 8 * n],
                                        None, ALU.is_equal))
                tt(SM[:, MASK:MASK + 16], SM[:, MASK:MASK + 16], SM[:, PLACE:PLACE + 16], ALU.add).then_inc(sem("masks"), 1)
                for half_e in range(2):
                    tt(view(BIG, GD + half_e * 1024, [[TOK, 4], [1, P]]), view(CON, CC["ident"], [[0, 4], [1, P]]),
                       view(SM, GATE + half_e * 4, [[1, 4], [0, P]]), ALU.mult)
                    lk(tt(view(BIG, GD + half_e * 1024 + P, [[TOK, 4], [1, P]]), view(CON, CC["ident"], [[0, 4], [1, P]]),
                          view(SM, GATE + 8 + half_e * 4, [[1, 4], [0, P]]), ALU.mult))
                    ve.nop().then_inc(sem("gate_diag"), 1)
                for half_e in range(2):
                    ve.wait_ge(sem("gate_ps"), half_e + 1)
                    ve.tensor_copy(big(GR + half_e * 1024, 512), bank[1 + 2 * half_e][:, :])
                    ve.tensor_copy(big(GR + half_e * 1024 + 512, 512), bank[2 + 2 * half_e][:, :])
                ve.memset(big(YE, 2048), 0.0)
                ve.wait_ge(sem("places"), 1)
                ve.tensor_copy(SM[:, PLACE:PLACE + 16], bank[5][:, 0:16])
                ve.tensor_copy(SMU[:, 16:24], bank[5][:, 16:24])
                lk(ve.tensor_copy(big(SLOTS, P), bank[5][:, 128:256]))
                for e in range(EXPERTS):
                    for n in range(NT):
                        c = 8 * n + e
                        place = SM[:, PLACE + c:PLACE + c + 1]
                        ve.tensor_scalar(big(SEL + (2 * e + n) * P, P), big(SLOTS, P), place, SM[:, MASK + c:MASK + c + 1],
                                         ALU.is_equal, ALU.mult)
                        ve.tensor_scalar(big(SELG + (2 * e + n) * P, P), big(SLOTS, P), place, SM[:, GATE + c:GATE + c + 1],
                                         ALU.is_equal, ALU.mult)
                stage_end(ve, "ve")
                ve.nop().then_inc(sem("gather_low"), 2)
                with ve.Fori(0, EXPERTS // 2) as i:
                    for j in range(2):
                        ve.wait_ge(sem("gather_ps"), i * 2 + (j + 1))
                        ve.tensor_copy(GATHERED[:, bass.ds(i * 2048 + j * 1024, 512)], bank[4 + 2 * j][:, :])\
                            .then_inc(sem("gather_low"), 1)
                ve.nop().then_inc(sem("expert_out"), 1)
                stage_end(ve, "ve")

                def dense_expert(e):
                    ffn_loop(BLK1, BLK1, UN["moe"], e)
                    ve.wait_ge(sem("unit_done"), e * (3 * BLK1) + (UN["moe"] + 3 * BLK1))
                    for b in range(4):
                        g = BIG[:, bass.ds(e * TOK + GR, TOK)]
                        for t in range(2):
                            ins = tt(big(YT + b * 512 + t * TOK, TOK), bank[4 + b][:, t * TOK:(t + 1) * TOK], g, ALU.mult)
                    ins.then_inc(sem("expert_out"), 1)
                    ve.wait_ge(sem("expert_out"), e + 2)
                    tt(big(YE, 2048), big(YE, 2048), big(YT, 2048), ALU.add).then_inc(sem("expert_sum"), 1)

                lk(ve.memset(big(ZEROS, 1024), 0.0))
                with ve.Fori(0, EXPERTS) as e:
                    count = ve.value_load(SMU[0:1, bass.ds(e + 16, 1)], min_val=0, max_val=TOK)
                    with ve.If(count <= P):
                        ffn_slots_v(UN["moe"], BLK1, BLK1, e)
                        ve.nop().then_inc(sem("expert_sum"), 1)
                    with ve.Else():
                        ve.tensor_copy(GATHERED[:, bass.ds(e * 1024, 1024)], big(ZEROS, 1024))
                        dense_expert(e)
                        ve.nop().then_inc(sem("xh_low"), 1)
                        ve.nop().then_inc(sem("x_low"), 3 * BLK1)
                        ve.nop().then_inc(sem("x_turned_low"), BLK1)
                    ve.wait_ge(sem("expert_sum"), e + 1)
                stage_end(ve, "ve")
                for b in range(4):
                    ve.wait_ge(sem("scatter"), b + 1)
                    ins = tt(big(YE + b * 512, 512), big(YE + b * 512, 512), bank[b][:, :], ALU.add)
                lk(ins)
                for t in range(KT):
                    ve.scalar_tensor_tensor(X[:, t * TOK:(t + 1) * TOK], big(YE + t * TOK, TOK), mod(l, 5, t, 1),
                                            X[:, t * TOK:(t + 1) * TOK], ALU.mult, ALU.add)
                stage_end(ve, "ve")
            norm_v(norms, ("final_norm", 0), False, X)
            stage_end(ve, "ve")
            norms += 1
            done_blocks = BLK1 * (1 + EXPERTS)

            def ffn2(name, l, last=False):
                nonlocal norms, done_blocks
                which = name[:4] + "_norm"
                room = {"ffn1_0": ROOM_S5, "ffn1_1": ROOM_KV}.get(name, ROOM)
                norm_v(norms, (which, l * 8), False, split=name, room=room)
                norms += 1
                ffn_split_v(name, BLK2, done_blocks, room)
                done_blocks += BLK2
                ve.wait_ge(sem("unit_done"), UN[name] + 3 * BLK2)
                for b in range(4):
                    ins = ve.scalar_tensor_tensor(X[:, b * 512:(b + 1) * 512], bank[4 + b][:, :], 0.5, X[:, b * 512:(b + 1) * 512],
                                                  ALU.mult, ALU.add)
                if last:
                    lk(ins)
                    ve.nop().then_inc(sem("result"), 1)
                else:
                    stage_end(ve, "ve")

            a_re, a_im = par("a_re", 32), par("a_im", 32)
            dt, mag, th = SM[:, 0:32], SM[:, 32:64], SM[:, 64:96]
            ve.wait_ge(sem("s5_dt"), 1)
            tt(mag, a_re, dt, ALU.mult).then_inc(sem("s5_mag_arg"), 1)
            lk(tt(th, a_im, dt, ALU.mult))
            PH, RN = 256, 512
            for k in range(8):
                ins = ve.tensor_scalar(SM[:, PH + 32 * k:PH + 32 * (k + 1)], th, float(2 ** k), None, ALU.mult)
            lk(ins)
            magic = 1.5 * 2.0 ** 23
            lk(ve.tensor_scalar(SM[:, RN:RN + 256], SM[:, PH:PH + 256], float(1 / TWO_PI), magic, ALU.mult, ALU.add))
            lk(ve.tensor_scalar(SM[:, RN:RN + 256], SM[:, RN:RN + 256], magic, None, ALU.subtract))
            p1 = 6.28125
            p2 = float(np.float32(np.round((TWO_PI - p1) * 2 ** 22) / 2 ** 22))
            p3 = float(np.float32(TWO_PI - p1 - p2))
            for part in (p1, p2, p3):
                lk(ve.scalar_tensor_tensor(SM[:, PH:PH + 256], SM[:, RN:RN + 256], -part, SM[:, PH:PH + 256], ALU.mult, ALU.add))
            PI = 3.1415925
            lk(ve.tensor_scalar(SM[:, PH:PH + 256], SM[:, PH:PH + 256], PI, -PI, ALU.min, ALU.max))
            lk(ve.scalar_tensor_tensor(SM[:, RN:RN + 256], SM[:, PH:PH + 256], -1.0, SM[:, PH:PH + 256], ALU.mult, ALU.max))
            ve.tensor_scalar(SM[:, RN:RN + 256], SM[:, RN:RN + 256], -1.0, float(np.pi / 2), ALU.mult, ALU.add)\
                .then_inc(sem("angles"), 1)
            ve.wait_ge(sem("s5_trig"), 1)
            cr, ci, den, zr, zi, t1 = (SM[:, 768 + 32 * k:800 + 32 * k] for k in range(6))
            lk(tt(cr, mag, SM[:, RN:RN + 32], ALU.mult))
            lk(ve.tensor_scalar(cr, cr, -1.0, None, ALU.add))
            lk(tt(ci, mag, SM[:, PH:PH + 32], ALU.mult))
            lk(tt(den, a_re, a_re, ALU.mult))
            lk(tt(t1, a_im, a_im, ALU.mult))
            lk(tt(den, den, t1, ALU.add))
            lk(ve.reciprocal(den, den))
            lk(tt(zr, cr, a_re, ALU.mult))
            lk(tt(t1, ci, a_im, ALU.mult))
            lk(tt(zr, zr, t1, ALU.add))
            lk(tt(zr, zr, den, ALU.mult))
            lk(tt(zi, ci, a_re, ALU.mult))
            lk(tt(t1, cr, a_im, ALU.mult))
            lk(tt(zi, zi, t1, ALU.subtract))
            lk(tt(zi, zi, den, ALU.mult))
            ve.wait_ge(sem("s5_here"), 64)
            lk(ve.memset(big(BBX, 2048), 0.0))
            lk(ve.memset(big(CX, 3072), 0.0))
            for g in range(2):
                p0 = 64 * g

                def src(i):
                    return view(BIG, S5P + i * 512, [[16, 32], [1, 16]], p0, 64)

                def bc(off):
                    return view(SM, off, [[1, 32], [0, 16]], p0, 64)

                def dst(off):
                    return view(BIG, off + 16 * g, [[32, 32], [1, 16]], p0, 64)

                tmp = view(BIG, BBT, [[16, 32], [1, 16]], p0, 64)
                zro, zio = 768 + 96, 768 + 128
                tt(dst(BBX), src(0), bc(zro), ALU.mult)
                lk(tt(tmp, src(1), bc(zio), ALU.mult))
                lk(tt(dst(BBX), dst(BBX), tmp, ALU.subtract))
                tt(dst(BBX + 1024), src(1), bc(zro), ALU.mult)
                lk(tt(tmp, src(0), bc(zio), ALU.mult))
                lk(tt(dst(BBX + 1024), dst(BBX + 1024), tmp, ALU.add))
                lk(ve.tensor_copy(dst(CX), src(2)))
                lk(ve.tensor_scalar(dst(CX + 1024), src(2), -1.0, None, ALU.mult))
                lk(ve.tensor_scalar(dst(CX + 2048), src(3), -1.0, None, ALU.mult))
            ve.nop().then_inc(sem("bb"), 1)
            ffn2("ffn1_0", 0)
            norm_v(norms, ("mix_norm", 0), False)
            norms += 1
            ve.wait_ge(sem("bt_ps"), 1)
            for b in range(4):
                ins = ve.tensor_copy(big(BBT + b * 512, 512), bank[(0, 1, 4, 5)[b]][:, :])
            lk(ins)
            ve.nop().then_inc(sem("bt"), 1)
            ve.wait_ge(sem("tables"), 1)

            def s5_out(k):
                ve.wait_ge(sem("y_ps"), k + 1)
                ve.scalar_tensor_tensor(big(YB + k * TOK, TOK), H[:, k * TOK:(k + 1) * TOK], par("s5_d", 1, k),
                                        bank[4 + k % 2][:, 0:TOK], ALU.mult, ALU.add).then_inc(sem("y_out"), 1)

            for k in range(KT):
                ve.wait_ge(sem("bu"), k + 1)

                vr, vi = VR, VI
                t1, t2 = (YR, YI) if k < 3 else rot(k - 2)[:2]
                if 0 < k < 3:
                    ve.wait_ge(sem("rotated"), k)
                if k >= 3:
                    ve.wait_ge(sem("y_ps"), k - 1)
                    ve.wait_ge(sem("scanned"), k)
                pairs = [[TOK, 4], [1, TOK]]
                c, s = view(BIG, TC + k * 1024, pairs), view(BIG, TS + k * 1024, pairs)
                re, im = view(PS, 0, [[512, 4], [1, TOK]]), view(PS, TOK, [[512, 4], [1, TOK]])
                tt(view(BIG, vr, pairs), re, c, ALU.mult)
                tt(view(BIG, t1, pairs), im, s, ALU.mult)
                tt(view(BIG, vi, pairs), im, c, ALU.mult)
                tt(view(BIG, t2, pairs), re, s, ALU.mult).then_inc(sem("bu_read"), 1)
                ve.wait_ge(sem("bu_read"), k + 1)
                lk(tt(big(vr, 1024), big(vr, 1024), big(t1, 1024), ALU.add))
                lk(tt(big(vi, 1024), big(vi, 1024), big(t2, 1024), ALU.subtract))
                if k > 1:
                    s5_out(k - 2)
                if k >= 3:
                    ve.wait_ge(sem("rotated"), k)
                for j in range(4):
                    m = view(SM, 32 + 4 * k + j, [[0, TOK]])
                    ve.tensor_tensor_scan(big(YR + j * TOK, TOK), m, big(vr + j * TOK, TOK), 0.0, ALU.mult, ALU.add)
                    ins = ve.tensor_tensor_scan(big(YI + j * TOK, TOK), m, big(vi + j * TOK, TOK), 0.0, ALU.mult, ALU.add)
                ins.then_inc(sem("scanned"), 1)
            s5_out(KT - 2)
            s5_out(KT - 1)
            stage_end(ve, "ve")
            ve.wait_ge(sem("glu_sig"), 4)
            lk(tt(big(SLOT["D"], 2048), big(SLOT["D"], 2048), big(YB, 2048), ALU.mult))
            tt(X[:, :], X[:, :], big(SLOT["D"], 2048), ALU.add)
            stage_end(ve, "ve")
            ffn2("ffn2_0", 0)
            norm_v(norms, ("kv_norm", 0), False)
            norms += 1
            for u in range(6):
                ve.wait_ge(sem("unit_done"), UN["kv"] + u + 1)
                ve.tensor_copy(big(KV + u * 512, 512), bank[u][:, :])
            stage_end(ve, "ve")
            tt(big(KSQ, 512), big(KV + 4 * TOK, 512), big(KV + 4 * TOK, 512), ALU.mult)
            lk(tt(big(KSQ + 512, 512), big(KV + 8 * TOK, 512), big(KV + 8 * TOK, 512), ALU.mult))
            ve.nop().then_inc(sem("kv_sq"), 1)
            for i, pos in enumerate(("pos_k", "pos_v")):
                for hf in range(2):
                    ins = tt(view(BIG, SRC + i * 1024 + hf * 512, [[16, 32], [1, 16]]),
                             view(BIG, KV + i * 512, [[16, 32], [1, 16]]),
                             view(PAR, PC[pos] + 16 * hf, [[0, 32], [1, 16]]), ALU.add)
            lk(ins)
            ve.nop().then_inc(sem("cmp_src"), 1)
            ve.wait_ge(sem("kv_sum"), 1)

            def refine(y, m, t):
                lk(tt(t, y, y, ALU.mult))
                lk(tt(t, t, m, ALU.mult))
                lk(ve.tensor_scalar(t, t, -0.5, 1.5, ALU.mult, ALU.add))
                lk(tt(y, y, t, ALU.mult))

            lk(ve.tensor_scalar(big(KSQ, 512), bank[0][:, :], 1 / 64, EPS, ALU.mult, ALU.add))
            lk(ve.tensor_scalar(big(KSQ + 512, 512), bank[1][:, :], 1 / 64, EPS, ALU.mult, ALU.add))
            ve.nop().then_inc(sem("kv_ms"), 1)
            ve.wait_ge(sem("kv_rs"), 1)
            refine(big(KRS, 1024), big(KSQ, 1024), big(KT2, 1024))
            for i, (t0, w) in enumerate(((4, "k_norm_slc"), (8, "k_norm_win"))):
                k = big(KV + t0 * TOK, 512)
                lk(ve.scalar_tensor_tensor(k, k, par(w, 1), big(KRS + i * 512, 512), ALU.mult, ALU.mult))
            ve.nop().then_inc(sem("k_normed"), 1)
            ve.wait_ge(sem("kv_vt"), 1)
            ve.tensor_copy(big(VN, 512), bank[2][:, :])
            ve.tensor_copy(big(VN + 512, 512), bank[3][:, :])
            ve.wait_ge(sem("bias_ps"), 1)
            lk(ve.memset(BIG[0:QH, BTAB:BTAB + 384], NEG))
            lk(ve.tensor_copy(BIG[0:QH, BTAB + 127:BTAB + 383], bank[4][0:QH, 0:256]))
            ve.nop().then_inc(sem("bias_tab"), 1)
            for n in range(NT):
                tt(view(BIG, CB + n * QH * NCMP, [[NCMP, QH], [1, NCMP]]), view(bank[5], n * QH * NCMP, [[1, QH], [QH, NCMP]]),
                   view(CON, CC["cmp_add"] + n * NCMP, [[0, QH], [1, NCMP]]), ALU.add)
            ve.wait_ge(sem("cmp_ps"), 1)
            for hf in range(2):
                ins = ve.tensor_copy(view(BIG, KC + hf * NCMP, [[2 * NCMP, 2], [1, NCMP]]),
                                     view(bank[7], hf * 2 * NCMP, [[NCMP, 2], [1, NCMP]]))
            lk(ins)
            ve.tensor_copy(BIG[0:NCMP, VC:VC + 256], bank[7][0:NCMP, 128:384])
            kc = big(KC, 4 * NCMP)
            lk(tt(SM[:, 128:128 + 4 * NCMP], kc, kc, ALU.mult))
            ve.nop().then_inc(sem("kc_sq"), 1)
            ve.wait_ge(sem("kc_sum"), 1)
            lk(ve.tensor_scalar(SM[:, 192:192 + 4 * NCMP], bank[7][:, 64:64 + 4 * NCMP], 1 / 64, EPS, ALU.mult, ALU.add))
            ve.nop().then_inc(sem("kc_ms"), 1)
            ve.wait_ge(sem("kc_rs"), 1)
            refine(SM[:, 256:256 + 4 * NCMP], SM[:, 192:192 + 4 * NCMP], SM[:, 320:320 + 4 * NCMP])
            ve.scalar_tensor_tensor(kc, kc, par("k_norm_cmp", 1), SM[:, 256:256 + 4 * NCMP], ALU.mult, ALU.mult)
            stage_end(ve, "ve")
            ffn2("ffn1_1", 1)
            norm_v(norms, ("mix_norm", 8), False)
            norms += 1
            for u in range(4):
                ve.wait_ge(sem("unit_done"), UN["q"] + u + 1)
                lk(ve.tensor_copy(big(QB + u * 512, 512), bank[u][:, :]))
            stage_end(ve, "ve")
            tt(big(PT, 2048), big(QB, 2048), big(QB, 2048), ALU.mult).then_inc(sem("q_sq"), 1)
            ve.wait_ge(sem("gate_exp"), 1)
            lk(ve.tensor_scalar(big(GT, 96), big(GT, 96), 1.0, None, ALU.add))
            ve.reciprocal(big(GT, 96), big(GT, 96))
            ve.wait_ge(sem("q_sum"), 1)
            for b in range(4):
                ins = ve.tensor_scalar(big(PT + b * 512, 512), bank[b][:, :], 1 / 64, EPS, ALU.mult, ALU.add)
            lk(ins)
            ve.nop().then_inc(sem("q_ms"), 1)
            ve.wait_ge(sem("q_rs"), 1)
            refine(big(PT + 2048, 2048), big(PT, 2048), big(PT + 4096, 2048))
            ve.scalar_tensor_tensor(big(QB, 2048), big(QB, 2048), par("q_norm", 1), big(PT + 2048, 2048), ALU.mult, ALU.mult)
            stage_end(ve, "ve")
            W_ = QH * NCMP
            ve.wait_ge(sem("cmp_logits"), 1)
            for b in range(2):
                every = [[2 * NCMP, QH], [1, NCMP]]
                lk(ve.scalar_tensor_tensor(view(BIG, CP + b * NCMP, every), view(bank[b], b * NCMP, every), 0.125,
                                           view(BIG, CB + b * NCMP, every), ALU.mult, ALU.add))
            c3 = view(BIG, CP, [[NCMP, 2 * QH], [1, NCMP]])
            lk(ve.tensor_reduce(SM[:, 0:32], c3, AX, ALU.max))
            lk(tt(c3, c3, view(SM, 0, [[1, 32], [0, NCMP]]), ALU.subtract))
            ve.nop().then_inc(sem("cmp_arg"), 1)
            ve.wait_ge(sem("cmp_exp"), 1)
            lk(ve.tensor_reduce(SM[:, 32:64], c3, AX, ALU.add))
            lk(ve.reciprocal(SM[:, 32:64], SM[:, 32:64]))
            lk(tt(SM[:, 32:64], SM[:, 32:64], view(BIG, GT, [[3, 32]]), ALU.mult))
            lk(tt(c3, c3, view(SM, 32, [[1, 32], [0, NCMP]]), ALU.mult))
            for n in range(NT):
                cn = view(BIG, CP + n * W_, [[NCMP, QH], [1, NCMP]])
                ins = tt(cn, cn, view(CON, CC["cmp_mul"] + n * NCMP, [[0, QH], [1, NCMP]]), ALU.mult)
            lk(ins)
            ve.nop().then_inc(sem("cmp_p"), 1)
            stage_end(ve, "ve")
            ve.wait_ge(sem("cmp_pt"), 1)
            for b in range(8):
                ve.tensor_copy(big(CPT + b * 512, 512, 0, NCMP), bank[b][0:NCMP, :])
            stage_end(ve, "ve")
            ve.wait_ge(sem("bias_here"), 16)
            for br in range(2):
                for h in range(QH):
                    b = bank[h % 8]
                    ve.wait_ge(sem("logits_ps"), br * 16 + h + 1)
                    two = [[P, 2], [1, P]]
                    ve.scalar_tensor_tensor(view(BIG, LG + h * 384, two), view(b, 0, two), 0.125,
                                            view(BIG, BT + h * 256 + P - 1, [[P, 2], [-1, P]]), ALU.mult, ALU.add)
                    ve.scalar_tensor_tensor(big(LG + h * 384 + 256, 128), b[:, 256:384], 0.125,
                                            view(BIG, BT + h * 256 + P - 1, [[-1, P]]),
                                            ALU.mult, ALU.add).then_inc(sem("logits_out"), 1)
                ve.wait_ge(sem("logits_out"), br * 16 + 16)
                lk(ve.tensor_reduce(SM[:, 0:16], view(BIG, LG, [[384, QH], [1, P]]), AX, ALU.max))
                lk(ve.tensor_reduce(SM[:, 16:32], view(BIG, LG + P, [[384, QH], [1, TOK]]), AX, ALU.max))
                lk(ve.tensor_scalar(SM[:, 32:64], SM[:, 0:32], -1.0, None, ALU.mult))
                ve.nop().then_inc(sem("row_max"), 1)
                ve.wait_ge(sem("row_exp"), br + 1)
                lk(ve.reciprocal(SM[:, 64:96], SM[:, 64:96]))
                lk(tt(SM[:, 64:96], SM[:, 64:96], view(BIG, GT + 1 + br, [[3, 32]]), ALU.mult))
                a0 = view(BIG, LG, [[384, QH], [1, P]])
                a1 = view(BIG, LG + P, [[384, QH], [1, TOK]])
                tt(a0, a0, view(SM, 64, [[1, 16], [0, P]]), ALU.mult)
                lk(tt(a1, a1, view(SM, 80, [[1, 16], [0, TOK]]), ALU.mult))
                ve.nop().then_inc(sem("probs"), 1)
                for h in range(QH):
                    ve.wait_ge(sem("pt_ps"), br * 16 + h + 1)
                    ve.tensor_copy(big(PT + h * 384, 384), bank[h % 8][:, 0:384]).then_inc(sem("pt_out"), 1)
                ve.wait_ge(sem("o_branch"), br + 1)
                for b in range(4):
                    if br == 0:
                        ve.tensor_copy(big(OB + b * 512, 512), bank[b][:, :])
                    else:
                        tt(big(OB + b * 512, 512), big(OB + b * 512, 512), bank[b][:, :], ALU.add)
                stage_end(ve, "ve")
            for b in range(4):
                ve.wait_ge(sem("unit_done"), UN["w_o"] + b + 1)
                tt(X[:, b * 512:(b + 1) * 512], X[:, b * 512:(b + 1) * 512], bank[b][:, :], ALU.add)
            stage_end(ve, "ve")
            ffn2("ffn2_1", 1, last=True)

        @stage.scalar
        def _(se):
            act = se.activation

            def lk(ins):
                link(se, "scalar_step", ins)

            def w_hi(n, room, i=0):
                se.wait_ge(sem(f"loaded{n % RING}"), i * 16 + 16 * (n // RING + 1))
                se.wait_ge(sem("unit_done"), i * RING + (n - 1))
                act(parts(w_high(room, n), UNIT), ring[n % RING][:, :], ACT.Copy).then_inc(sem("w_high"), 1)

            def h_hi(room):
                act(parts(h_high(room), 2048), H, ACT.Copy).then_inc(sem("h_high"), 1)

            def ffn_split_s(name, blocks, base, room):
                n, b0 = UN[name], SPLIT_BLOCKS[name]

                def step(p, i=0):
                    which, b = unit_role(p)
                    g = (b % 2) * 512
                    if p + 2 < 3 * blocks:
                        w_hi(n + p + 2, room, i)
                    if which == 0:
                        se.wait_ge(sem("unit_done"), i * RING + (n + p + 1))
                        if b > 1:
                            se.wait_ge(sem("g_low"), i * 2 + (b0 + b - 1))
                        act(FS[:, g:g + 512], bank[2 * (b % 2)][:, :], ACT.Silu).then_inc(sem("silu"), 1)
                    if which == 1:
                        se.wait_ge(sem("gated"), i * 2 + (base + b + 1))
                        act(parts(FSB + g, 512), FG[:, g:g + 512], ACT.Copy).then_inc(sem("g_high"), 1)

                h_hi(room)
                for p in range(5):
                    step(p)
                with se.Fori(0, loop_rounds(blocks)) as i:
                    for p in range(5, 11):
                        step(p, i)
                for p in range(5 + 6 * loop_rounds(blocks), 3 * blocks - 1):
                    step(p)

            def norm_s(i, shift=None, split=None, room=ROOM):
                if split is not None:
                    if split == "ffn1_0":
                        se.wait_ge(sem("bb"), 1)
                    w_hi(UN[split], room)
                    w_hi(UN[split] + 1, room)
                se.wait_ge(*at("norm_sum", 1, i))
                lk(act(LNB[:, :], bank[7][:, 0:TOK], ACT.Ln, bias=EPSB[:, 0:1], scale=1 / D))
                act(RS[:, :], LNB[:, :], ACT.Exp, scale=-0.5).then_inc(sem("norm_rs"), 1)
                if shift is not None:
                    l, part = shift
                    for t in range(KT):
                        se.wait_ge(sem("norm_scaled"), counts["scaled"] + t + 1)
                        act(H[:, t * TOK:(t + 1) * TOK], H[:, t * TOK:(t + 1) * TOK], ACT.Identity,
                            bias=MOD[:, l * 48 + part * 8 + t:l * 48 + part * 8 + t + 1]).then_inc(sem("normed"), 1)
                    counts["scaled"] += KT

            counts = {"scaled": 0}

            def ffn_slots_s(n, blocks, base, e):
                def x_hi(p, i):
                    r = (n + p) % RING
                    se.wait_ge(sem(f"loaded{r}"), i * 16 + 16 * ((n + p) // RING + 1))
                    se.wait_ge(sem("unit_done"), i * RING + (n + p - 2))
                    act(slot_high(n + p), ring[r][:, :], ACT.Copy).then_inc(sem("x_high"), 1)

                def turned_hi(b, i):
                    se.wait_ge(sem("x_turned"), i * 2 + (b + 1))
                    act(turned(FSB, b), bank[6 + b % 2][:, 0:TOK], ACT.Copy).then_inc(sem("x_turned_high"), 1)

                def step(p, i):
                    which, b = unit_role(p)
                    if which == 0:
                        g = (b % 2) * 512
                        se.wait_ge(sem("unit_done"), i * RING + (n + p + 1))
                        if b > 1:
                            se.wait_ge(sem("gated"), i * 2 + (base + b - 1))
                        act(FS[:, g:g + TOK], bank[2 * (b % 2)][:, 0:TOK], ACT.Silu).then_inc(sem("silu"), 1)
                        if b:
                            turned_hi(b - 1, i)
                    if p + 3 < 3 * blocks:
                        x_hi(p + 3, i)

                se.wait_ge(sem("unit_done"), e * (3 * BLK1) + n)
                x_hi(0, e * EXPERT_ROUNDS)
                act(parts(XH, 1024), GATHERED[:, bass.ds(e * 1024, 1024)], ACT.Copy).then_inc(sem("xh_high"), 1)
                for p in range(1, 3):
                    x_hi(p, e * EXPERT_ROUNDS)
                for p in range(5):
                    step(p, e * EXPERT_ROUNDS)
                with se.Fori(0, loop_rounds(blocks)) as i:
                    for p in range(5, 11):
                        step(p, i + e * EXPERT_ROUNDS)
                for p in range(5 + 6 * loop_rounds(blocks), 3 * blocks - 1):
                    step(p, e * EXPERT_ROUNDS)
                turned_hi(blocks - 1, e * EXPERT_ROUNDS)

            def ffn_s(blocks, base, units0, expert=None):
                b0 = base if expert is None else expert * blocks + base
                u0 = units0 if expert is None else expert * (3 * blocks) + units0

                def silu(par2, count, units):
                    se.wait_ge(sem("unit_done"), units)
                    c = count - 1
                    if not (isinstance(c, int) and c <= 0):
                        se.wait_ge(sem("gated"), c)
                    act(FS[:, par2 * 512:(par2 + 1) * 512], bank[2 * par2][:, :], ACT.Silu).then_inc(sem("silu"), 1)

                silu(0, b0, u0 + 1)
                silu(1, b0 + 1, u0 + 3)
                steps_left = blocks - 2
                with se.Fori(0, steps_left // 2) as i:
                    for hs in range(2):
                        silu(hs, i * 2 + (b0 + 2 + hs), i * 6 + (u0 + 6 + 3 * hs))
                done = steps_left // 2 * 2
                if steps_left % 2:
                    silu(0, b0 + 2 + done, u0 + 6 + 3 * done)

            se.wait_ge(sem("eps_set"), 1)
            se.wait_ge(sem("inputs"), 48)
            act(SM[:, 0:8], par("c", 8), ACT.Silu).then_inc(sem("c_act"), 1)
            se.nop().then_inc(sem("evac"), 6)
            stage_end(se, "se")
            norms = 0
            for l in range(LAYERS):
                name = f"w_in{l}"
                norm_s(norms, (l, 0), split=name, room=ROOM_MIX)
                se.wait_ge(*at("normed", 8, norms))
                norms += 1
                h_hi(ROOM_MIX)

                def evacuate(p, dst):
                    i, u = (0, p) if isinstance(p, int) else p
                    if isinstance(p, tuple) or p + 2 < PROJECTIONS:
                        w_hi(UN[name] + u + 2, ROOM_MIX, i)
                    se.wait_ge(sem("unit_done"), i * RING + (UN[name] + u + 1))
                    act(dst, bank[u % RING][:, :], ACT.Copy).then_inc(sem("evac"), 1)

                def silus(i):
                    se.wait_ge(sem("conv_tap"), i * 4 + (l * 12 + 4))
                    c = BIG[:, bass.ds(i * 2048 + CONV, 2048)]
                    act(c, c, ACT.Silu)

                with se.Fori(0, 2) as i:
                    for u in range(RING):
                        evacuate((i, u), BIG[:, bass.ds(i * 3072 + (PROJ + u * 512), 512)])
                with se.Fori(0, 2) as i:
                    for u in range(RING):
                        evacuate((i, 12 + u), BIG[:, bass.ds(i * 3072 + (PROJ + 6144 + u * 512), 512)])
                    silus(i)
                for p in range(24, PROJECTIONS):
                    evacuate(p, big(PROJ + p * 512, 512))
                silus(2)
                se.wait_ge(sem("evac"), l * 30 + 36)
                lk(act(big(Z_, 2048), big(Z_, 2048), ACT.Silu))
                act(big(GATES, 4096), big(GATES, 4096), ACT.Sigmoid)
                stage_end(se, "se")
                act(view(SM, 0, [[8, 2], [1, 8]]), view(bank[6], 0, [[16, 2], [1, 8]]), ACT.Exp, scale=-1.0).then_inc(sem("beta_exp"), 1)
                lk(act(SM[:, 48:64], par("a_log", 16, l * 16), ACT.Exp))
                se.wait_ge(*at("a_abs", 1, l, 1))
                lk(act(SM[:, 32:48], SM[:, 32:48], ACT.Exp, scale=-1.0))
                act(SM[:, 32:48], SM[:, 32:48], ACT.Ln, bias=1.0).then_inc(sem("a_ln"), 1)
                se.wait_ge(*at("qk_sum", 1, l, 1))
                for b in range(8):
                    ins = act(big(SLOT["D"] + b * 512, 512), bank[b][:, :], ACT.Ln, bias=EPSB[:, 0:1])
                lk(ins)
                lk(act(big(SLOT["D"], 2048), big(SLOT["D"], 2048), ACT.Exp, scale=-0.5, bias=EPSB[:, 1:2]))
                act(big(SLOT["E"], 2048), big(SLOT["E"], 2048), ACT.Exp, scale=-0.5).then_inc(sem("qk_rs"), 1)
                se.wait_ge(*at("decay_arg", 1, l, 1))
                act(big(EG, 512), bank[2][:, :], ACT.Exp)
                act(big(EG + 512, 512), bank[3][:, :], ACT.Exp)
                act(big(SLOT["B"], 2048), big(SLOT["B"], 2048), ACT.Exp)
                act(big(SLOT["C"], 2048), big(SLOT["C"], 2048), ACT.Exp, scale=-1.0)
                se.wait_ge(*at("kd_arg", 1, l, 1))
                act(SM[:, 128:144], SM[:, 112:128], ACT.Exp)
                lk(act(SM[:, 144:160], SM[:, 80:96], ACT.Exp))
                se.nop().then_inc(sem("decay_exp"), 1)
                stage_end(se, "se")
                se.wait_ge(*at("lt", 1, l, 1))
                for b in range(4):
                    ins = act(big(SLOT["C"] + b * 512, 512), bank[b][:, :], ACT.Copy)
                ins.then_inc(sem("lt_out"), 1)
                stage_end(se, "se")
                for s in range(6):
                    for q in range(4):
                        se.wait_ge(*at("level_u", 4 * s + q + 1, l, 24))
                        act(big(UBUF + q * 512, 512), bank[q][:, :], ACT.Copy).then_inc(sem("level_uc"), 1)
                stage_end(se, "se")
                stage_end(se, "se")
                se.wait_ge(*at("vnew_ps", 1, l, 1))
                act(big(WT, 512), bank[2][:, :], ACT.Copy, scale=-1.0)
                act(big(WT + 512, 512), bank[3][:, :], ACT.Copy, scale=-1.0).then_inc(sem("w_neg"), 1)
                se.wait_ge(*at("o_ps", 1, l, 1))
                for b in range(4):
                    ins = act(big(SLOT["E"] + b * 512, 512), bank[b][:, :], ACT.Square)
                ins.then_inc(sem("o_sq"), 1)
                se.wait_ge(*at("o_sum", 1, l, 1))
                for b in range(4):
                    ins = act(big(SLOT["E"] + b * 512, 512), bank[4 + b][:, :], ACT.Ln, bias=EPSB[:, 0:1], scale=1 / P)
                lk(ins)
                act(big(SLOT["E"], 2048), big(SLOT["E"], 2048), ACT.Exp, scale=-0.5).then_inc(sem("o_rs"), 1)
                stage_end(se, "se")
                se.wait_ge(*at("z_out", 8, l, 8))
                lk(act(big(SP, 3072), big(ZB, 3072), ACT.Abs))
                lk(act(big(SP, 3072), big(SP, 3072), ACT.Exp, scale=-1.0))
                act(big(SP, 3072), big(SP, 3072), ACT.Ln, bias=1.0).then_inc(sem("sp_ln"), 1)
                se.wait_ge(*at("stick_arg", 1, l, 1))
                act(big(ZB, 3072), big(ZB, 3072), ACT.Exp).then_inc(sem("stick_p"), 1)
                stage_end(se, "se")
                stage_end(se, "se")
                norm_s(norms, (l, 3), split="ffn" if l == 0 else None)
                if l == 0:
                    se.wait_ge(*at("normed", 8, norms))
                norms += 1
                if l == 0:
                    ffn_split_s("ffn", BLK1, 0, ROOM)
                    stage_end(se, "se")
                    continue
                se.wait_ge(sem("hn_ps"), 1)
                for b in range(4):
                    ins = act(big(HN + b * 512, 512), bank[4 + b][:, :], ACT.Copy)
                ins.then_inc(sem("hn_out"), 1)
                se.wait_ge(sem("route_arg"), 1)
                act(SM[:, 48:50], SM[:, 48:50], ACT.Exp).then_inc(sem("route_exp"), 1)
                stage_end(se, "se")
                se.nop().then_inc(sem("gather_high"), 2)
                with se.Fori(0, EXPERTS // 2) as i:
                    for j in range(2):
                        se.wait_ge(sem("gather_ps"), i * 2 + (j + 1))
                        act(GATHERED[:, bass.ds(i * 2048 + (j * 1024 + 512), 512)], bank[5 + 2 * j][:, :], ACT.Copy)\
                            .then_inc(sem("gather_high"), 1)
                se.wait_ge(sem("selt_ps"), 1)
                for b in range(4):
                    act(big(SELT + b * 512, 512), bank[b][:, :], ACT.Copy)
                stage_end(se, "se")
                with se.Fori(0, EXPERTS) as e:
                    count = se.value_load(SMU[0:1, bass.ds(e + 16, 1)], min_val=0, max_val=TOK)
                    with se.If(count <= P):
                        ffn_slots_s(UN["moe"], BLK1, BLK1, e)
                    with se.Else():
                        ffn_s(BLK1, BLK1, UN["moe"], e)
                        se.nop().then_inc(sem("xh_high"), 1)
                        se.nop().then_inc(sem("x_high"), 3 * BLK1)
                        se.nop().then_inc(sem("x_turned_high"), BLK1)
                stage_end(se, "se")
                stage_end(se, "se")
            norm_s(norms)
            stage_end(se, "se")
            norms += 1
            done_blocks = BLK1 * (1 + EXPERTS)

            def ffn2(name):
                nonlocal norms, done_blocks
                room = {"ffn1_0": ROOM_S5, "ffn1_1": ROOM_KV}.get(name, ROOM)
                norm_s(norms, split=name, room=room)
                se.wait_ge(*at("normed", 8, norms))
                norms += 1
                ffn_split_s(name, BLK2, done_blocks, room)
                done_blocks += BLK2
                if name != "ffn2_1":
                    stage_end(se, "se")

            act(SM[:, 0:32], par("log_dt", 32), ACT.Exp).then_inc(sem("s5_dt"), 1)
            se.wait_ge(sem("s5_mag_arg"), 1)
            lk(act(SM[:, 32:64], SM[:, 32:64], ACT.Exp))
            se.wait_ge(sem("angles"), 1)
            lk(act(SM[:, 256:768], SM[:, 256:768], ACT.Sin))
            se.nop().then_inc(sem("s5_trig"), 1)
            ffn2("ffn1_0")
            norm_s(norms)
            norms += 1
            se.wait_ge(sem("y_out"), KT)
            act(big(YB, 2048), big(YB, 2048), ACT.Gelu_apprx_tanh).then_inc(sem("y_gelu"), 1)
            stage_end(se, "se")
            for u in range(4):
                se.wait_ge(sem("unit_done"), UN["glu"] + u + 1)
                act(big(SLOT["D"] + u * 512, 512), bank[u][:, :], ACT.Sigmoid).then_inc(sem("glu_sig"), 1)
            stage_end(se, "se")
            ffn2("ffn2_0")
            norm_s(norms)
            norms += 1
            stage_end(se, "se")
            se.wait_ge(sem("kv_ms"), 1)
            lk(act(big(KRS, 1024), big(KSQ, 1024), ACT.Ln))
            act(big(KRS, 1024), big(KRS, 1024), ACT.Exp, scale=-0.5).then_inc(sem("kv_rs"), 1)
            se.wait_ge(sem("k_normed"), 1)
            for br, t0 in enumerate((4, 8)):
                for g in range(4):
                    s0 = 64 * (g % 2)
                    for d0 in (0, 64):
                        se.dma_start(BIG[d0:d0 + 64, KD + br * 1024 + g * TOK:KD + br * 1024 + (g + 1) * TOK],
                                     BIG[s0:s0 + 64, KV + (t0 + g // 2) * TOK:KV + (t0 + g // 2 + 1) * TOK]).then_inc(sem("k_dup"), 16)
            se.wait_ge(sem("bias_tab"), 1)
            se.dma_start(tab_dram, BIG[0:QH, BTAB:BTAB + 384]).then_inc(sem("tab_out"), 16)
            se.wait_ge(sem("tab_out"), 16)
            for blk in range(2):
                se.dma_start(view(BIG, BT + blk * P, [[TOK, QH], [1, P]]),
                             bass.AP(tensor=tab_dram.tensor, offset=P * blk, ap=[[1, P], [384, QH], [1, P]]))\
                    .then_inc(sem("bias_here"), 16)
            se.wait_ge(sem("hid_ps"), 1)
            for hf in range(2):
                ins = act(view(SM, hf * 2 * NCMP, [[4 * NCMP, 2], [1, 2 * NCMP]]), view(PS, HID[hf], [[2 * NCMP, 2], [1, 2 * NCMP]]),
                          ACT.Gelu_apprx_tanh)
            ins.then_inc(sem("hid"), 1)
            se.wait_ge(sem("kc_ms"), 1)
            lk(act(SM[:, 256:256 + 4 * NCMP], SM[:, 192:192 + 4 * NCMP], ACT.Ln))
            act(SM[:, 256:256 + 4 * NCMP], SM[:, 256:256 + 4 * NCMP], ACT.Exp, scale=-0.5).then_inc(sem("kc_rs"), 1)
            se.wait_ge(sem("k_dup"), 16 * 16)
            se.wait_ge(sem("bias_here"), 32)
            stage_end(se, "se")
            ffn2("ffn1_1")
            norm_s(norms)
            norms += 1
            stage_end(se, "se")
            se.wait_ge(sem("gate_logits"), 1)
            act(big(GT, 96), bank[4][:, 0:96], ACT.Exp, scale=-1.0).then_inc(sem("gate_exp"), 1)
            se.wait_ge(sem("q_ms"), 1)
            lk(act(big(PT + 2048, 2048), big(PT, 2048), ACT.Ln))
            act(big(PT + 2048, 2048), big(PT + 2048, 2048), ACT.Exp, scale=-0.5).then_inc(sem("q_rs"), 1)
            stage_end(se, "se")
            se.wait_ge(sem("cmp_arg"), 1)
            act(big(CP, 2 * QH * NCMP), big(CP, 2 * QH * NCMP), ACT.Exp).then_inc(sem("cmp_exp"), 1)
            stage_end(se, "se")
            stage_end(se, "se")
            for br in range(2):
                se.wait_ge(sem("row_max"), br + 1)
                for h in range(QH):
                    for n in range(NT):
                        r = big(LG + h * 384 + n * P, P * (n + 1))
                        ins = act(r, r, ACT.Exp, bias=SM[:, 32 + n * 16 + h:33 + n * 16 + h],
                                  accum_out=SM[:, 64 + n * 16 + h:65 + n * 16 + h])
                lk(ins)
                se.nop().then_inc(sem("row_exp"), 1)
                stage_end(se, "se")
            stage_end(se, "se")
            ffn2("ffn2_1")

        @stage.gpsimd
        def _(po):
            def lk(ins):
                link(po, "pool_step", ins)

            po.memset(EPSB[:, 0:1], EPS)
            po.memset(EPSB[:, 1:2], float(-0.5 * np.log(P))).then_inc(sem("eps_set"), 1)
            po.wait_ge(sem("inputs"), 48)
            stage_end(po, "po")
            for l in range(LAYERS):
                stage_end(po, "po")
                stage_end(po, "po")
                stage_end(po, "po")
                for s in range(6):
                    if s >= 2:
                        po.wait_ge(*at("level_u", 4 * (s - 1), l, 24))
                    for q in range(4):
                        po.tensor_tensor(view(BIG, LTS[s % 2] + q * 512, [[P, 4], [1, P]]), view(BIG, SLOT["C"] + q * 512, [[P, 4], [1, P]]),
                                         view(CON, CC["level"] + (s + 1) * P, [[0, 4], [1, P]]), ALU.mult).then_inc(sem("level_mask"), 1)
                stage_end(po, "po")
                stage_end(po, "po")
                stage_end(po, "po")
                stage_end(po, "po")
                stage_end(po, "po")
                if l == 0:
                    stage_end(po, "po")
            stage_end(po, "po")
            stage_end(po, "po")
            stage_end(po, "po")
            stage_end(po, "po")
            stage_end(po, "po")
            for i, name in enumerate(("b_re", "b_im", "c_re", "c_im")):
                po.dma_start(big(S5P + i * 512, 512), A[name]).then_inc(sem("s5_here"), 16)
            for q in range(4):
                po.memset(view(BIG, TC + q * 2048, [[TOK, 8], [1, 1]]), 1.0)
                ins = po.memset(view(BIG, TS + q * 2048, [[TOK, 8], [1, 1]]), 0.0)
            lk(ins)
            po.wait_ge(sem("s5_trig"), 1)
            for q in range(4):
                c0, s0 = TC + q * 2048, TS + q * 2048
                for k in range(8):
                    n = 2 ** k

                    for p0 in range(0, n, 64):
                        w = min(n, 64)

                        def old(b):
                            return view(BIG, b + p0, [[TOK, 8], [1, w]])

                        def new(b):
                            return view(BIG, b + n + p0, [[TOK, 8], [1, w]])

                        cw = view(SM, 512 + 32 * k + 8 * q, [[1, 8], [0, w]])
                        sw = view(SM, 256 + 32 * k + 8 * q, [[1, 8], [0, w]])
                        t1 = view(BIG, PT1, [[w, 8], [1, w]])
                        po.tensor_tensor(new(c0), old(c0), cw, ALU.mult)
                        po.tensor_tensor(new(s0), old(s0), cw, ALU.mult)
                        lk(po.tensor_tensor(t1, old(s0), sw, ALU.mult))
                        lk(po.tensor_tensor(new(c0), new(c0), t1, ALU.subtract))
                        lk(po.tensor_tensor(t1, old(c0), sw, ALU.mult))
                        lk(po.tensor_tensor(new(s0), new(s0), t1, ALU.add))
            po.nop().then_inc(sem("tables"), 1)
            stage_end(po, "po")
            for k in range(KT):
                po.wait_ge(sem("scanned"), k + 1)
                c, s = big(TC + k * 1024, 1024), big(TS + k * 1024, 1024)
                to = rot(k)
                po.tensor_tensor(big(to[0], 1024), c, big(YR, 1024), ALU.mult)
                po.tensor_tensor(big(to[1], 1024), s, big(YI, 1024), ALU.mult)
                if k:
                    po.wait_ge(sem("y_ps"), k)
                po.tensor_tensor(big(to[2], 1024), s, big(YR, 1024), ALU.mult)
                lk(po.tensor_tensor(big(to[3], 1024), c, big(YI, 1024), ALU.mult))
                po.nop().then_inc(sem("rotated"), 1)
            stage_end(po, "po")
            stage_end(po, "po")
            stage_end(po, "po")
            for i, name in enumerate(("w1_k", "w1_v")):
                po.dma_start(big(W1 + i * 4096, 4096), A[name]).then_inc(sem("w1_here"), 16)
            stage_end(po, "po")
            stage_end(po, "po")
            stage_end(po, "po")
            stage_end(po, "po")
            stage_end(po, "po")
            stage_end(po, "po")
            stage_end(po, "po")
            stage_end(po, "po")
            stage_end(po, "po")
            stage_end(po, "po")


def laid_out(inputs):
    a = {k: np.asarray(v) for k, v in inputs.items()}

    def cols(w, kt=KT, tiles=2):
        k, n = w.shape
        return w.reshape(kt, P, n // (tiles * P), tiles * P).transpose(2, 1, 0, 3).reshape(-1, P, UNIT)

    def rows(w):
        return w.reshape(w.shape[0] // 256, 2, P, D).transpose(0, 2, 1, 3).reshape(-1, P, UNIT)

    def swiglu(w1, w3, w2):
        u1, u3, u2 = cols(w1), cols(w3), rows(w2)
        n = len(u1)
        out = [u1[0], u3[0]]
        for b in range(1, n):
            out += [u1[b], u3[b], u2[b - 1]]
        return out + [u2[n - 1]]

    wall = np.empty((NUNITS, P, UNIT), np.float32)
    at = 0

    def put(units):
        nonlocal at
        for u in units:
            wall[at] = u
            at += 1

    b0, b1 = 3072 + D, 3072 + D + 16
    for l in range(LAYERS):
        put(cols(a["ada_w"][l]))
    for l in range(LAYERS):
        w = a["w_in"][l]
        put(cols(np.concatenate([w[:, :b0], w[:, b1:]], 1)))
        put(cols(a["w_up_dn"][l]))
        put(cols(a["w_up_sb"][l], 4, 4))
        put(cols(a["w_out"][l]))
        if l == 0:
            put(swiglu(a["ffn_w1"][0], a["ffn_w3"][0], a["ffn_w2"][0]))
        else:
            for e in range(EXPERTS):
                put(swiglu(a["moe_w1"][0, e], a["moe_w3"][0, e], a["moe_w2"][0, e]))

    def ffn2(i, l):
        w = a[f"ffn{i}_w_in_2"][l]
        put(swiglu(w[:, :FF2], w[:, FF2:], a[f"ffn{i}_w_out_2"][l]))

    ffn2(1, 0)
    put(cols(a["s5_w_glu_2"][0]))
    ffn2(2, 0)
    put(cols(a["w_kv_2"]))
    ffn2(1, 1)
    put(cols(a["w_qg_2"][0][:, :D]))
    put(cols(a["w_o_2"][0]))
    ffn2(2, 1)
    assert at == NUNITS

    def chan(v):
        return v.reshape(-1, P).T

    def narrow(w):
        return w.reshape(KT, P, -1).transpose(1, 0, 2).reshape(P, -1)

    def spread(v):
        return np.broadcast_to(v, (P, v.size))

    def twice(v):
        return np.concatenate([v, v], 0)

    def by_state(v):
        return v.reshape(PAIRS, P).T

    def by_state3(v):
        return np.ascontiguousarray(v.reshape(PAIRS, P, 16).transpose(1, 0, 2).reshape(P, 512))

    par = np.zeros((P, PC["width"]), np.float32)

    def small(name, v):
        par[:v.shape[0], PC[name]:PC[name] + v.shape[1]] = v

    small("c", chan(a["c"][0]))
    small("ada_b", np.concatenate([chan(a["ada_b"][l]) for l in range(LAYERS)], 1))
    for name, key in (("norm_mix", "norm_mix"), ("norm_ffn", "norm_ffn"), ("ffn1_norm", "ffn1_norm_2"),
                      ("mix_norm", "mix_norm_2"), ("ffn2_norm", "ffn2_norm_2")):
        small(name, np.concatenate([chan(a[key][l]) for l in range(LAYERS)], 1))
    small("conv_w", a["conv_w"].reshape(LAYERS, 4, 24, P).transpose(3, 0, 2, 1).reshape(P, -1))
    small("dn_out_norm", a["dn_out_norm"].T)
    small("dt_bias", spread(np.concatenate([v for l in range(LAYERS) for v in (a["dn_dt_bias"][l],) * NT])))
    small("a_log", spread(np.concatenate([v for l in range(LAYERS) for v in (a["dn_a_log"][l],) * NT])))
    small("final_norm", chan(a["final_norm"]))
    small("router_b", spread(np.concatenate([a["router_b"][0]] * NT)))
    small("s5_d", chan(a["s5_d_2"][0].reshape(-1)))
    small("kv_norm", chan(a["kv_norm_2"]))
    for name in ("k_norm_cmp", "k_norm_slc", "k_norm_win"):
        small(name, twice(a[name + "_2"])[:, None])
    small("q_norm", twice(a["q_norm_2"][0])[:, None])
    small("a_re", by_state(a["s5_a_re_2"][0]))
    small("a_im", by_state(a["s5_a_im_2"][0]))
    small("log_dt", by_state(np.repeat(a["s5_log_dt_2"][0][:, None], STATES, 1)))
    small("pos_k", twice(a["cmp_pos_k_2"].T))
    small("pos_v", twice(a["cmp_pos_v_2"].T))
    small("w_ba", np.concatenate([narrow(a["w_in"][l][:, b0:b1]) for l in range(LAYERS)], 1))
    small("router_w", narrow(a["router_w"][0]))
    small("w_gate", narrow(a["w_qg_2"][0][:, D:]))
    small("w2_k", np.concatenate([a["cmp_k_w2_2"]] * 2, 1))
    small("w2_v", np.concatenate([a["cmp_v_w2_2"]] * 2, 1))
    small("rel_bias", a["rel_bias_2"])

    def first(w):
        return np.ascontiguousarray(twice(w.transpose(1, 0, 2).reshape(64, -1)))

    return {
        "wall": wall, "par": par, "con": constants(),
        "x": np.ascontiguousarray(a["x"][0].reshape(TOK, KT, P).transpose(2, 1, 0).reshape(P, -1)),
        "b_re": by_state3(a["s5_b_re_2"][0]), "b_im": by_state3(a["s5_b_im_2"][0]),
        "c_re": by_state3(a["s5_c_re_2"][0].transpose(0, 2, 1)), "c_im": by_state3(a["s5_c_im_2"][0].transpose(0, 2, 1)),
        "w1_k": first(a["cmp_k_w1_2"]), "w1_v": first(a["cmp_v_w1_2"]),
    }


def constants():
    con = np.zeros((P, CC["width"]), np.float32)
    i, j = np.arange(P)[:, None], np.arange(P)[None, :]

    def put(name, v, extra=0):
        con[:v.shape[0], CC[name] + extra:CC[name] + extra + v.shape[1]] = v

    put("ident", i == j)
    put("ones", np.ones((P, P)))
    put("half_ones", i // 64 == j // 64)
    put("upper", i <= j)
    put("lower_strict", j < i)
    put("key_after", i >= j)
    for s in range(7):
        b = 2 ** s
        put("level", (i // b % 2 == 0) & (j // b == i // b + 1), s * P)
    put("level0_lower", (i % 2 == 1) & (j == i - 1))
    diag = np.where(i >= j, NEG, 0.0)
    put("stick_mask", np.concatenate([diag, np.zeros((P, P)), diag], 1))
    put("iota", np.broadcast_to(np.arange(8), (P, 8)))
    for n in range(NT):
        dist = (n * P + i) - (16 * np.arange(NCMP)[None, :] + 31)
        put("cmp_add", np.where(dist >= 0, 0.0, NEG), n * NCMP)
        put("cmp_mul", dist >= 0, n * NCMP)
    dist = np.arange(TOK)
    far = np.log(np.maximum(dist, 1).astype(np.float32) / np.float32(16)) / np.float32(np.log(128 / 16))
    bucket = np.where(dist < 16, dist, np.minimum(16 + (far * 16).astype(np.int32), 31))
    onehot = (np.arange(32)[:, None] == bucket[None, :]).astype(np.float32)
    put("onehot", onehot, 255)
    return con


def build(nc):
    A = {}
    for name, shape in (("wall", (NUNITS, P, UNIT)), ("par", (P, PC["width"])), ("con", (P, CC["width"])), ("x", (P, 2048)),
                        ("b_re", (P, 512)), ("b_im", (P, 512)), ("c_re", (P, 512)), ("c_im", (P, 512)),
                        ("w1_k", (P, 4096)), ("w1_v", (P, 4096))):
        A[name] = nc.dram_tensor(f"in_{name}", shape, F32, kind="ExternalInput").ap()
    A["tab"] = nc.dram_tensor("bias_table", (QH, 384), F32, kind="Internal").ap()
    A["out"] = nc.dram_tensor("out", (P, 2048), F32, kind="ExternalOutput").ap()
    program(nc, A)


def kernel(**inputs):
    import concourse.bacc as _bacc
    from concourse.bass_utils import run_bass_kernel_spmd as _run

    nc = _bacc.Bacc("TRN2", target_bir_lowering=False, num_devices=1)
    arrays = {f"in_{k}": v for k, v in laid_out(inputs).items()}
    build(nc)
    r = _run(nc, [arrays], core_ids=[0])
    got = np.asarray(r.results[0]["out"])
    return np.ascontiguousarray(got.reshape(P, KT, TOK).transpose(2, 1, 0).reshape(1, TOK, D))
```
